# Optimizing a Trainium2 kernel written in Bass

```python
import math
import jax, jax.numpy as jnp
from jax import lax
import numpy as np

D_MODEL = 2048
BATCH = 1
SEQ = 256
DEPTH = 1

MOBA_HEADS = 8
MOBA_HEAD_DIM = 128
MOBA_WIDTH = MOBA_HEADS * MOBA_HEAD_DIM
MOBA_BLOCK = 256
MOBA_TOPK = 3
MOBA_Q_CHUNK = 64
PARTIAL_ROPE_DIM = MOBA_HEAD_DIM // 4
MLA_HEADS = 8
MLA_NOPE_DIM = 128
MLA_ROPE_DIM = 64
MLA_V_DIM = 128
MLA_Q_RANK = 512
MLA_KV_RANK = 256
MLA_WIDTH = MLA_HEADS * MLA_V_DIM
MLA_Q_BLOCK = 128
ROPE_THETA = 500000.0
D_FF = -(-8 * D_MODEL // (3 * 256)) * 256
EPS = 1e-6
N_BRANCHES = 2
IN_SIZES = (MOBA_WIDTH, MOBA_WIDTH, MOBA_WIDTH, MLA_Q_RANK, MLA_KV_RANK, MLA_ROPE_DIM, N_BRANCHES * D_MODEL)
IN_COLS = sum(IN_SIZES)


def rmsnorm(x, g):
    x32 = x.astype(jnp.float32)
    y = x32 * lax.rsqrt(jnp.mean(x32 * x32, axis=-1, keepdims=True) + EPS)
    return (y * g.astype(jnp.float32)).astype(x.dtype)

def rope(x, positions):
    d = x.shape[-1]
    inv_freq = ROPE_THETA ** (-jnp.arange(0, d, 2, dtype=jnp.float32) / d)
    ang = positions.astype(jnp.float32)[..., None] * inv_freq
    cos = jnp.cos(ang)[:, :, None, :]
    sin = jnp.sin(ang)[:, :, None, :]
    x32 = x.astype(jnp.float32)
    x1, x2 = x32[..., : d // 2], x32[..., d // 2:]
    out = jnp.concatenate([x1 * cos - x2 * sin, x2 * cos + x1 * sin], axis=-1)
    return out.astype(x.dtype)

def moba_attention(q, k, v):
    B, S, H, Dh = q.shape
    nb = -(-S // MOBA_BLOCK)
    n_sel = min(MOBA_TOPK, nb)
    pad = nb * MOBA_BLOCK - S
    kp = jnp.pad(k, ((0, 0), (0, pad), (0, 0), (0, 0)))
    vp = jnp.pad(v, ((0, 0), (0, pad), (0, 0), (0, 0)))
    kb = kp.reshape(B, nb, MOBA_BLOCK, H, Dh).transpose(0, 3, 1, 2, 4)
    vb = vp.reshape(B, nb, MOBA_BLOCK, H, Dh).transpose(0, 3, 1, 2, 4)
    k_mean = jnp.mean(kb.astype(jnp.float32), axis=3)
    scale = Dh ** -0.5
    bidx = jnp.arange(B)[:, None, None, None]
    hidx = jnp.arange(H)[None, None, :, None]

    def chunk(c):
        start = c * MOBA_Q_CHUNK
        qc = lax.dynamic_slice_in_dim(q, start, MOBA_Q_CHUNK, axis=1)
        blk = start // MOBA_BLOCK
        qpos = start + jnp.arange(MOBA_Q_CHUNK)
        gate = jnp.einsum('bqhd,bhnd->bqhn', qc.astype(jnp.float32), k_mean)
        past = jnp.arange(nb) < blk
        gate = jnp.where(past[None, None, None, :], gate, -jnp.inf)
        _, sel = lax.top_k(gate, n_sel)
        sel_valid = jnp.arange(n_sel) < blk
        k_sel = kb[bidx, hidx, sel]
        v_sel = vb[bidx, hidx, sel]
        s_sel = jnp.einsum('bqhd,bqhkjd->bqhkj', qc, k_sel).astype(jnp.float32) * scale
        s_sel = jnp.where(sel_valid[None, None, None, :, None], s_sel, -jnp.inf)
        s_sel = s_sel.reshape(B, MOBA_Q_CHUNK, H, n_sel * MOBA_BLOCK)
        k_own = lax.dynamic_slice_in_dim(kp, blk * MOBA_BLOCK, MOBA_BLOCK, axis=1)
        v_own = lax.dynamic_slice_in_dim(vp, blk * MOBA_BLOCK, MOBA_BLOCK, axis=1)
        s_own = jnp.einsum('bqhd,bjhd->bqhj', qc, k_own).astype(jnp.float32) * scale
        kpos = blk * MOBA_BLOCK + jnp.arange(MOBA_BLOCK)
        causal = kpos[None, :] <= qpos[:, None]
        s_own = jnp.where(causal[None, :, None, :], s_own, -jnp.inf)
        p = jax.nn.softmax(jnp.concatenate([s_sel, s_own], axis=-1), axis=-1).astype(v.dtype)
        p_sel = p[..., : n_sel * MOBA_BLOCK].reshape(B, MOBA_Q_CHUNK, H, n_sel, MOBA_BLOCK)
        p_own = p[..., n_sel * MOBA_BLOCK:]
        return (jnp.einsum('bqhkj,bqhkjd->bqhd', p_sel, v_sel)
                + jnp.einsum('bqhj,bjhd->bqhd', p_own, v_own))

    outs = lax.map(chunk, jnp.arange(S // MOBA_Q_CHUNK))
    return outs.transpose(1, 0, 2, 3, 4).reshape(B, S, H, Dh)

def mla_attention(q_nope, q_rope, k_nope, k_rope, v):
    B, S, H, _ = q_nope.shape
    scale = (MLA_NOPE_DIM + MLA_ROPE_DIM) ** -0.5
    kpos = jnp.arange(S)

    def block(c):
        start = c * MLA_Q_BLOCK
        qn = lax.dynamic_slice_in_dim(q_nope, start, MLA_Q_BLOCK, axis=1)
        qr = lax.dynamic_slice_in_dim(q_rope, start, MLA_Q_BLOCK, axis=1)
        s = (jnp.einsum('bqhd,bkhd->bhqk', qn, k_nope)
             + jnp.einsum('bqhd,bkd->bhqk', qr, k_rope)).astype(jnp.float32) * scale
        qpos = start + jnp.arange(MLA_Q_BLOCK)
        s = jnp.where((kpos[None, :] <= qpos[:, None])[None, None], s, -jnp.inf)
        p = jax.nn.softmax(s, axis=-1).astype(v.dtype)
        return jnp.einsum('bhqk,bkhd->bqhd', p, v)

    outs = lax.map(block, jnp.arange(S // MLA_Q_BLOCK))
    return outs.transpose(1, 0, 2, 3, 4).reshape(B, S, H * MLA_V_DIM)

def first_inputs(seed: int = 0) -> dict:
    key = jax.random.key(seed)
    ks = jax.random.split(key, 17)

    def dense(k, shape, fan_in):
        return jax.random.normal(k, shape, jnp.float32) * (fan_in ** -0.5)

    def gain(k, shape):
        return 1.0 + 0.02 * jax.random.normal(k, shape, jnp.float32)

    L = DEPTH
    return {
        "x": jax.random.normal(ks[0], (BATCH, SEQ, D_MODEL), jnp.float32),
        "positions": jnp.broadcast_to(jnp.arange(SEQ, dtype=jnp.int32), (BATCH, SEQ)),
        "attn_norm": gain(ks[1], (L, D_MODEL)),
        "w_in": dense(ks[2], (L, D_MODEL, IN_COLS), D_MODEL),
        "q_norm": gain(ks[3], (L, MLA_Q_RANK)),
        "w_uq": dense(ks[4], (L, MLA_Q_RANK, MLA_HEADS * (MLA_NOPE_DIM + MLA_ROPE_DIM)), MLA_Q_RANK),
        "kv_norm": gain(ks[5], (L, MLA_KV_RANK)),
        "w_ukv": dense(ks[6], (L, MLA_KV_RANK, MLA_HEADS * (MLA_NOPE_DIM + MLA_V_DIM)), MLA_KV_RANK),
        "w_branch_a": dense(ks[7], (L, MOBA_WIDTH, D_MODEL), MOBA_WIDTH),
        "w_branch_b": dense(ks[8], (L, MLA_WIDTH, D_MODEL), MLA_WIDTH),
        "w_out": dense(ks[9], (L, D_MODEL, D_MODEL), D_MODEL),
        "ffn_norm": gain(ks[10], (L, D_MODEL)),
        "w_gate": dense(ks[11], (L, D_MODEL, D_FF), D_MODEL),
        "w_up": dense(ks[12], (L, D_MODEL, D_FF), D_MODEL),
        "w_down": dense(ks[13], (L, D_FF, D_MODEL), D_FF),
        "final_norm": gain(ks[14], (D_MODEL,)),
    }

def first_block(x, positions, attn_norm, w_in, q_norm, w_uq, kv_norm, w_ukv, w_branch_a, w_branch_b,
              w_out, ffn_norm, w_gate, w_up, w_down, final_norm):
    B, S, _ = x.shape
    split_at = np.cumsum(np.array(IN_SIZES))[:-1].tolist()
    h = x
    for l in range(DEPTH):
        xn = rmsnorm(h, attn_norm[l])
        proj = xn @ w_in[l]
        q_a, k_a, v_a, c_q, c_kv, k_r, gates = jnp.split(proj, split_at, axis=-1)

        q_a = q_a.reshape(B, S, MOBA_HEADS, MOBA_HEAD_DIM)
        k_a = k_a.reshape(B, S, MOBA_HEADS, MOBA_HEAD_DIM)
        v_a = v_a.reshape(B, S, MOBA_HEADS, MOBA_HEAD_DIM)
        q_a = jnp.concatenate([rope(q_a[..., :PARTIAL_ROPE_DIM], positions), q_a[..., PARTIAL_ROPE_DIM:]], axis=-1)
        k_a = jnp.concatenate([rope(k_a[..., :PARTIAL_ROPE_DIM], positions), k_a[..., PARTIAL_ROPE_DIM:]], axis=-1)
        y_a = moba_attention(q_a, k_a, v_a).reshape(B, S, MOBA_WIDTH)

        qh = (rmsnorm(c_q, q_norm[l]) @ w_uq[l]).reshape(B, S, MLA_HEADS, MLA_NOPE_DIM + MLA_ROPE_DIM)
        q_nope, q_rope = qh[..., :MLA_NOPE_DIM], rope(qh[..., MLA_NOPE_DIM:], positions)
        kv = (rmsnorm(c_kv, kv_norm[l]) @ w_ukv[l]).reshape(B, S, MLA_HEADS, MLA_NOPE_DIM + MLA_V_DIM)
        k_nope, v_b = kv[..., :MLA_NOPE_DIM], kv[..., MLA_NOPE_DIM:]
        k_rope = rope(k_r[:, :, None, :], positions)[:, :, 0, :]
        y_b = mla_attention(q_nope, q_rope, k_nope, k_rope, v_b)

        g = jax.nn.sigmoid(gates.astype(jnp.float32)).astype(x.dtype)
        g_a, g_b = g[..., :D_MODEL], g[..., D_MODEL:]
        mixed = g_a * (y_a @ w_branch_a[l]) + g_b * (y_b @ w_branch_b[l])
        h = h + mixed @ w_out[l]

        hn = rmsnorm(h, ffn_norm[l])
        h = h + (jax.nn.silu(hn @ w_gate[l]) * (hn @ w_up[l])) @ w_down[l]
    return rmsnorm(h, final_norm)


GLA_HEADS = 4
GLA_DK = 128
GLA_DV = 256
GLA_RANK = 16
GLA_TAU = 16.0
GLA_CHUNK = 64
DIFF_HEADS = 4
DIFF_DQK = 128
DIFF_DV = 2 * DIFF_DQK
Q_BLOCK = 128
D_FF_2 = 5632
CONV_W = 3

GLA_QK = GLA_HEADS * GLA_DK
GLA_V = GLA_HEADS * GLA_DV
DIFF_QK = DIFF_HEADS * 2 * DIFF_DQK
DIFF_V = DIFF_HEADS * DIFF_DV
MIX_WIDTH = GLA_V + DIFF_V
IN_SPLITS = (GLA_QK, GLA_QK, GLA_V, GLA_V, GLA_RANK, DIFF_QK, DIFF_QK, DIFF_V)
IN_COLS_2 = sum(IN_SPLITS)


def rmsnorm_2(x, g):
    xf = x.astype(jnp.float32)
    y = xf * lax.rsqrt(jnp.mean(xf * xf, axis=-1, keepdims=True) + EPS)
    return (y * g.astype(jnp.float32)).astype(x.dtype)

def gla_chunked(q, k, v, log_a):
    B, S = q.shape[0], q.shape[1]
    n = S // GLA_CHUNK

    def to_chunks(t):
        t = t.astype(jnp.float32).reshape(B, n, GLA_CHUNK, GLA_HEADS, t.shape[-1])
        return jnp.transpose(t, (1, 0, 3, 2, 4))

    qc = to_chunks(q * (GLA_DK ** -0.5))
    kc, vc, ac = to_chunks(k), to_chunks(v), to_chunks(log_a)
    causal = jnp.tril(jnp.ones((GLA_CHUNK, GLA_CHUNK), dtype=bool))

    def step(state, inp):
        qi, ki, vi, ai = inp
        b = jnp.cumsum(ai, axis=2)
        o_inter = jnp.einsum('bhcd,bhde->bhce', qi * jnp.exp(b), state)
        diff = b[:, :, :, None, :] - b[:, :, None, :, :]
        decay = jnp.exp(jnp.where(causal[:, :, None], diff, -jnp.inf))
        scores = jnp.einsum('bhid,bhjd,bhijd->bhij', qi, ki, decay)
        o_intra = jnp.einsum('bhij,bhje->bhie', scores, vi)
        b_last = b[:, :, -1:, :]
        state = (jnp.exp(b_last[:, :, 0, :])[..., None] * state
                 + jnp.einsum('bhcd,bhce->bhde', ki * jnp.exp(b_last - b), vi))
        return state, o_inter + o_intra

    s0 = jnp.zeros((B, GLA_HEADS, GLA_DK, GLA_DV), jnp.float32)
    _, o = lax.scan(step, s0, (qc, kc, vc, ac))
    return jnp.transpose(o, (1, 0, 3, 2, 4)).reshape(B, S, GLA_HEADS, GLA_DV)

def diff_attention(q, k, v, lam):
    B, S = q.shape[0], q.shape[1]
    nb = S // Q_BLOCK
    slopes = jnp.asarray(2.0 ** (-8.0 * np.arange(1, DIFF_HEADS + 1) / DIFF_HEADS), jnp.float32)
    qb = jnp.transpose(q.reshape(B, nb, Q_BLOCK, DIFF_HEADS, 2, DIFF_DQK), (1, 0, 2, 3, 4, 5))
    k_pos = jnp.arange(S, dtype=jnp.int32)
    scale = DIFF_DQK ** -0.5

    def block(args):
        qi, bi = args
        q_pos = bi * Q_BLOCK + jnp.arange(Q_BLOCK, dtype=jnp.int32)
        dist = q_pos[:, None] - k_pos[None, :]
        bias = -slopes[:, None, None] * dist.astype(jnp.float32)
        s = jnp.einsum('bqhcd,bkhcd->bhcqk', qi, k,
                       preferred_element_type=jnp.float32) * scale + bias[None, :, None]
        s = jnp.where(dist >= 0, s, -jnp.inf)
        p = jax.nn.softmax(s, axis=-1)
        a = p[:, :, 0] - lam * p[:, :, 1]
        return jnp.einsum('bhqk,bkhe->bqhe', a, v.astype(jnp.float32))

    o = lax.map(block, (qb, jnp.arange(nb, dtype=jnp.int32)))
    return jnp.transpose(o, (1, 0, 2, 3, 4)).reshape(B, S, DIFF_HEADS, DIFF_DV)

def token_mixer(h, w_in, w_alpha_up, b_alpha, gla_norm, lambda_q1, lambda_k1,
                lambda_q2, lambda_k2, diff_norm, w_o, lambda_init):
    B, S, _ = h.shape
    proj = h @ w_in
    offs = np.cumsum((0,) + IN_SPLITS)
    gq, gk, gv, gg, ga, dq, dk, dv = [proj[..., int(offs[i]):int(offs[i + 1])]
                                      for i in range(len(IN_SPLITS))]
    log_a = jax.nn.log_sigmoid((ga @ w_alpha_up + b_alpha).astype(jnp.float32)) / GLA_TAU
    o_a = gla_chunked(gq.reshape(B, S, GLA_HEADS, GLA_DK), gk.reshape(B, S, GLA_HEADS, GLA_DK),
                      gv.reshape(B, S, GLA_HEADS, GLA_DV), log_a.reshape(B, S, GLA_HEADS, GLA_DK))
    gate = jax.nn.silu(gg.astype(jnp.float32)).reshape(B, S, GLA_HEADS, GLA_DV)
    o_a = (rmsnorm_2(o_a, gla_norm) * gate).reshape(B, S, GLA_V)
    f32 = jnp.float32
    lam = (jnp.exp(jnp.sum(lambda_q1.astype(f32) * lambda_k1.astype(f32)))
           - jnp.exp(jnp.sum(lambda_q2.astype(f32) * lambda_k2.astype(f32))) + lambda_init)
    o_b = diff_attention(dq.reshape(B, S, DIFF_HEADS, 2, DIFF_DQK),
                         dk.reshape(B, S, DIFF_HEADS, 2, DIFF_DQK),
                         dv.reshape(B, S, DIFF_HEADS, DIFF_DV), lam)
    o_b = (rmsnorm_2(o_b, diff_norm) * (1.0 - lambda_init)).reshape(B, S, DIFF_V)
    o = jnp.concatenate([o_a, o_b], axis=-1).astype(h.dtype)
    return o @ w_o

def conv_ffn(h, w_ffn_in, conv_w, conv_b, w_ffn_out):
    S = h.shape[1]
    up = h @ w_ffn_in
    a, b = up[..., :D_FF_2], up[..., D_FF_2:]
    a_pad = jnp.pad(a, ((0, 0), (CONV_W - 1, 0), (0, 0)))
    a = (conv_w[0] * a_pad[:, 0:S] + conv_w[1] * a_pad[:, 1:S + 1]
         + conv_w[2] * a_pad[:, 2:S + 2] + conv_b)
    return (jax.nn.gelu(a, approximate=True) * b) @ w_ffn_out

def second_inputs(seed: int = 0) -> dict:
    key = jax.random.key(seed)
    ks = jax.random.split(key, 20)
    nrm = lambda k, shape: jax.random.normal(k, shape, jnp.float32)
    gain = lambda k, n: 1.0 + 0.1 * nrm(k, (DEPTH, n))
    return {
        'x': nrm(ks[0], (BATCH, SEQ, D_MODEL)),
        'attn_pre_norm': gain(ks[1], D_MODEL),
        'w_in': nrm(ks[2], (DEPTH, D_MODEL, IN_COLS_2)) * D_MODEL ** -0.5,
        'w_alpha_up': nrm(ks[3], (DEPTH, GLA_RANK, GLA_QK)) * GLA_RANK ** -0.5,
        'b_alpha': 0.1 * nrm(ks[4], (DEPTH, GLA_QK)),
        'gla_norm': gain(ks[5], GLA_DV),
        'lambda_q1': 0.1 * nrm(ks[6], (DEPTH, DIFF_DQK)),
        'lambda_k1': 0.1 * nrm(ks[7], (DEPTH, DIFF_DQK)),
        'lambda_q2': 0.1 * nrm(ks[8], (DEPTH, DIFF_DQK)),
        'lambda_k2': 0.1 * nrm(ks[9], (DEPTH, DIFF_DQK)),
        'diff_norm': gain(ks[10], DIFF_DV),
        'w_o': nrm(ks[11], (DEPTH, MIX_WIDTH, D_MODEL)) * MIX_WIDTH ** -0.5,
        'attn_post_norm': gain(ks[12], D_MODEL),
        'ffn_pre_norm': gain(ks[13], D_MODEL),
        'w_ffn_in': nrm(ks[14], (DEPTH, D_MODEL, 2 * D_FF_2)) * D_MODEL ** -0.5,
        'conv_w': nrm(ks[15], (DEPTH, CONV_W, D_FF_2)) * CONV_W ** -0.5,
        'conv_b': 0.02 * nrm(ks[16], (DEPTH, D_FF_2)),
        'w_ffn_out': nrm(ks[17], (DEPTH, D_FF_2, D_MODEL)) * D_FF_2 ** -0.5,
        'ffn_post_norm': gain(ks[18], D_MODEL),
    }

def second_block(x, attn_pre_norm, w_in, w_alpha_up, b_alpha, gla_norm, lambda_q1, lambda_k1,
              lambda_q2, lambda_k2, diff_norm, w_o, attn_post_norm, ffn_pre_norm, w_ffn_in,
              conv_w, conv_b, w_ffn_out, ffn_post_norm):
    for l in range(DEPTH):
        lambda_init = 0.8 - 0.6 * math.exp(-0.3 * l)
        h = rmsnorm_2(x, attn_pre_norm[l])
        m = token_mixer(h, w_in[l], w_alpha_up[l], b_alpha[l], gla_norm[l], lambda_q1[l],
                        lambda_k1[l], lambda_q2[l], lambda_k2[l], diff_norm[l], w_o[l], lambda_init)
        x = x + rmsnorm_2(m, attn_post_norm[l])
        h = rmsnorm_2(x, ffn_pre_norm[l])
        f = conv_ffn(h, w_ffn_in[l], conv_w[l], conv_b[l], w_ffn_out[l])
        x = x + rmsnorm_2(f, ffn_post_norm[l])
    return x


def setup_inputs(seed=0):
    out = dict(first_inputs(seed))
    for name, value in second_inputs(seed + 1).items():
        if name != "x":
            out[name + "_2"] = value
    return out


def reference(
    x, positions, attn_norm, w_in, q_norm, w_uq, kv_norm, w_ukv, w_branch_a, w_branch_b, w_out,
    ffn_norm, w_gate, w_up, w_down, final_norm, attn_pre_norm_2, w_in_2, w_alpha_up_2,
    b_alpha_2, gla_norm_2, lambda_q1_2, lambda_k1_2, lambda_q2_2, lambda_k2_2, diff_norm_2,
    w_o_2, attn_post_norm_2, ffn_pre_norm_2, w_ffn_in_2, conv_w_2, conv_b_2, w_ffn_out_2,
    ffn_post_norm_2,
):
    x = first_block(
        x, positions, attn_norm, w_in, q_norm, w_uq, kv_norm, w_ukv, w_branch_a, w_branch_b,
        w_out, ffn_norm, w_gate, w_up, w_down, final_norm,
    )
    return second_block(
        x, attn_pre_norm_2, w_in_2, w_alpha_up_2, b_alpha_2, gla_norm_2, lambda_q1_2,
        lambda_k1_2, lambda_q2_2, lambda_k2_2, diff_norm_2, w_o_2, attn_post_norm_2,
        ffn_pre_norm_2, w_ffn_in_2, conv_w_2, conv_b_2, w_ffn_out_2, ffn_post_norm_2,
    )


_drawn_inputs = setup_inputs


def setup_inputs(seed=0):
    import zlib

    import numpy as np

    out = dict(_drawn_inputs(seed))
    spreads = {}
    factors = {'attn_norm': 5.311,
     'q_norm': 8.0,
     'kv_norm': 8.0,
     'b_alpha_2': 2.754,
     'lambda_q1_2': 8.0,
     'conv_b_2': 4.983,
     'ffn_norm': 8.0}
    for name, (base, spread) in spreads.items():
        noise = np.random.default_rng([zlib.crc32(name.encode()), seed]).standard_normal(out[name].shape)
        drawn = base * np.exp(spread * noise) if base else spread * noise
        out[name] = __import__('jax').numpy.asarray(drawn.astype(out[name].dtype))
    for name, factor in factors.items():
        out[name] = (out[name] * factor).astype(out[name].dtype)
    return out
```

```python
from contextlib import ExitStack

import numpy as np

import concourse.bass as bass
from concourse import mybir

F32 = mybir.dt.float32
F32R = mybir.dt.float32r
I32 = mybir.dt.int32
ALU = mybir.AluOpType
ACT = mybir.ActivationFunctionType
AX = mybir.AxisListType
ds = bass.ds

P = 128
TT = 2
T = P * TT
W = 512
CK = 2
RING = 4
LEAD = 3
D = 2048
KD = D // P
DT = D // W
DFF = 5632
KF = DFF // P
FT = DFF // W
EPS = 1e-6
NEG = -1e30

MH, MD = 8, 128
NOPE, ROPE, QR, KVR = 128, 64, 512, 256
MROPE = 32
QKV = 3 * MH * MD
C_CQ = QKV
C_CKV = C_CQ + QR
W_CKV = KVR + ROPE
C_GATE = C_CKV + W_CKV
UQ = MH * (NOPE + ROPE)
UKV = MH * (NOPE + MD)
THETA = 500000.0

GH, GK, GV, GR = 4, 128, 256, 16
LEVELS = 8
C2 = dict(gq=0, gk=512, gv=1024, gg=2048, ga=3072, dq=3088, dk=4112, dv=5136)
IN2 = 6160
TWO_PI = (6.28125, 0.0019350051879882812, 3.0198494e-07)
MAGIC = 12582912.0
LAMBDA_INIT = 0.2

A0, E0, H0, B0, R0, M0 = 0, 8192, 22528, 26624, 34816, 47104
END = 53200

V_ATT, V_Q, V_KV, V_FFN, V_FIN, V_PRE2, V_PRE3, V_BAL, V_GLA, V_DIF, V_ROWS = 0, 16, 20, 22, 38, 54, 70, 86, 90, 92, 94
V_CW, V_CB = 94, 94 + 3 * KF
V_ALL = V_CB + KF


class Count:

    def __init__(self, start, i=0, per=0):
        self.start, self.i, self.per = start, i, per

    def at(self, k):
        if self.per == 0 or (isinstance(self.i, int) and self.i == 0):
            return self.start + k
        return self.i * self.per + (self.start + k)

    def low(self, k):
        return self.start + k + (self.per * self.i if isinstance(self.i, int) else self.per)


class Chain:

    def __init__(self, eng, sem):
        self.eng, self.sem, self.base, self.k = eng, sem, 0, 0
        self.i, self.i0, self.per = 0, 0, 0

    def loop(self, i, i0, per):
        self.base, self.k = self.base + self.k, 0
        self.i, self.i0, self.per = i, i0, per

    def end(self, turns):
        assert self.k == self.per, f"the body's chain has {self.k} steps, not {self.per}"
        self.base, self.k, self.per = self.base + turns * self.per, 0, 0

    def mark(self, ins):
        ins.then_inc(self.sem, 1)
        self.k += 1

    def join(self):
        value = self.base + self.k
        if self.per:
            value = self.i * self.per + (value - self.i0 * self.per)
        self.eng.wait_ge(self.sem, value)

    def step(self, ins):
        self.mark(ins)
        self.join()


def pairs(eng, n):
    yield 0
    if n > 1:
        with eng.Fori(1, n) as i:
            yield i


def landed(n, c):
    return Count(16 * ((n.start + c) // RING + 1), n.i, 16 * n.per // RING).at(0)


def rows_of(w):
    return w.rearrange("l (k p) n -> p (l k) n", p=P)


def two_blocks(nc, a, out):
    ctx = ExitStack()
    with ctx:
        base = -(-nc.sbuf_base // 64) * 64

        def psum(name, shape):
            return ctx.enter_context(nc.psum_tensor(name, shape, F32))

        def sem(name):
            return ctx.enter_context(nc.semaphore(name))

        def at(name, word, shape, dt=F32):
            return nc.alloc_sbuf_tensor_at(name, [P] + shape, dt, offset=base + 4 * word)

        xa = [at("xa_hi", A0, [KD, T], F32R), at("xa_lo", A0 + 4096, [KD, T], F32R)]
        xb = [at("xb_hi", B0, [KD, T], F32R), at("xb_lo", B0 + 4096, [KD, T], F32R)]
        ff = [at("ff_hi", A0, [KF, T], F32R), at("ff_lo", A0 + KF * T, [KF, T], F32R)]
        xin = at("xin", H0, [TT, D])
        hres = at("hres", H0, [TT, D])
        ct = [at("ct_hi", H0, [6, T], F32R), at("ct_lo", H0 + 6 * T, [6, T], F32R)]
        qm = at("qm", E0, [TT, UQ])
        kvm = at("kvm", E0 + TT * UQ, [TT, UKV])
        qkv = at("qkv", E0 + 8192, [TT, QKV])
        gates = at("gates", E0 + 10240, [TT, 2 * D])
        proj2 = at("proj2", E0, [TT, IN2])
        g2bc = at("g2bc", E0 + 6144, [D])
        mres = at("mres", E0, [TT, D])
        frow = at("frow", B0, [TT, D])
        gfbc = at("gfbc", A0, [D])
        gf2bc = at("gf2bc", B0 + 4096, [D])
        obuf = at("obuf", B0, [TT, D])
        sqx2 = at("sqx2", A0 + 2048, [TT, D])
        raw = at("raw", R0, [RING, CK, W])
        hi = at("hi", R0 + 4096, [RING, CK, W], F32R)
        lo = at("lo", R0 + 8192, [RING, CK, W], F32R)
        m = M0
        stg = at("stg", m, [TT, W]); m += 1024
        stg2 = at("stg2", m, [TT, W]); m += 1024
        res = at("res", m, [TT, W])
        conv = at("conv", m, [4, T]); m += 1024
        lmask = at("lmask", m, [LEVELS, P])
        turned_a = at("turned_a", m, [4, T]); m += 1024
        ident = at("ident", m, [P]); m += P
        vec = at("vec", m, [V_ALL]); m += V_ALL + (-V_ALL) % 8
        gfin = at("gfin", m, [KD]); m += KD
        cs = at("cs", m, [TT, 2, ROPE // 2]); m += 128
        causal = at("causal", m, [384]); m += 384
        kr = at("kr", m, [TT, ROPE]); m += 128
        small = at("small", m, [256]); m += 256
        assert m <= END, m
        rows = at("rows", E0, [3, P])
        ang = at("ang", E0 + 512, [TT, 32])
        trn = at("trn", E0 + 640, [2, TT, 32])
        rnd = at("rnd", E0 + 768, [2, TT, 32])
        invf = at("invf", E0 + 896, [32])
        posi = at("posi", E0 + 960, [TT], I32)
        posf = at("posf", E0 + 968, [TT])
        junk = at("junk", E0 + 1024, [TT, D])
        def attention_buffers(tag, w0):
            b = {}
            b["q"] = [at(f"{tag}q{s}", w0 + 256 * s, [TT, P]) for s in range(2)]
            b["k"] = [at(f"{tag}k{s}", w0 + 512 + 256 * s, [TT, P]) for s in range(2)]
            b["qk"] = [at(f"{tag}qk{s}", w0 + 1024 + 512 * s, [2, T]) for s in range(2)]
            b["p"] = [at(f"{tag}p{s}", w0 + 2048 + 384 * s, [384]) for s in range(2)]
            b["pt"] = [at(f"{tag}pt{s}", w0 + 2816 + 384 * s, [384]) for s in range(2)]
            return b
        ab = attention_buffers("ab_", H0)
        vs = [at(f"vs{s}", H0 + 3584 + 256 * s, [TT, P]) for s in range(2)]
        qrs = [at(f"qrs{s}", E0 + 7168 + 128 * s, [TT, ROPE]) for s in range(2)]
        qrt = [at(f"qrt{s}", E0 + 7424 + 256 * s, [T]) for s in range(2)]
        krt = at("krt", E0 + 7936, [T])
        rope_t = [at(f"rope_t{j}", B0 + 512 * j, [512]) for j in range(4)]
        db = attention_buffers("db_", A0)
        dbias = at("dbias", E0 + TT * IN2, [384])
        lamr = at("lamr", E0 + TT * IN2 + 384, [4, P])
        lamj = at("lamj", E0 + TT * IN2 + 896, [2, P])
        sig = at("sig", A0 + 4864, [TT, GH * GV])
        G = A0
        gq_s = at("gq_s", G, [TT, P])
        gk_s = at("gk_s", G + 256, [TT, P])
        g_qk = at("g_qk", G + 512, [2, T])
        g_z = at("g_z", G + 1024, [T])
        g_e = at("g_e", G + 1280, [T])
        g_b = at("g_b", G + 1536, [T])
        g_x = at("g_x", G + 1792, [LEVELS, T])
        g_m = at("g_m", G + 3840, [LEVELS, P])
        g_at = at("g_at", G + 4864, [3, P])
        g_w = at("g_w", G + 5248, [P])
        g_chunk = at("g_chunk", G + 5376, [T])
        gat = at("gat", G + 5632, [T])
        walpha = at("walpha", G + 5888, [GH * GK])
        sq = at("sq", G + 6400, [TT, GV])

        def stat(k, n):
            return small[:, k:k + n]

        rs_x, ss_x = stat(0, 2), stat(2, 2)
        ss_c, rs_c = stat(4, 4), stat(8, 4)
        ss_h4, ss_h, rs_h = stat(12, 8), stat(20, 2), stat(22, 2)
        ss_f4, ss_f, rs_f = stat(24, 8), stat(32, 2), stat(34, 2)
        ss_x2, rs_x2, rs_in2 = stat(36, 2), stat(38, 2), stat(40, 2)
        ss_o, rs_o = stat(42, 16), stat(58, 16)
        ss_m4, ss_m, rs_m = stat(74, 8), stat(82, 2), stat(84, 2)
        ss_x3, rs_x3 = stat(94, 2), stat(96, 2)
        ss_g4, ss_g, rs_g = stat(98, 8), stat(106, 2), stat(108, 2)
        mx = [stat(110 + 2 * s, 2) for s in range(2)]
        sm = [stat(114 + 2 * s, 2) for s in range(2)]
        rc = [stat(118 + 2 * s, 2) for s in range(2)]
        lam2, lam = stat(122, 2), stat(124, 1)
        rs_tmp = stat(126, 16)

        acc = [psum(f"acc{j}", [P, TT, W]) for j in range(2)]
        mis = [psum(f"mis{j}", [P, 4, T]) for j in range(2)]
        misf = [x[:, :, :].rearrange("p a b -> p (a b)") for x in mis]
        accf = [x[:, :, :].rearrange("p a b -> p (a b)") for x in acc]

        raw_in = [sem(f"raw_in{j}") for j in range(RING)]
        hi_ready = sem("hi_ready")
        lo_ready = sem("lo_ready")
        chunk_used = sem("chunk_used")
        acc_free = [sem(f"acc_free{j}") for j in range(2)]
        staged = sem("staged")
        turned = sem("turned")
        hi_side = sem("hi_side")
        side = sem("side")
        x_in = sem("x_in")
        rows_in = sem("rows_in")
        tab_in = sem("tab_in")
        ident_ok = sem("ident_ok")
        masks_ok = sem("masks_ok")
        rows_turned = sem("rows_turned")
        vec_ok = sem("vec_ok")
        squares = sem("squares")
        var_ok = sem("var_ok")
        root_ok = sem("root_ok")
        rstd_ok = sem("rstd_ok")
        ang_ok = sem("ang_ok")
        cs_ok = sem("cs_ok")
        act_out = sem("act_out")
        dve_out = sem("dve_out")
        roped = sem("roped")
        head_in = sem("head_in")
        head_turned = sem("head_turned")
        head_qk = sem("head_qk")
        head_scores = sem("head_scores")
        head_masked = sem("head_masked")
        head_max = sem("head_max")
        head_exp = sem("head_exp")
        head_probs = sem("head_probs")
        probs_turned = sem("probs_turned")
        probs_in = sem("probs_in")
        head_y = sem("head_y")
        y_hi = sem("y_hi")
        y_done = sem("y_done")
        krt_turned = sem("krt_turned")
        krt_in = sem("krt_in")
        bias_ok = sem("bias_ok")
        lam_in = sem("lam_in")
        lam_sum = sem("lam_sum")
        lam_exp = sem("lam_exp")
        lam_ok = sem("lam_ok")
        ga_turned = sem("ga_turned")
        ga_in = sem("ga_in")
        wa_in = sem("wa_in")
        gl_staged = sem("gl_staged")
        gl_turned = sem("gl_turned")
        gl_qk = sem("gl_qk")
        gl_z = sem("gl_z")
        gl_abs = sem("gl_abs")
        gl_ln = sem("gl_ln")
        gl_dec = sem("gl_dec")
        gl_exp = sem("gl_exp")
        gl_x = sem("gl_x")
        gl_lev = sem("gl_lev")
        gl_at = sem("gl_at")
        gl_o = sem("gl_o")
        gl_sq = sem("gl_sq")
        gl_out = sem("gl_out")
        silu_ok = sem("silu_ok")
        res_in = sem("res_in")
        res_free = sem("res_free")
        h_in = sem("h_in")
        gbc_in = sem("gbc_in")
        x2_ok = sem("x2_ok")
        x3_ok = sem("x3_ok")
        conv_tap = sem("conv_tap")
        conv_ok = sem("conv_ok")
        gelu_ok = sem("gelu_ok")
        prod_ok = sem("prod_ok")
        fin_ok = sem("fin_ok")
        out_done = sem("out_done")
        act_chain = sem("act_chain")
        dve_chain = sem("dve_chain")
        pool_chain = sem("pool_chain")

        w_in, w_in2 = rows_of(a["w_in"]), rows_of(a["w_in_2"])
        w_uq, w_ukv = rows_of(a["w_uq"]), rows_of(a["w_ukv"])
        w_a, w_b, w_out = rows_of(a["w_branch_a"]), rows_of(a["w_branch_b"]), rows_of(a["w_out"])
        w_gate, w_up, w_down = rows_of(a["w_gate"]), rows_of(a["w_up"]), rows_of(a["w_down"])
        w_o2, w_f2, w_fo2 = rows_of(a["w_o_2"]), rows_of(a["w_ffn_in_2"]), rows_of(a["w_ffn_out_2"])

        PH = {}
        order = [
            ("qkv", 6, KD, 0), ("cq", 1, KD, 1), ("ckv", 1, KD, 1), ("uq", 3, 4, 0), ("ukv", 4, 2, 0),
            ("gate", 8, KD, 0), ("branch", 8, 8, 4), ("out", 4, KD, 4), ("ffn", 2 * FT, KD, FT),
            ("down", 4, KF, 4), ("in2a", 6, KD, 0), ("ga", 1, KD, 0), ("in2b", 6, KD, 4),
            ("o2", 4, KD, 4), ("ffn2", 2 * FT, KD, FT), ("down2", 4, KF, 0)]
        n_chunk = n_tile = 0
        n_item = 4
        for name, tiles, k, items in order:
            PH[name] = (n_chunk, n_tile, n_item, k // CK)
            n_chunk += tiles * k // CK
            n_tile += tiles
            n_item += items

        SQ = dict(x=1, c=2, h=6, f=10, x2=11, m=15, x3=16, g=20)

        def gains(row, n=4):
            return [vec[:, row + q:row + q + 1] for q in range(n)]

        def stages(item):
            return 2 * (item - 4 + 1)

        block = ctx.enter_context(nc.Block())

        @block.sync
        def _(sp):
            for t in range(TT):
                sp.dma_start(xin[:, t, :], a["x"][0, t * P:(t + 1) * P, :]).then_inc(x_in, 16)

            def load(n, c, src):
                slot = (n.start + c) % RING
                if n.low(c) >= RING:
                    sp.wait_ge(lo_ready, n.at(c - RING + 1))
                w = src.shape[2]
                sp.dma_start(raw[:, slot, :, 0:w], src).then_inc(raw_in[slot], 16)

            def tile(n, c0, w, col, k, width=W):
                for c in range(k // CK):
                    load(n, c0 + c, w[:, CK * c:CK * c + CK, ds(col, width)])

            def plain(phase, w, col, k, n_pairs):
                n0 = PH[phase][0]
                per = 2 * k // CK
                for i in pairs(sp, n_pairs):
                    n = Count(n0, i, per)
                    tile(n, 0, w, col + i * (2 * W), k)
                    tile(n, k // CK, w, (col + W) + i * (2 * W), k)

            def couple(phase, w1, w2, col1, col2, k, n_pairs):
                n0 = PH[phase][0]
                per = 2 * k // CK
                for i in pairs(sp, n_pairs):
                    n = Count(n0, i, per)
                    tile(n, 0, w1, col1 + i * W, k)
                    tile(n, k // CK, w2, col2 + i * W, k)

            plain("qkv", w_in, 0, KD, 3)
            tile(Count(PH["cq"][0]), 0, w_in, C_CQ, KD)
            tile(Count(PH["ckv"][0]), 0, w_in, C_CKV, KD, W_CKV)
            for j in range(3):
                tile(Count(PH["uq"][0]), 2 * j, w_uq, j * W, 4)
            for j in range(4):
                tile(Count(PH["ukv"][0]), j, w_ukv, j * W, 2)
            plain("gate", w_in, C_GATE, KD, 4)
            couple("branch", w_a, w_b, 0, 0, 8, DT)
            plain("out", w_out, 0, KD, 2)
            couple("ffn", w_gate, w_up, 0, 0, KD, FT)
            plain("down", w_down, 0, KF, 2)
            plain("in2a", w_in2, 0, KD, 3)
            tile(Count(PH["ga"][0]), 0, w_in2, C2["ga"], KD, GR)
            plain("in2b", w_in2, C2["dq"], KD, 3)
            plain("o2", w_o2, 0, KD, 2)
            couple("ffn2", w_f2, w_f2, 0, DFF, KD, FT)
            plain("down2", w_fo2, 0, KF, 2)
            for j in range(DT):
                sp.wait_ge(fin_ok, 2 * (j + 1))
                sp.dma_start(out[0].rearrange("(t p) n -> p t n", p=P)[:, :, j * W:(j + 1) * W],
                             frow[:, :, j * W:(j + 1) * W]).then_inc(out_done, 16)
            sp.wait_ge(out_done, 16 * DT)

        @block.tensor
        def _(pe):
            def turn(item, src, pair, blocks=4, wait=True):
                if wait:
                    pe.wait_ge(staged, stages(item))
                for kb in range(blocks):
                    for t in range(TT):
                        last = nc.tensor.transpose(mis[pair][:, kb, t * P:(t + 1) * P],
                                                   src[:, t, kb * P:(kb + 1) * P], ident[:, :])
                last.then_inc(turned, 1)

            def tile(n, c0, k, x, tile_no, par, width=W, k0=0, sides=None, hook=None, more=None):
                for c in range(k // CK):
                    if hook and c in hook:
                        hook[c]()
                    if c == 0 and tile_no.low(0) >= 2:
                        pe.wait_ge(acc_free[par], tile_no.at(0))
                    if sides is not None and c % 2 == 0:
                        pe.wait_ge(side, sides + c // 2 + 1)
                    slot = (n.start + c0 + c) % RING
                    pe.wait_ge(lo_ready, n.at(c0 + c + 1))
                    for kk in range(CK):
                        kb = c * CK + kk
                        for t in range(TT):
                            xh = x[0][:, k0 + kb, t * P:(t + 1) * P]
                            xl = x[1][:, k0 + kb, t * P:(t + 1) * P]
                            o = acc[par][:, t, 0:width]
                            wh, wl = hi[:, slot, kk, 0:width], lo[:, slot, kk, 0:width]
                            nc.tensor.matmul(o, xh, wh, start=kb == 0, stop=False)
                            nc.tensor.matmul(o, xh, wl, start=False, stop=False)
                            last = nc.tensor.matmul(o, xl, wh, start=False, stop=kb == k - 1)
                    last.then_inc(chunk_used, 1)

            def tiles_of(tile0, i=0, per=0):
                return Count(tile0 - tile0 % 2, i, per)

            def plain(phase, k, x, n_pairs, sides=None, item=None):
                n0, t0, _, per = PH[phase]
                with pe.Fori(0, n_pairs) as i:
                    n = Count(n0, i, 2 * per)
                    for j in range(2):
                        hook = None
                        if item is not None:
                            hook = {4: lambda j=j: turn(i * 2 + (item + j), stg, 0)}
                        tile(n, j * per, k, x, tiles_of(t0 + j, i, 2), (t0 + j) % 2,
                             sides=sides if j == 0 else None, hook=hook)

            def couple(phase, k, xs, n_pairs, hooks, sides=None, k0=(0, 0)):
                n0, t0, _, per = PH[phase]
                with pe.Fori(0, n_pairs) as i:
                    n = Count(n0, i, 2 * per)
                    for j in range(2):
                        tile(n, j * per, k, xs, tiles_of(t0 + j, i, 2), (t0 + j) % 2, k0=k0[j],
                             sides=sides if j == 0 else None,
                             hook={4: lambda: hooks(i)} if hooks and j == 0 else None)

            pe.wait_ge(ident_ok, 2)
            pe.wait_ge(rows_in, 16 * 14)
            for j, r in enumerate((V_ROWS, 2 * KF, 2 * KF)):
                last = nc.tensor.transpose(misf[1][:, j * P:j * P + r], rows[0:r, j, :], ident[0:r, 0:r])
            last.then_inc(rows_turned, 1)
            pe.wait_ge(x_in, 32)
            for j in range(4):
                if j == 1:
                    pe.wait_ge(vec_ok, 1)
                if j >= 2:
                    pe.wait_ge(side, j - 1)
                turn(j, xin[:, :, j * W:(j + 1) * W], j % 2, wait=False)
            plain("qkv", KD, xa, 3, sides=0)
            n0, t0, i0, per = PH["cq"]
            tile(Count(n0), 0, KD, xa, tiles_of(t0), t0 % 2)
            n0, t0, _, per = PH["ckv"]
            tile(Count(n0), 0, KD, xa, tiles_of(t0), t0 % 2, width=W_CKV,
                 hook={4: lambda: turn(i0, stg, 0)})
            n0, t0, _, per = PH["uq"]
            for j in range(3):
                if j == 1:
                    turn(i0 + 1, stg, 0, blocks=2)
                if j == 0:
                    pe.wait_ge(side, i0 + 1)
                tile(Count(n0), 2 * j, 4, ct, tiles_of(t0 + j), (t0 + j) % 2)
            n0, t0, _, per = PH["ukv"]
            pe.wait_ge(side, i0 + 2)
            for j in range(4):
                tile(Count(n0), j, 2, ct, tiles_of(t0 + j), (t0 + j) % 2, k0=4)

            def attend(n_bodies, head0, b, rope, diff):
                for i in pairs(pe, n_bodies):
                    h = Count(head0, i, 2)
                    for s in range(2):
                        pe.wait_ge(head_in, h.at(s + 1))
                        if h.low(s) >= 2:
                            pe.wait_ge(y_done, h.at(s - 1))
                        for x, src in enumerate((b["q"][s], b["k"][s])):
                            for t in range(TT):
                                last = nc.tensor.transpose(
                                    misf[s][:, x * T + t * P:x * T + (t + 1) * P], src[:, t, :], ident[:, :])
                        if rope:
                            for t in range(TT):
                                last = nc.tensor.transpose(misf[s][0:ROPE, W + t * P:W + (t + 1) * P],
                                                           qrs[s][:, t, :], ident[:, :])
                        last.then_inc(head_turned, 1)
                    for s in range(2):
                        pe.wait_ge(head_qk, h.at(s + 1))
                        for t in range(TT):
                            o = misf[s][:, W + t * P:W + t * P + (t + 1) * P]
                            last = nc.tensor.matmul(o, b["qk"][s][:, 0, t * P:(t + 1) * P],
                                                    b["qk"][s][:, 1, 0:(t + 1) * P], start=True, stop=not rope)
                            if rope:
                                last = nc.tensor.matmul(o, qrt[s][0:ROPE, t * P:(t + 1) * P],
                                                        krt[0:ROPE, 0:(t + 1) * P], start=False, stop=True)
                        last.then_inc(head_scores, 1)
                    if not diff:
                        for s in range(2):
                            pe.wait_ge(head_probs, h.at(s + 1))
                            for x in range(3):
                                last = nc.tensor.transpose(misf[s][:, x * P:(x + 1) * P],
                                                           b["p"][s][:, x * P:(x + 1) * P], ident[:, :])
                            last.then_inc(probs_turned, 1)
                        for s in range(2):
                            pe.wait_ge(probs_in, h.at(s + 1))
                            o = misf[s][:, W:W + T]
                            nc.tensor.matmul(o, vs[s][:, 0, :], b["pt"][s][:, 0:T], start=True, stop=False)
                            nc.tensor.matmul(misf[s][:, W + P:W + T], vs[s][:, 1, :], b["pt"][s][:, T:T + P],
                                             start=False, stop=True).then_inc(head_y, 1)
                    else:
                        pe.wait_ge(head_probs, h.at(2))
                        for x in range(3):
                            last = nc.tensor.transpose(misf[0][:, x * P:(x + 1) * P],
                                                       b["p"][0][:, x * P:(x + 1) * P], ident[:, :])
                        last.then_inc(probs_turned, 2)
                        pe.wait_ge(probs_in, h.at(2))
                        v = [proj2[:, t, ds(i * GV + C2["dv"], GV)] for t in range(TT)]
                        nc.tensor.matmul(misf[0][:, W:W + GV], b["pt"][0][:, 0:P], v[0], start=True, stop=True)
                        nc.tensor.matmul(misf[0][:, W + GV:W + 2 * GV], b["pt"][0][:, P:T], v[0],
                                         start=True, stop=False)
                        nc.tensor.matmul(misf[0][:, W + GV:W + 2 * GV], b["pt"][0][:, T:T + P], v[1],
                                         start=False, stop=True).then_inc(head_y, 2)

            pe.wait_ge(roped, 1)
            for t in range(TT):
                last = nc.tensor.transpose(misf[1][0:ROPE, t * P:(t + 1) * P], kr[:, t, :], ident[:, :])
            last.then_inc(krt_turned, 1)
            pe.wait_ge(krt_in, 1)
            attend(MH // 2, 0, ab, False, False)
            attend(MH // 2, MH, ab, True, False)

            plain("gate", KD, xa, 4)
            pe.wait_ge(y_done, 2 * MH)
            i0 = PH["branch"][2]
            n0, t0, _, per = PH["branch"]
            for i in pairs(pe, DT):
                n = Count(n0, i, 2 * per)
                tile(n, 0, 8, xb, tiles_of(t0, i, 2), t0 % 2)
                tile(n, per, 8, xb, tiles_of(t0 + 1, i, 2), (t0 + 1) % 2, k0=8,
                     hook=None if isinstance(i, int) else {0: lambda: turn(i + (i0 - 1), stg, 0)})
            i1 = PH["out"][2]
            n0, t0, _, per = PH["out"]
            tile(Count(n0), 0, KD, xa, tiles_of(t0), t0 % 2, sides=i0,
                 hook={4: lambda: turn(i1 - 1, stg, 0)})
            for j in range(1, DT):
                tile(Count(n0), j * per, KD, xa, tiles_of(t0 + j), (t0 + j) % 2,
                     hook={4: lambda j=j: turn(i1 + j - 1, stg, 0)})
            i2 = PH["ffn"][2]
            couple("ffn", KD, xb, FT, lambda i: turn(i + (i2 - 1), stg, 0), sides=i1)
            i3 = PH["down"][2]
            plain("down", KF, ff, 2, sides=i2, item=i3 - 1)
            i4 = PH["in2b"][2]
            n0, t0, _, per = PH["in2a"]
            tile(Count(n0), 0, KD, xb, tiles_of(t0), t0 % 2, sides=i3,
                 hook={4: lambda: turn(i4 - 1, stg, 0)})
            tile(Count(n0), per, KD, xb, tiles_of(t0 + 1), (t0 + 1) % 2)
            with pe.Fori(1, 3) as i:
                n = Count(n0, i, 2 * per)
                for j in range(2):
                    tile(n, j * per, KD, xb, tiles_of(t0 + j, i, 2), (t0 + j) % 2)
            n0, t0, _, per = PH["ga"]
            tile(Count(n0), 0, KD, xb, tiles_of(t0), t0 % 2, width=GR)
            plain("in2b", KD, xb, 3)

            n0, t0, _, per = PH["in2b"]
            for par in range(2):
                pe.wait_ge(acc_free[par], 2 * ((t0 + 6 + 1 - par) // 2))
            for t in range(TT):
                last = nc.tensor.transpose(misf[1][0:GR, t * P:(t + 1) * P], kr[:, t, 0:GR], ident[:, :])
            last.then_inc(ga_turned, 1)
            with pe.Fori(0, GH) as i:
                h = Count(0, i, 1)
                pe.wait_ge(gl_staged, h.at(1))
                for x, src in enumerate((gq_s, gk_s)):
                    for t in range(TT):
                        nc.tensor.transpose(misf[0][:, x * T + t * P:x * T + (t + 1) * P], src[:, t, :], ident[:, :])
                pe.wait_ge(ga_in, 1)
                nc.tensor.matmul(misf[0][:, W:W + T], g_w[0:GR, :], gat[0:GR, :], start=True, stop=True)\
                    .then_inc(gl_turned, 1)
                pe.wait_ge(gl_x, h.at(1))
                for t in range(TT):
                    tt = slice(t * P, (t + 1) * P)
                    for lv in range(LEVELS - 1):
                        nc.tensor.matmul(accf[t][:, lv * P:(lv + 1) * P], g_x[:, lv, tt], g_x[:, lv, tt],
                                         start=True, stop=True)
                    last = nc.tensor.matmul(accf[t][:, (LEVELS - 1) * P:], g_qk[:, 1, tt], g_qk[:, 0, tt],
                                            start=True, stop=True)
                last = nc.tensor.matmul(misf[0][:, W + T:W + T + P], g_x[:, LEVELS - 1, 0:P],
                                        g_x[:, LEVELS - 1, P:T], start=True, stop=True)
                last.then_inc(gl_lev, 1)
                pe.wait_ge(gl_at, h.at(1))
                v = [proj2[:, t, ds(i * GV + C2["gv"], GV)] for t in range(TT)]
                nc.tensor.matmul(misf[1][:, 0:GV], g_at[:, 0, :], v[0], start=True, stop=True)
                nc.tensor.matmul(misf[1][:, GV:2 * GV], g_at[:, 1, :], v[1], start=True, stop=False)
                nc.tensor.matmul(misf[1][:, GV:2 * GV], g_at[:, 2, :], v[0], start=False, stop=True)\
                    .then_inc(gl_o, 1)
                pe.wait_ge(gl_out, h.at(1))
            attend(GH, 2 * MH, db, False, True)

            i4 = PH["in2b"][2]
            for j in range(4):
                if j >= 2:
                    pe.wait_ge(side, i4 + j - 1)
                turn(i4 + j, obuf[:, :, j * W:(j + 1) * W], j % 2)
            n0, t0, _, per = PH["o2"]
            with pe.Fori(0, 2) as i:
                n = Count(n0, i, 2 * per)
                for j in range(2):
                    tile(n, j * per, KD, xa, tiles_of(t0 + j, i, 2), (t0 + j) % 2, sides=i4 if j == 0 else None)
            i5 = PH["o2"][2]
            for j in range(4):
                if j >= 2:
                    pe.wait_ge(side, i5 + j - 1)
                turn(i5 + j, hres[:, :, j * W:(j + 1) * W], j % 2)
            i6 = PH["ffn2"][2]

            def turn_both(k, a_read):
                pe.wait_ge(staged, k)
                pe.wait_ge(acc_free[PH["ffn2"][1] % 2], a_read)
                for pair, src in ((0, stg), (1, stg2)):
                    for kb in range(4):
                        for t in range(TT):
                            last = nc.tensor.transpose(mis[pair][:, kb, t * P:(t + 1) * P],
                                                       src[:, t, kb * P:(kb + 1) * P], ident[:, :])
                last.then_inc(turned, 1)

            n0, t0, _, per = PH["ffn2"]
            tile(Count(n0), 0, KD, xb, tiles_of(t0), t0 % 2, sides=i5)
            tile(Count(n0), per, KD, xb, tiles_of(t0 + 1), (t0 + 1) % 2)
            with pe.Fori(1, FT) as i:
                n = Count(n0, i, 2 * per)
                tile(n, 0, KD, xb, tiles_of(t0, i, 2), t0 % 2,
                     hook={4: lambda: turn_both(i * 2 + (stages(i6) - 2), i * 2 + (t0 - t0 % 2))})
                tile(n, per, KD, xb, tiles_of(t0 + 1, i, 2), (t0 + 1) % 2)
            even = t0 - t0 % 2 + 2 * FT
            n0, t0, _, per = PH["down2"]
            tile(Count(n0), 0, KF, ff, tiles_of(t0), t0 % 2, sides=i6,
                 hook={4: lambda: turn_both(stages(i6 + FT - 1), even)})
            tile(Count(n0), per, KF, ff, tiles_of(t0 + 1), (t0 + 1) % 2)
            for j in range(2, 4):
                tile(Count(n0), j * per, KF, ff, tiles_of(t0 + j), (t0 + j) % 2)

        @block.scalar
        def _(act):
            chain = Chain(act, act_chain)

            for row, name, n in ((V_ATT, "attn_norm", 16), (V_Q, "q_norm", 4), (V_KV, "kv_norm", 2),
                                 (V_FFN, "ffn_norm", 16), (V_FIN, "final_norm", 16),
                                 (V_PRE2, "attn_pre_norm_2", 16), (V_PRE3, "ffn_pre_norm_2", 16),
                                 (V_BAL, "b_alpha_2", 4), (V_GLA, "gla_norm_2", 2), (V_DIF, "diff_norm_2", 2)):
                v = a[name]
                v = v.rearrange("l (k p) -> (l k) p", p=P) if len(v.shape) == 2 else v.rearrange("(k p) -> k p", p=P)
                act.dma_start(rows[row:row + n, 0, :], v).then_inc(rows_in, 16)
            cw = a["conv_w_2"][0].rearrange("w (k p) -> w k p", p=P)
            act.dma_start(rows[0:KF, 1, :], cw[0]).then_inc(rows_in, 16)
            act.dma_start(rows[KF:2 * KF, 1, :], cw[1]).then_inc(rows_in, 16)
            act.dma_start(rows[0:KF, 2, :], cw[2]).then_inc(rows_in, 16)
            act.dma_start(rows[KF:2 * KF, 2, :], a["conv_b_2"].rearrange("l (k p) -> (l k) p", p=P))\
                .then_inc(rows_in, 16)
            for t in range(TT):
                act.dma_start(posi[:, t:t + 1], a["positions"][0:1, t * P:(t + 1) * P].rearrange("b p -> p b"))\
                    .then_inc(tab_in, 16)
            act.dma_start(invf[:, :], a["inv_freq"].partition_broadcast(P)).then_inc(tab_in, 16)

            def split(n, c, width=W):
                slot = (n.start + c) % RING
                act.wait_ge(raw_in[slot], landed(n, c))
                if n.low(c) >= RING:
                    act.wait_ge(chunk_used, n.at(c - RING + 1))
                nc.scalar.activation(hi[:, slot, :, 0:width], raw[:, slot, :, 0:width], ACT.Copy)\
                    .then_inc(hi_ready, 1)

            def root(k, dst):
                act.wait_ge(var_ok, k + 1)
                nc.scalar.activation(dst, dst, ACT.Sqrt).then_inc(root_ok, 1)

            def side_hi(item, dst, kb, gain=None, pair=0, blocks=4):
                act.wait_ge(turned, item + 1)
                if gain is None:
                    for half in range(2):
                        last = nc.scalar.activation(dst[0][:, ds(kb + 2 * half, 2), :],
                                                    mis[pair][:, 2 * half:2 * half + 2, :], ACT.Copy)
                else:
                    for j in range(blocks):
                        last = nc.scalar.activation(dst[0][:, ds(kb + j, 1), :], mis[pair][:, j:j + 1, :],
                                                    ACT.Copy, scale=gain[j])
                last.then_inc(hi_side, 1)

            def results(n, c):
                act.wait_ge(chunk_used, n.at(c + 1))

            def ev(dst, par, scale, width=W):
                nc.scalar.activation(dst, acc[par][:, 0, 0:width], ACT.Copy, scale=scale)\
                    .then_inc(acc_free[par], 1)

            def square(src, dst, total):
                return nc.scalar.activation(dst, src, ACT.Square, accum_out=total)

            def keep(item, ss4, j):
                act.wait_ge(staged, stages(item) - 1)
                for t in range(TT):
                    last = square(stg[:, t, :], stg2[:, t, :], ss4[:, 4 * t + j:4 * t + j + 1])
                last.then_inc(squares, 1)
                nc.scalar.activation(hres[:, :, j * W:(j + 1) * W], stg[:, :, :], ACT.Copy).then_inc(staged, 1)

            act.wait_ge(vec_ok, 1)
            for j in range(4):
                side_hi(j, xa, 4 * j, gains(V_ATT + 4 * j), j % 2)

            def first_norm():
                act.wait_ge(x_in, 32)
                for t in range(TT):
                    last = square(xin[:, t, :], junk[:, t, :], ss_x[:, t:t + 1])
                last.then_inc(squares, 1)
                root(0, rs_x)
                act.wait_ge(ang_ok, 1)
                for t in range(TT):
                    last = nc.scalar.activation(cs[:, t, :, :], trn[:, :, t, :], ACT.Sin)
                last.then_inc(cs_ok, 1)
                act.wait_ge(rstd_ok, 1)

            n0, t0, _, per = PH["qkv"]
            for i in pairs(act, 3):
                n = Count(n0, i, 2 * per)
                for j in range(2):
                    for c in range(per):
                        if c == 6 and j == 0 and isinstance(i, int):
                            first_norm()
                        if c == LEAD and (j == 1 or not isinstance(i, int)):
                            results(n, j * per - 1)
                            ev(qkv[:, 0, ds(i * (2 * W) + (j - 1) * W, W)], (t0 + j - 1) % 2, rs_x[:, 0:1])
                        split(n, j * per + c)
            n0, t0, i0, per = PH["cq"]
            n = Count(n0)
            for c in range(per):
                if c == LEAD:
                    results(n, -1)
                    ev(qkv[:, 0, 5 * W:], (t0 - 1) % 2, rs_x[:, 0:1])
                split(n, c)
            n = Count(PH["ckv"][0])
            for c in range(per):
                if c == LEAD:
                    results(n, -1)
                    ev(stg[:, 0, :], t0 % 2, rs_x[:, 0:1])
                    act.wait_ge(acc_free[t0 % 2], 2 * (t0 // 2 + 1))
                    for t in range(TT):
                        square(stg[:, t, :], stg2[:, t, :], ss_c[:, t:t + 1]).then_inc(staged, 1)
                split(n, c, W_CKV)
            side_hi(i0, ct, 0, gains(V_Q))
            n, tu = Count(PH["uq"][0]), PH["uq"][1]
            for c in range(6):
                if c == LEAD:
                    results(n, -1)
                    ev(stg[:, 0, 0:W_CKV], (tu - 1) % 2, rs_x[:, 0:1], W_CKV)
                    act.wait_ge(acc_free[(tu - 1) % 2], 2 * ((tu - 1) // 2 + 1))
                    for t in range(TT):
                        square(stg[:, t, 0:KVR], stg2[:, t, 0:KVR], ss_c[:, 2 + t:3 + t]).then_inc(staged, 1)
                    nc.scalar.activation(kr[:, :, :], stg[:, :, KVR:W_CKV], ACT.Copy).then_inc(squares, 1)
                    root(1, rs_c)
                    side_hi(i0 + 1, ct, 4, gains(V_KV, 2), blocks=2)
                    act.wait_ge(rstd_ok, 2)
                    results(n, 1)
                    ev(qm[:, 0, 0:W], tu % 2, rs_c[:, 0:1])
                split(n, c)
            n, tk = Count(PH["ukv"][0]), PH["ukv"][1]
            split(n, 0)
            results(n, -3)
            ev(qm[:, 0, W:2 * W], (tu + 1) % 2, rs_c[:, 0:1])
            split(n, 1)
            results(n, -1)
            ev(qm[:, 0, 2 * W:3 * W], (tu + 2) % 2, rs_c[:, 0:1])
            for j in range(4):
                if j < 2:
                    split(n, j + 2)
                results(n, j)
                ev(kvm[:, 0, j * W:(j + 1) * W], (tk + j) % 2, rs_c[:, 2:3])
            act.wait_ge(krt_turned, 1)
            nc.scalar.activation(krt[0:ROPE, :], misf[1][0:ROPE, 0:T], ACT.Copy).then_inc(krt_in, 1)

            def attend(n_bodies, head0, b, rope, diff):
                with act.Fori(0, n_bodies) as i:
                    h = Count(head0, i, 2)
                    for s in range(2):
                        act.wait_ge(head_turned, h.at(s + 1))
                        last = nc.scalar.activation(b["qk"][s][:, :, :].rearrange("p a b -> p (a b)"),
                                                    misf[s][:, 0:W], ACT.Copy)
                        if rope:
                            last = nc.scalar.activation(qrt[s][0:ROPE, :], misf[s][0:ROPE, W:W + T], ACT.Copy)
                        last.then_inc(head_qk, 1)
                    for s in range(2):
                        act.wait_ge(head_max, h.at(s + 1))
                        nc.scalar.activation(b["p"][s][:, 0:P], b["p"][s][:, 0:P], ACT.Exp,
                                             bias=mx[s][:, 0:1], accum_out=sm[s][:, 0:1])
                        nc.scalar.activation(b["p"][s][:, P:], b["p"][s][:, P:], ACT.Exp,
                                             bias=mx[s][:, 1:2], accum_out=sm[s][:, 1:2]).then_inc(head_exp, 1)
                    for s in range(1 if diff else 2):
                        act.wait_ge(probs_turned, h.at(2 if diff else s + 1))
                        nc.scalar.activation(b["pt"][s][:, :], misf[s][:, 0:384], ACT.Copy)\
                            .then_inc(probs_in, 2 if diff else 1)
                    for s in range(1 if diff else 2):
                        act.wait_ge(head_y, h.at(2 if diff else s + 1))
                        if not diff:
                            nc.scalar.activation(xb[0][:, ds(i * 2 + (head0 + s), 1), :],
                                                 mis[s][:, 2:3, :], ACT.Copy).then_inc(y_hi, 1)
                        else:
                            for t in range(TT):
                                last = square(misf[0][:, W + t * GV:W + (t + 1) * GV], b["qk"][0][:, t, :],
                                              ss_o[:, ds(i + (8 + 4 * t), 1)])
                            last.then_inc(y_hi, 2)

            attend(MH // 2, 0, ab, False, False)
            attend(MH // 2, MH, ab, True, False)

            n0, t0, _, per = PH["gate"]

            def sigmoid(par, col):
                for t in range(TT):
                    nc.scalar.activation(gates[:, t, ds(col, W)], acc[par][:, t, :], ACT.Sigmoid,
                                         scale=rs_x[:, t:t + 1]).then_inc(acc_free[par], 1)

            for i in pairs(act, 4):
                n = Count(n0, i, 2 * per)
                for j in range(2):
                    for c in range(per):
                        if c == LEAD and (j == 1 or not isinstance(i, int)):
                            results(n, j * per - 1)
                            sigmoid((t0 + j - 1) % 2, i * (2 * W) + (j - 1) * W)
                        split(n, j * per + c)
            n0, t0, i0, per = PH["branch"]
            for i in pairs(act, DT):
                n = Count(n0, i, 2 * per)
                first = isinstance(i, int)
                for c in range(2 * per):
                    if first and c == LEAD:
                        results(n, -1)
                        sigmoid((t0 - 1) % 2, 7 * W)
                    if not first and c == 7:
                        side_hi(i + (i0 - 1), xa, i * 4 - 4)
                    split(n, c)
            i1 = PH["out"][2]
            n0, t0, _, per = PH["out"]
            for j in range(DT):
                for c in range(per):
                    if c == LEAD and j > 0:
                        keep(i1 + j - 1, ss_h4, j - 1)
                    if c == 7 and j == 0:
                        side_hi(i1 - 1, xa, 4 * (DT - 1))
                    if c == 7 and j > 0:
                        side_hi(i1 + j - 1, xb, 4 * (j - 1), gains(V_FFN + 4 * (j - 1)))
                    split(Count(n0), j * per + c)
            n0, t0, i2, per = PH["ffn"]
            for i in pairs(act, FT):
                n = Count(n0, i, 2 * per)
                first = isinstance(i, int)
                for c in range(2 * per):
                    if c == LEAD and first:
                        keep(i2 - 1, ss_h4, DT - 1)
                        root(2, rs_h)
                    if c == 7 and first:
                        side_hi(i2 - 1, xb, 4 * (DT - 1), gains(V_FFN + 12))
                        act.wait_ge(rstd_ok, 3)
                    if c == 7 and not first:
                        side_hi(i + (i2 - 1), ff, i * 4 - 4)
                    if c == per + LEAD:
                        results(n, per - 1)
                        for t in range(TT):
                            nc.scalar.activation(stg2[:, t, :], acc[t0 % 2][:, t, :], ACT.Silu,
                                                 scale=rs_h[:, t:t + 1]).then_inc(acc_free[t0 % 2], 1)
                    split(n, c)
            n0, t0, i3, per = PH["down"]
            for j in range(DT):
                for c in range(per):
                    if c == LEAD and j > 0:
                        keep(i3 + j - 1, ss_f4, j - 1)
                    if c == 7 and j == 0:
                        side_hi(i3 - 1, ff, 4 * (FT - 1))
                    if c == 7 and j > 0:
                        side_hi(i3 + j - 1, xb, 4 * (j - 1), [gfin[:, 4 * j - 4 + q:4 * j - 3 + q] for q in range(4)])
                    split(Count(n0), j * per + c)
            n0, t0, _, per = PH["in2a"]
            for i in pairs(act, 3):
                n = Count(n0, i, 2 * per)
                first = isinstance(i, int)
                for j in range(2):
                    for c in range(per):
                        if c == LEAD and first and j == 0:
                            keep(i3 + DT - 1, ss_f4, DT - 1)
                            root(3, rs_f)
                        if c == 7 and first and j == 0:
                            side_hi(i3 + DT - 1, xb, 12, [gfin[:, q:q + 1] for q in range(12, 16)])
                        if c == 1 and first and j == 1:
                            act.wait_ge(x2_ok, 1)
                            for t in range(TT):
                                last = square(hres[:, t, :], sqx2[:, t, :], ss_x2[:, t:t + 1])
                            last.then_inc(squares, 1)
                            root(4, rs_x2)
                            act.wait_ge(rstd_ok, 5)
                        if c == LEAD and (j == 1 or not first):
                            results(n, j * per - 1)
                            ev(proj2[:, 0, ds(i * (2 * W) + (j - 1) * W, W)], (t0 + j - 1) % 2, rs_in2[:, 0:1])
                        split(n, j * per + c)
            n, t1 = Count(PH["ga"][0]), PH["ga"][1]
            for c in range(per):
                if c == LEAD:
                    results(n, -1)
                    ev(proj2[:, 0, 5 * W:6 * W], (t1 - 1) % 2, rs_in2[:, 0:1])
                split(n, c, GR)
            n0, t0, i4, per = PH["in2b"]
            for i in pairs(act, 3):
                n = Count(n0, i, 2 * per)
                for j in range(2):
                    for c in range(per):
                        if c == LEAD:
                            results(n, j * per - 1)
                            if isinstance(i, int) and j == 0:
                                ev(kr[:, 0, 0:GR], t1 % 2, rs_in2[:, 0:1], GR)
                            else:
                                ev(proj2[:, 0, ds(i * (2 * W) + ((j - 1) * W + C2["dq"]), W)],
                                   (t0 + j - 1) % 2, rs_in2[:, 0:1])
                        split(n, j * per + c)
            results(Count(n0), 6 * per - 1)
            ev(proj2[:, 0, 5 * W + C2["dq"]:6 * W + C2["dq"]], (t0 + 5) % 2, rs_in2[:, 0:1])

            act.wait_ge(ga_turned, 1)
            nc.scalar.activation(gat[0:GR, :], misf[1][0:GR, 0:T], ACT.Copy).then_inc(ga_in, 1)
            with act.Fori(0, GH) as i:
                h = Count(0, i, 1)
                chain.loop(i, 0, 3)
                act.wait_ge(gl_turned, h.at(1))
                nc.scalar.activation(g_qk[:, :, :].rearrange("p a b -> p (a b)"), misf[0][:, 0:W], ACT.Copy)\
                    .then_inc(gl_qk, 1)
                act.wait_ge(gl_z, h.at(1))
                chain.step(nc.scalar.activation(g_e[:, :], g_z[:, :], ACT.Abs))
                chain.step(nc.scalar.activation(g_e[:, :], g_e[:, :], ACT.Exp, scale=-1.0))
                nc.scalar.activation(g_e[:, :], g_e[:, :], ACT.Ln, bias=1.0).then_inc(gl_ln, 1)
                act.wait_ge(gl_dec, h.at(1))
                gx = g_x[:, :, :].rearrange("p a b -> p (a b)")
                chain.step(nc.scalar.activation(gx, gx, ACT.Abs))
                nc.scalar.activation(gx, gx, ACT.Exp, scale=-1.0 / 16.0).then_inc(gl_exp, 1)
                act.wait_ge(gl_o, h.at(1))
                for t in range(TT):
                    last = square(misf[1][:, t * GV:(t + 1) * GV], sq[:, t, :], ss_o[:, ds(i + 4 * t, 1)])
                last.then_inc(gl_sq, 1)
            chain.end(GH)
            act.wait_ge(lam_sum, 1)
            nc.scalar.activation(lam2, lam2, ACT.Exp).then_inc(lam_exp, 1)
            attend(GH, 2 * MH, db, False, True)
            nc.scalar.activation(sig[:, :, :], proj2[:, :, C2["gg"]:C2["gg"] + GH * GV], ACT.Silu)\
                .then_inc(silu_ok, 1)
            root(5, rs_o)
            for j in range(4):
                g0 = V_GLA if j < 2 else V_DIF
                side_hi(i4 + j, xa, 4 * j, gains(g0, 2) * 2, j % 2)

            n0, t0, i5, per = PH["o2"]

            def result_squares(par, ss4, j):
                for t in range(TT):
                    last = square(acc[par][:, t, :], stg2[:, t, :], ss4[:, 4 * t + j:4 * t + j + 1])
                    last.then_inc(squares if t == 0 else acc_free[par], 1)

            for j in range(DT):
                for c in range(per):
                    if c == LEAD and j > 0:
                        results(Count(n0), j * per - 1)
                        result_squares((t0 + j - 1) % 2, ss_m4, j - 1)
                    split(Count(n0), j * per + c)
            n0, t0, i6, per = PH["ffn2"]
            for c in range(LEAD):
                split(Count(n0), c)
            results(Count(n0), -1)
            result_squares((t0 - 1) % 2, ss_m4, DT - 1)
            root(6, rs_m)
            for j in range(DT):
                side_hi(i5 + j, xb, 4 * j, gains(V_PRE3 + 4 * j), j % 2)

            def conv_act(c, item, kb):
                if c == 7:
                    act.wait_ge(turned, item + 1)
                    for q in range(4):
                        last = nc.scalar.activation(conv[:, q, :], mis[0][:, q, :], ACT.Identity,
                                                    bias=vec[:, ds(kb + (V_CB + q), 1)],
                                                    scale=vec[:, ds(kb + (V_CW + 2 * KF + q), 1)])
                    last.then_inc(conv_tap, 1)
                if c == 9:
                    act.wait_ge(conv_ok, item + (1 - i6))
                    nc.scalar.activation(turned_a[:, :, :], conv[:, :, :], ACT.Gelu_apprx_tanh).then_inc(gelu_ok, 1)
                if c == 12:
                    act.wait_ge(prod_ok, item + (1 - i6))
                    nc.scalar.activation(ff[0][:, ds(kb, 4), :], conv[:, :, :], ACT.Copy).then_inc(hi_side, 1)

            for i in pairs(act, FT):
                n = Count(n0, i, 2 * per)
                first = isinstance(i, int)
                for c in range(2 * per):
                    if not first:
                        conv_act(c, i + (i6 - 1), i * 4 - 4)
                    if first and c == 5:
                        act.wait_ge(staged, stages(i5 + DT - 1))
                        for t in range(TT):
                            last = square(hres[:, t, :], mres[:, t, :], ss_x3[:, t:t + 1])
                        last.then_inc(squares, 1)
                    if first and c == 7:
                        root(7, rs_x3)
                        act.wait_ge(rstd_ok, 8)
                    if c == per + LEAD:
                        results(n, per - 1)
                        for t in range(TT):
                            nc.scalar.activation(stg[:, t, :], acc[t0 % 2][:, t, :], ACT.Copy,
                                                 scale=rs_x3[:, t:t + 1]).then_inc(acc_free[t0 % 2], 1)
                    if not (first and c < LEAD):
                        split(n, c)
            n0, t0, _, per = PH["down2"]
            for j in range(DT):
                for c in range(per):
                    if j == 0:
                        conv_act(c, i6 + FT - 1, 4 * (FT - 1))
                    if c == LEAD and j > 0:
                        results(Count(n0), j * per - 1)
                        result_squares((t0 + j - 1) % 2, ss_g4, j - 1)
                    split(Count(n0), j * per + c)
            results(Count(n0), DT * per - 1)
            result_squares((t0 + 3) % 2, ss_g4, DT - 1)
            root(8, rs_g)

        @block.vector
        def _(dve):
            chain = Chain(dve, dve_chain)
            V = nc.vector

            def split(n, c, width=W):
                slot = (n.start + c) % RING
                dve.wait_ge(hi_ready, n.at(c + 1))
                V.tensor_tensor(lo[:, slot, :, 0:width], raw[:, slot, :, 0:width],
                                hi[:, slot, :, 0:width].bitcast(F32), ALU.subtract).then_inc(lo_ready, 1)

            def norm(k, ss, rs, count, after):
                if after:
                    dve.wait_ge(squares, after)
                V.tensor_scalar(rs, ss, 1.0 / count, EPS, ALU.mult, ALU.add).then_inc(var_ok, 1)
                dve.wait_ge(root_ok, k + 1)
                V.reciprocal(rs, rs).then_inc(rstd_ok, 1)
                dve.wait_ge(rstd_ok, k + 1)

            def norm4(k, ss4, ss, rs, after):
                dve.wait_ge(squares, after)
                chain.step(V.tensor_reduce(ss, ss4.rearrange("p (t j) -> p t j", t=TT), AX.X, ALU.add))
                norm(k, ss, rs, D, 0)

            def side_lo(item, dst, kb, gain=None, pair=0, blocks=4):
                dve.wait_ge(hi_side, item + 1)
                if gain is None:
                    for half in range(2):
                        last = V.tensor_tensor(dst[1][:, ds(kb + 2 * half, 2), :],
                                               mis[pair][:, 2 * half:2 * half + 2, :],
                                               dst[0][:, ds(kb + 2 * half, 2), :].bitcast(F32), ALU.subtract)
                else:
                    for j in range(blocks):
                        last = V.scalar_tensor_tensor(dst[1][:, ds(kb + j, 1), :], mis[pair][:, j:j + 1, :], gain[j],
                                                      dst[0][:, ds(kb + j, 1), :].bitcast(F32), ALU.mult, ALU.subtract)
                last.then_inc(side, 1)

            def results(n, c):
                dve.wait_ge(chunk_used, n.at(c + 1))

            def ev(dst, par, scale, width=W):
                V.tensor_scalar(dst, acc[par][:, 1, 0:width], scale, None, ALU.mult).then_inc(acc_free[par], 1)

            dve.wait_ge(rows_turned, 1)
            V.tensor_copy(vec[:, 0:V_ROWS], misf[1][:, 0:V_ROWS])
            V.tensor_copy(vec[:, V_CW:V_CW + 2 * KF], misf[1][:, P:P + 2 * KF])
            V.tensor_copy(vec[:, V_CW + 2 * KF:V_ALL], misf[1][:, 2 * P:2 * P + 2 * KF]).then_inc(vec_ok, 1)
            dve.wait_ge(vec_ok, 1)
            chain.mark(V.tensor_tensor(gfin[:, :], vec[:, V_FIN:V_FIN + KD], vec[:, V_PRE2:V_PRE2 + KD], ALU.mult))
            dve.wait_ge(tab_in, 48)
            chain.step(V.tensor_copy(posf[:, :], posi[:, :]))
            for t in range(TT):
                chain.mark(V.tensor_scalar(ang[:, t, :], invf[:, :], posf[:, t:t + 1], None, ALU.mult))
            chain.join()
            chain.mark(V.tensor_scalar(trn[:, 0, :, :], ang[:, :, :], 1.0 / (2 * np.pi), 0.25, ALU.mult, ALU.add))
            chain.step(V.tensor_scalar(trn[:, 1, :, :], ang[:, :, :], 1.0 / (2 * np.pi), None, ALU.mult))
            chain.step(V.tensor_scalar(rnd[:, :, :, :], trn[:, :, :, :], MAGIC, None, ALU.add))
            chain.step(V.tensor_scalar(rnd[:, :, :, :], rnd[:, :, :, :], MAGIC, None, ALU.subtract))
            for k, part in enumerate(TWO_PI):
                for f in range(2):
                    chain.mark(V.scalar_tensor_tensor(trn[:, f, :, :], rnd[:, f, :, :], -part,
                                                      ang[:, :, :] if k == 0 else trn[:, f, :, :], ALU.mult, ALU.add))
                chain.join()
            chain.step(V.tensor_scalar(trn[:, 0, :, :], trn[:, 0, :, :], float(np.pi / 2), None, ALU.add))
            V.tensor_scalar(trn[:, :, :, :], trn[:, :, :, :], 3.1415925, -3.1415925, ALU.min, ALU.max)\
                .then_inc(ang_ok, 1)
            for j in range(4):
                side_lo(j, xa, 4 * j, gains(V_ATT + 4 * j), j % 2)
            n0, t0, _, per = PH["qkv"]
            for i in pairs(dve, 3):
                n = Count(n0, i, 2 * per)
                for j in range(2):
                    for c in range(per):
                        if c == 6 and j == 0 and isinstance(i, int):
                            norm(0, ss_x, rs_x, D, SQ["x"])
                        if c == LEAD and (j == 1 or not isinstance(i, int)):
                            results(n, j * per - 1)
                            ev(qkv[:, 1, ds(i * (2 * W) + (j - 1) * W, W)], (t0 + j - 1) % 2, rs_x[:, 1:2])
                        split(n, j * per + c)
            n0, t0, i0, per = PH["cq"]
            n = Count(n0)
            for c in range(per):
                if c == LEAD:
                    results(n, -1)
                    ev(qkv[:, 1, 5 * W:], (t0 - 1) % 2, rs_x[:, 1:2])
                split(n, c)
            n = Count(PH["ckv"][0])
            for c in range(per):
                if c == LEAD:
                    results(n, -1)
                    ev(stg[:, 1, :], t0 % 2, rs_x[:, 1:2])
                split(n, c, W_CKV)
            side_lo(i0, ct, 0, gains(V_Q))
            n, tu = Count(PH["uq"][0]), PH["uq"][1]
            for c in range(6):
                if c == LEAD:
                    results(n, -1)
                    ev(stg[:, 1, 0:W_CKV], (tu - 1) % 2, rs_x[:, 1:2], W_CKV)
                    dve.wait_ge(squares, SQ["c"])
                    chain.mark(V.tensor_scalar(rs_c[:, 0:2], ss_c[:, 0:2], 1.0 / QR, EPS, ALU.mult, ALU.add))
                    V.tensor_scalar(rs_c[:, 2:4], ss_c[:, 2:4], 1.0 / KVR, EPS, ALU.mult, ALU.add).then_inc(var_ok, 1)
                    dve.wait_ge(root_ok, 2)
                    V.reciprocal(rs_c, rs_c).then_inc(rstd_ok, 1)
                    side_lo(i0 + 1, ct, 4, gains(V_KV, 2), blocks=2)
                    dve.wait_ge(rstd_ok, 2)
                    results(n, 1)
                    ev(qm[:, 1, 0:W], tu % 2, rs_c[:, 1:2])
                split(n, c)
            n, tk = Count(PH["ukv"][0]), PH["ukv"][1]
            split(n, 0)
            results(n, -3)
            ev(qm[:, 1, W:2 * W], (tu + 1) % 2, rs_c[:, 1:2])
            split(n, 1)
            results(n, -1)
            ev(qm[:, 1, 2 * W:3 * W], (tu + 2) % 2, rs_c[:, 1:2])
            for j in range(4):
                if j < 2:
                    split(n, j + 2)
                results(n, j)
                ev(kvm[:, 1, j * W:(j + 1) * W], (tk + j) % 2, rs_c[:, 3:4])

            for par in range(2):
                dve.wait_ge(acc_free[par], 2 * ((tk + 4 + 1 - par) // 2))
            dve.wait_ge(cs_ok, 1)

            def rotate(x, t, heads, half, step):
                x1, x2 = x[:, :, 0:half], x[:, :, half:2 * half]
                co, si = (cs[:, t, f, ::step].unsqueeze(1).to_broadcast([P, heads, half]) for f in range(2))
                b = [r[:, 0:heads * half].rearrange("p (h f) -> p h f", h=heads) for r in rope_t]
                chain.mark(V.tensor_tensor(b[0], x1, co, ALU.mult))
                chain.mark(V.tensor_tensor(b[1], x2, si, ALU.mult))
                chain.mark(V.tensor_tensor(b[2], x2, co, ALU.mult))
                chain.step(V.tensor_tensor(b[3], x1, si, ALU.mult))
                chain.mark(V.tensor_tensor(x1, b[0], b[1], ALU.subtract))
                chain.step(V.tensor_tensor(x2, b[2], b[3], ALU.add))

            for t in range(TT):
                rotate(kr[:, t, :].unsqueeze(1), t, 1, ROPE // 2, 1)
                rotate(qkv[:, t, 0:2 * MH * MD].rearrange("p (h f) -> p h f", f=MD)[:, :, 0:MROPE], t,
                       2 * MH, MROPE // 2, 2)
                rotate(qm[:, t, :].rearrange("p (h f) -> p h f", f=NOPE + ROPE)[:, :, NOPE:], t,
                       MH, ROPE // 2, 1)
            V.engine_nop().then_inc(roped, 1)

            def attend(n_bodies, head0, b, scale, bias, diff):
                per = 7 if diff else 6
                with dve.Fori(0, n_bodies) as i:
                    h = Count(head0, i, 2)
                    chain.loop(i, 0, per)
                    for s in range(2):
                        dve.wait_ge(head_scores, h.at(s + 1))
                        p = b["p"][s]
                        chain.step(V.scalar_tensor_tensor(p[:, :], misf[s][:, W:W + 384], scale, bias[:, :],
                                                          ALU.mult, ALU.add))
                        V.tensor_reduce(mx[s][:, 0:1], p[:, 0:P], AX.X, ALU.max, negate=True)
                        V.tensor_reduce(mx[s][:, 1:2], p[:, P:384], AX.X, ALU.max, negate=True).then_inc(head_max, 1)
                    for s in range(2):
                        dve.wait_ge(head_exp, h.at(s + 1))
                        p = b["p"][s]
                        chain.step(V.reciprocal(rc[s][:, :], sm[s][:, :]))
                        if diff and s == 1:
                            chain.step(V.tensor_scalar(rc[s][:, :], rc[s][:, :], lam[:, 0:1], -1.0, ALU.mult, ALU.mult))
                            p0 = b["p"][0]
                            V.scalar_tensor_tensor(p0[:, 0:P], p[:, 0:P], rc[1][:, 0:1], p0[:, 0:P], ALU.mult, ALU.add)
                            V.scalar_tensor_tensor(p0[:, P:384], p[:, P:384], rc[1][:, 1:2], p0[:, P:384],
                                                   ALU.mult, ALU.add).then_inc(head_probs, 1)
                            continue
                        chain.mark(V.tensor_scalar(p[:, 0:P], p[:, 0:P], rc[s][:, 0:1], None, ALU.mult))
                        V.tensor_scalar(p[:, P:384], p[:, P:384], rc[s][:, 1:2], None, ALU.mult)\
                            .then_inc(head_probs, 1)
                        if diff:
                            dve.wait_ge(head_probs, h.at(1))
                    if not diff:
                        for s in range(2):
                            dve.wait_ge(y_hi, h.at(s + 1))
                            y = ds(i * 2 + (head0 + s), 1)
                            V.tensor_tensor(xb[1][:, y, :], mis[s][:, 2:3, :], xb[0][:, y, :].bitcast(F32),
                                            ALU.subtract).then_inc(y_done, 1)
                    else:
                        chain.step(V.tensor_scalar(bias[:, :], bias[:, :], 0.25, None, ALU.mult))
                        dve.wait_ge(y_hi, h.at(2))
                        V.tensor_copy(obuf[:, :, ds(i * GV + GH * GV, GV)],
                                      misf[0][:, W:W + 2 * GV].rearrange("p (t e) -> p t e", t=TT))\
                            .then_inc(y_done, 2)
                chain.end(n_bodies)

            dve.wait_ge(masks_ok, 1)
            attend(MH // 2, 0, ab, float(MD) ** -0.5, causal, False)
            attend(MH // 2, MH, ab, float(NOPE + ROPE) ** -0.5, causal, False)

            n0, t0, _, per = PH["gate"]
            with dve.Fori(0, 4) as i:
                for c in range(2 * per):
                    split(Count(n0, i, 2 * per), c)
            n0, t0, i0, per = PH["branch"]

            def gated(par, dst, col):
                for t in range(TT):
                    V.tensor_tensor(dst[:, t, :], acc[par][:, t, :], gates[:, t, ds(col, W)], ALU.mult)\
                        .then_inc(acc_free[par], 1)

            def mix(tile_b, col):
                par = (t0 + 1) % 2
                gated(par, stg2, col)
                dve.wait_ge(acc_free[par], tile_b.at(2))
                V.tensor_tensor(stg[:, :, :], stg[:, :, :], stg2[:, :, :], ALU.add).then_inc(staged, 2)

            even = t0 - t0 % 2
            odd = (t0 + 1) - (t0 + 1) % 2
            for i in pairs(dve, DT):
                n = Count(n0, i, 2 * per)
                first = isinstance(i, int)
                for c in range(2 * per):
                    if c == LEAD and not first:
                        results(n, -1)
                        mix(Count(odd - 2, i, 2), i * W + (D - W))
                    if not first and c == 7:
                        side_lo(i + (i0 - 1), xa, i * 4 - 4)
                    if c == 7:
                        if first:
                            for par in range(2):
                                dve.wait_ge(acc_free[par], 2 * ((t0 + 1 - par) // 2))
                        results(n, per - 1)
                        gated(t0 % 2, stg, i * W)
                    split(n, c)

            def add(item, n, c, par, old):
                results(n, c)
                for t in range(TT):
                    V.tensor_tensor(stg[:, t, :], acc[par][:, t, :], old[:, t, :], ALU.add).then_inc(acc_free[par], 1)
                V.engine_nop().then_inc(staged, 1)

            i1 = PH["out"][2]
            n0, t1, _, per = PH["out"]
            for j in range(DT):
                for c in range(per):
                    if c == LEAD and j == 0:
                        results(Count(n0), -1)
                        mix(Count(odd + 2 * (DT - 1)), D + (DT - 1) * W)
                    if c == LEAD and j > 0:
                        dve.wait_ge(res_in, 16 * j)
                        add(i1 + j - 1, Count(n0), j * per - 1, (t1 + j - 1) % 2, res)
                    if c == 7 and j == 0:
                        side_lo(i1 - 1, xa, 4 * (DT - 1))
                    if c == 7 and j > 0:
                        side_lo(i1 + j - 1, xb, 4 * (j - 1), gains(V_FFN + 4 * (j - 1)))
                    split(Count(n0), j * per + c)
            n0, t0, i2, per = PH["ffn"]

            def swiglu(n, gate_tiles):
                par = (t0 + 1) % 2
                dve.wait_ge(acc_free[t0 % 2], gate_tiles)
                results(n, -1)
                for t in range(TT):
                    V.scalar_tensor_tensor(stg[:, t, :], acc[par][:, t, :], rs_h[:, t:t + 1], stg2[:, t, :],
                                           ALU.mult, ALU.mult).then_inc(acc_free[par], 1)
                V.engine_nop().then_inc(staged, 2)

            for i in pairs(dve, FT):
                n = Count(n0, i, 2 * per)
                first = isinstance(i, int)
                for c in range(2 * per):
                    if c == LEAD and first:
                        dve.wait_ge(res_in, 16 * DT)
                        add(i2 - 1, n, -1, (t0 - 1) % 2, res)
                        norm4(2, ss_h4, ss_h, rs_h, SQ["h"])
                    if c == LEAD and not first:
                        swiglu(n, i * 2 + (t0 - t0 % 2))
                    if c == 7 and first:
                        side_lo(i2 - 1, xb, 4 * (DT - 1), gains(V_FFN + 12))
                    if c == 7 and not first:
                        side_lo(i + (i2 - 1), ff, i * 4 - 4)
                    split(n, c)
            tg = t0 - t0 % 2 + 2 * FT
            n0, t1, i3, per = PH["down"]
            for j in range(DT):
                for c in range(per):
                    if c == LEAD and j == 0:
                        swiglu(Count(n0), tg)
                    if c == LEAD and j > 0:
                        add(i3 + j - 1, Count(n0), j * per - 1, (t1 + j - 1) % 2, hres[:, :, (j - 1) * W:j * W])
                    if c == 7 and j == 0:
                        side_lo(i3 - 1, ff, 4 * (FT - 1))
                    if c == 7 and j > 0:
                        side_lo(i3 + j - 1, xb, 4 * (j - 1), [gfin[:, 4 * j - 4 + q:4 * j - 3 + q] for q in range(4)])
                    split(Count(n0), j * per + c)
            n0, t0, _, per = PH["in2a"]
            for i in pairs(dve, 3):
                n = Count(n0, i, 2 * per)
                first = isinstance(i, int)
                for j in range(2):
                    for c in range(per):
                        if c == LEAD and first and j == 0:
                            add(i3 + DT - 1, n, -1, (t0 - 1) % 2, hres[:, :, (DT - 1) * W:])
                            norm4(3, ss_f4, ss_f, rs_f, SQ["f"])
                        if c == 7 and first and j == 0:
                            side_lo(i3 + DT - 1, xb, 12, [gfin[:, q:q + 1] for q in range(12, 16)])
                        if c == 0 and first and j == 1:
                            dve.wait_ge(gbc_in, 16)
                            dve.wait_ge(staged, stages(i3 + DT - 1))
                            for t in range(TT):
                                last = V.scalar_tensor_tensor(hres[:, t, :], hres[:, t, :], rs_f[:, t:t + 1],
                                                              gfbc[:, :], ALU.mult, ALU.mult)
                            last.then_inc(x2_ok, 1)
                        if c == 1 and first and j == 1:
                            dve.wait_ge(squares, SQ["x2"])
                            V.tensor_scalar(rs_x2, ss_x2, 1.0 / D, EPS, ALU.mult, ALU.add).then_inc(var_ok, 1)
                            dve.wait_ge(root_ok, 5)
                            chain.step(V.reciprocal(rs_x2, rs_x2))
                            V.tensor_tensor(rs_in2, rs_x2, rs_f, ALU.mult).then_inc(rstd_ok, 1)
                            dve.wait_ge(rstd_ok, 5)
                        if c == LEAD and (j == 1 or not first):
                            results(n, j * per - 1)
                            ev(proj2[:, 1, ds(i * (2 * W) + (j - 1) * W, W)], (t0 + j - 1) % 2, rs_in2[:, 1:2])
                        split(n, j * per + c)
            n, t1 = Count(PH["ga"][0]), PH["ga"][1]
            for c in range(per):
                if c == LEAD:
                    results(n, -1)
                    ev(proj2[:, 1, 5 * W:6 * W], (t1 - 1) % 2, rs_in2[:, 1:2])
                split(n, c, GR)
            n0, t0, i4, per = PH["in2b"]
            for i in pairs(dve, 3):
                n = Count(n0, i, 2 * per)
                for j in range(2):
                    for c in range(per):
                        if c == LEAD:
                            results(n, j * per - 1)
                            if isinstance(i, int) and j == 0:
                                ev(kr[:, 1, 0:GR], t1 % 2, rs_in2[:, 1:2], GR)
                            else:
                                ev(proj2[:, 1, ds(i * (2 * W) + ((j - 1) * W + C2["dq"]), W)],
                                   (t0 + j - 1) % 2, rs_in2[:, 1:2])
                        split(n, j * per + c)
            results(Count(n0), 6 * per - 1)
            ev(proj2[:, 1, 5 * W + C2["dq"]:6 * W + C2["dq"]], (t0 + 5) % 2, rs_in2[:, 1:2])

            with dve.Fori(0, GH) as i:
                h = Count(0, i, 1)
                chain.loop(i, 0, 5)
                dve.wait_ge(gl_turned, h.at(1))
                V.tensor_scalar(g_z[:, :], misf[0][:, W:W + T], vec[:, ds(i + V_BAL, 1)], None, ALU.add)\
                    .then_inc(gl_z, 1)
                dve.wait_ge(gl_ln, h.at(1))
                chain.step(V.scalar_tensor_tensor(g_z[:, :], g_z[:, :], 0.0, g_e[:, :], ALU.min, ALU.subtract))
                chain.step(V.tensor_tensor_scan(g_b[:, :], g_chunk[:, :], g_z[:, :], 0.0, ALU.mult, ALU.add))
                for lv in range(6):
                    s = 1 << lv
                    b = g_b[:, :].rearrange("p (n s) -> p n s", s=2 * s)
                    V.tensor_tensor(g_x[:, lv, :].rearrange("p (n s) -> p n s", s=2 * s), b,
                                    b[:, :, s - 1:s].to_broadcast([P, T // (2 * s), 2 * s]), ALU.subtract)
                b = g_b[:, :].rearrange("p (n s) -> p n s", s=64)
                x6 = g_x[:, 6, :].rearrange("p (n s) -> p n s", s=64)
                x7 = g_x[:, 7, :].rearrange("p (n s) -> p n s", s=64)
                for k in range(4):
                    if k % 2 == 0:
                        V.tensor_scalar(x6[:, k, :], b[:, k, :], b[:, k, 63:64], None, ALU.subtract)
                    else:
                        V.tensor_copy(x6[:, k, :], b[:, k, :])
                V.tensor_scalar(x7[:, 0, :], b[:, 0, :], b[:, 0, 63:64], b[:, 1, 63:64], ALU.subtract, ALU.subtract)
                V.tensor_scalar(x7[:, 1, :], b[:, 1, :], b[:, 1, 63:64], None, ALU.subtract)
                V.tensor_copy(x7[:, 2, :], b[:, 2, :])
                V.tensor_scalar(x7[:, 3, :], b[:, 3, :], b[:, 2, 63:64], None, ALU.add).then_inc(gl_dec, 1)
                dve.wait_ge(gl_exp, h.at(1))
                dve.wait_ge(gl_qk, h.at(1))
                for lv in range(LEVELS):
                    s = 1 << lv
                    for half, x in ((0, 1), (1, 0)):
                        o = g_x[:, lv, :].rearrange("p (n h s) -> p n h s", h=2, s=s)[:, :, half, :]
                        v = g_qk[:, x, :].rearrange("p (n h s) -> p n h s", h=2, s=s)[:, :, half, :]
                        last = V.tensor_tensor(o, o, v, ALU.mult)
                last.then_inc(gl_x, 1)
                dve.wait_ge(gl_lev, h.at(1))
                gm = g_m[:, :, :].rearrange("p a b -> p (a b)")
                for t in range(TT):
                    chain.step(V.tensor_tensor(gm, accf[t], lmask[:, :, :].rearrange("p a b -> p (a b)"), ALU.mult))
                    last = V.tensor_reduce(g_at[:, t, :], g_m[:, :, :].rearrange("p l i -> p i l"), AX.X, ALU.add)
                    if t == 0:
                        chain.step(last)
                V.tensor_scalar(g_at[:, 2, :], misf[0][:, W + T:W + T + P], float(GK) ** -0.5, None, ALU.mult)\
                    .then_inc(gl_at, 1)
                dve.wait_ge(gl_sq, h.at(1))
                V.tensor_copy(obuf[:, :, ds(i * GV, GV)], misf[1][:, 0:2 * GV].rearrange("p (t e) -> p t e", t=TT))\
                    .then_inc(gl_out, 1)
            chain.end(GH)
            dve.wait_ge(lam_in, 64)
            chain.step(V.tensor_tensor(lamj[:, :, :], lamr[:, 0:2, :], lamr[:, 2:4, :], ALU.mult))
            V.tensor_reduce(lam2, lamj[:, :, :], AX.X, ALU.add).then_inc(lam_sum, 1)
            dve.wait_ge(lam_exp, 1)
            chain.step(V.tensor_tensor(lam, lam2[:, 0:1], lam2[:, 1:2], ALU.subtract))
            chain.step(V.tensor_scalar(lam, lam, LAMBDA_INIT, None, ALU.add))
            dve.wait_ge(bias_ok, 1)
            attend(GH, 2 * MH, db, float(GK) ** -0.5, dbias, True)
            dve.wait_ge(gl_sq, GH)
            dve.wait_ge(y_done, 4 * MH - 2 * MH + 2 * GH)
            norm(5, ss_o, rs_o, GV, 0)
            dve.wait_ge(silu_ok, 1)

            def strip_o(j):
                for t in range(TT):
                    for g in range(2):
                        h = (2 * j + g) % GH
                        o = obuf[:, t, j * W + g * GV:j * W + (g + 1) * GV]
                        if j < 2:
                            V.scalar_tensor_tensor(o, o, rs_o[:, 4 * t + h:4 * t + h + 1],
                                                   sig[:, t, h * GV:(h + 1) * GV], ALU.mult, ALU.mult)
                        else:
                            V.tensor_scalar(o, o, rs_o[:, 8 + 4 * t + h:9 + 4 * t + h], 1.0 - LAMBDA_INIT,
                                            ALU.mult, ALU.mult)
                V.engine_nop().then_inc(staged, 2)

            strip_o(0)
            strip_o(1)
            for j in range(4):
                g0 = V_GLA if j < 2 else V_DIF
                side_lo(i4 + j, xa, 4 * j, gains(g0, 2) * 2, j % 2)
                if j + 2 < 4:
                    strip_o(j + 2)
            n0, t0, i5, per = PH["o2"]

            def gained(dst, tile_no, gain, squared):
                par = tile_no % 2
                dve.wait_ge(squares, squared)
                V.tensor_tensor(dst[:, 0, :], acc[par][:, 0, :], gain, ALU.mult)
                dve.wait_ge(acc_free[par], 2 * (tile_no // 2) + 1)
                V.tensor_tensor(dst[:, 1, :], acc[par][:, 1, :], gain, ALU.mult).then_inc(acc_free[par], 1)

            for j in range(DT):
                for c in range(per):
                    if c == LEAD and j > 0:
                        results(Count(n0), j * per - 1)
                        dve.wait_ge(gbc_in, 32)
                        gained(mres[:, :, (j - 1) * W:j * W], t0 + j - 1, g2bc[:, (j - 1) * W:j * W],
                               SQ["x2"] + j)
                    split(Count(n0), j * per + c)
            t_last = t0 + DT - 1
            n0, t0, i6, per = PH["ffn2"]
            for c in range(LEAD):
                split(Count(n0), c)
            results(Count(n0), -1)
            gained(mres[:, :, (DT - 1) * W:], t_last, g2bc[:, (DT - 1) * W:], SQ["m"])
            dve.wait_ge(acc_free[t_last % 2], 2 * (t_last // 2 + 1))
            norm4(6, ss_m4, ss_m, rs_m, SQ["m"])

            def strip_x3(j):
                for t in range(TT):
                    x = hres[:, t, j * W:(j + 1) * W]
                    V.scalar_tensor_tensor(x, mres[:, t, j * W:(j + 1) * W], rs_m[:, t:t + 1], x, ALU.mult, ALU.add)
                V.engine_nop().then_inc(staged, 2)

            strip_x3(0)
            strip_x3(1)
            for j in range(DT):
                side_lo(i5 + j, xb, 4 * j, gains(V_PRE3 + 4 * j), j % 2)
                if j + 2 < DT:
                    strip_x3(j + 2)

            def conv_dve(c, item, kb):
                if c == 8:
                    dve.wait_ge(conv_tap, item + (1 - i6))
                    for shift in (1, 2):
                        for q in range(4):
                            last = V.scalar_tensor_tensor(
                                conv[:, q, shift:T], mis[0][:, q, 0:T - shift],
                                vec[:, ds(kb + (V_CW + (2 - shift) * KF + q), 1)], conv[:, q, shift:T],
                                ALU.mult, ALU.add)
                            if shift == 1:
                                chain.mark(last)
                        if shift == 1:
                            chain.join()
                    last.then_inc(conv_ok, 1)
                if c == 10:
                    dve.wait_ge(gelu_ok, item + (1 - i6))
                    V.tensor_tensor(conv[:, :, :], turned_a[:, :, :], mis[1][:, :, :], ALU.mult).then_inc(prod_ok, 1)
                if c == 13:
                    dve.wait_ge(hi_side, item + 1)
                    V.tensor_tensor(ff[1][:, ds(kb, 4), :], conv[:, :, :], ff[0][:, ds(kb, 4), :].bitcast(F32),
                                    ALU.subtract).then_inc(side, 1)

            def stage_b(n):
                results(n, -1)
                for t in range(TT):
                    V.tensor_scalar(stg2[:, t, :], acc[(t0 + 1) % 2][:, t, :], rs_x3[:, t:t + 1], None, ALU.mult)\
                        .then_inc(acc_free[(t0 + 1) % 2], 1)
                V.engine_nop().then_inc(staged, 2)

            for i in pairs(dve, FT):
                n = Count(n0, i, 2 * per)
                first = isinstance(i, int)
                if not first:
                    chain.loop(i, 1, 4)
                for c in range(2 * per):
                    if not first:
                        if c == LEAD:
                            stage_b(n)
                        conv_dve(c, i + (i6 - 1), i * 4 - 4)
                    if first and c == 7:
                        norm(7, ss_x3, rs_x3, D, SQ["x3"])
                    if not (first and c < LEAD):
                        split(n, c)
            chain.end(FT - 1)
            n0, t1, _, per = PH["down2"]
            for j in range(DT):
                for c in range(per):
                    if j == 0:
                        if c == LEAD:
                            stage_b(Count(n0))
                        conv_dve(c, i6 + FT - 1, 4 * (FT - 1))
                    if c == LEAD and j > 0:
                        results(Count(n0), j * per - 1)
                        dve.wait_ge(gbc_in, 48)
                        gained(frow[:, :, (j - 1) * W:j * W], t1 + j - 1, gf2bc[:, (j - 1) * W:j * W],
                               SQ["x3"] + j)
                    split(Count(n0), j * per + c)
            results(Count(n0), DT * per - 1)
            gained(frow[:, :, (DT - 1) * W:], t1 + 3, gf2bc[:, (DT - 1) * W:], SQ["g"])
            dve.wait_ge(acc_free[(t1 + 3) % 2], 2 * ((t1 + 3) // 2 + 1))
            norm4(8, ss_g4, ss_g, rs_g, SQ["g"])
            for j in range(DT):
                for t in range(TT):
                    x = frow[:, t, j * W:(j + 1) * W]
                    V.scalar_tensor_tensor(x, x, rs_g[:, t:t + 1], hres[:, t, j * W:(j + 1) * W], ALU.mult, ALU.add)\
                        .then_inc(fin_ok, 1)

        @block.gpsimd
        def _(pool):
            chain = Chain(pool, pool_chain)
            G_ = nc.gpsimd

            def select(out, pattern, base, mult, compare, fill):
                return G_.affine_select(out=out, in_=out, compare_op=compare, fill=fill, base=base,
                                        pattern=pattern, channel_multiplier=mult)

            G_.memset(ident[:, :], 0.0).then_inc(ident_ok, 1)
            pool.wait_ge(ident_ok, 1)
            select(ident[:, :], [[-1, P]], 0, 1, ALU.not_equal, 1.0).then_inc(ident_ok, 1)
            chain.step(G_.memset(causal[:, :], 0.0))
            select(causal[:, 0:P], [[-1, P]], 0, 1, ALU.is_ge, NEG)
            select(causal[:, P:384], [[-1, T]], P, 1, ALU.is_ge, NEG).then_inc(masks_ok, 1)

            def stage(n_bodies, head0, parts, last_part):
                for i in pairs(pool, n_bodies):
                    h = Count(head0, i, 2)
                    for s in range(2):
                        if h.low(s) >= 2:
                            pool.wait_ge(last_part, h.at(s - 1))
                        for dst, src, col, width in parts:
                            last = G_.tensor_copy(dst[s][:, :, :], src[:, :, ds(i * (2 * width[1]) + (col + s * width[1]), width[0])])
                        last.then_inc(head_in, 1)

            pool.wait_ge(roped, 1)
            stage(MH // 2, 0, [(ab["q"], qkv, 0, (MD, MD)), (ab["k"], qkv, MH * MD, (MD, MD)),
                               (vs, qkv, 2 * MH * MD, (MD, MD))], head_y)
            stage(MH // 2, MH, [(ab["q"], qm, 0, (NOPE, NOPE + ROPE)), (qrs, qm, NOPE, (ROPE, NOPE + ROPE)),
                                (ab["k"], kvm, 0, (NOPE, NOPE + MD)), (vs, kvm, NOPE, (MD, NOPE + MD))], head_y)
            for j in range(DT):
                if j:
                    pool.wait_ge(staged, stages(PH["out"][2] + j - 1) - 1)
                pool.dma_start(res[:, :, :], a["x"][0].rearrange("(t p) n -> p t n", p=P)[:, :, j * W:(j + 1) * W])\
                    .then_inc(res_in, 16)
            pool.wait_ge(chunk_used, PH["in2a"][0])
            pool.dma_start(gfbc[:, :], a["final_norm"].partition_broadcast(P)).then_inc(gbc_in, 16)
            for k, name in enumerate(("lambda_q1_2", "lambda_q2_2", "lambda_k1_2", "lambda_k2_2")):
                pool.dma_start(lamr[:, k, :], a[name][0].partition_broadcast(P)).then_inc(lam_in, 16)
            chain.step(G_.iota(dbias[:, 0:P], [[-1, P]], base=0, channel_multiplier=1,
                               allow_small_or_imprecise_dtypes=True))
            chain.step(G_.iota(dbias[:, P:384], [[-1, T]], base=P, channel_multiplier=1,
                               allow_small_or_imprecise_dtypes=True))
            chain.step(select(dbias[:, 0:P], [[-1, P]], 0, 1, ALU.is_ge, -NEG))
            chain.step(select(dbias[:, P:384], [[-1, T]], P, 1, ALU.is_ge, -NEG))
            G_.tensor_scalar(dbias[:, :], dbias[:, :], -0.25, None, ALU.mult).then_inc(bias_ok, 1)
            pool.wait_ge(rstd_ok, 5)
            pool.dma_start(walpha[0:GR, :], a["w_alpha_up_2"][0]).then_inc(wa_in, 16)
            chain.step(G_.memset(g_chunk[:, :], 1.0))
            chain.step(G_.memset(g_chunk[:, ::64], 0.0))
            sc = float(GK) ** -0.5
            chain.step(G_.memset(lmask[:, :, :], 0.0))
            for lv in range(LEVELS - 1):
                s = 1 << lv
                mk = lmask[:, lv, :].rearrange("p (n h s) -> p n h s", h=2, s=s)
                chain.step(G_.memset(mk[:, :, 1, :], sc))
                nb = P // (2 * s)
                flat = lmask[:, lv, :].rearrange("p (n s) -> p n s", s=2 * s)
                chain.step(select(flat, [[-2 * s, nb], [0, 2 * s]], 0, 1, ALU.is_ge, 0.0))
                chain.step(select(flat, [[2 * s, nb], [0, 2 * s]], s - 1, -1, ALU.is_ge, 0.0))
            chain.step(select(lmask[:, LEVELS - 1, :], [[-1, P]], 0, 1, ALU.not_equal, sc))
            pool.wait_ge(wa_in, 16)
            n0, t0, _, per = PH["in2b"]
            for par in range(2):
                pool.wait_ge(acc_free[par], 2 * ((t0 + 6 + 1 - par) // 2))
            with pool.Fori(0, GH) as i:
                h = Count(0, i, 1)
                pool.wait_ge(gl_turned, h.at(0))
                G_.tensor_copy(g_w[0:GR, :], walpha[0:GR, ds(i * GK, GK)])
                G_.tensor_copy(gq_s[:, :, :], proj2[:, :, ds(i * GK + C2["gq"], GK)])
                G_.tensor_copy(gk_s[:, :, :], proj2[:, :, ds(i * GK + C2["gk"], GK)]).then_inc(gl_staged, 1)
            pool.wait_ge(gl_out, GH)
            pool.wait_ge(gl_sq, GH)
            stage(GH, 2 * MH, [(db["q"], proj2, C2["dq"], (GK, GK)), (db["k"], proj2, C2["dk"], (GK, GK))], head_turned)
            pool.wait_ge(y_done, 2 * MH + 2 * GH)
            pool.wait_ge(silu_ok, 1)
            pool.dma_start(g2bc[:, :], a["attn_post_norm_2"][0].partition_broadcast(P)).then_inc(gbc_in, 16)
            pool.wait_ge(chunk_used, PH["down2"][0])
            pool.dma_start(gf2bc[:, :], a["ffn_post_norm_2"][0].partition_broadcast(P)).then_inc(gbc_in, 16)


_INS = ["x", "positions", "attn_norm", "w_in", "q_norm", "w_uq", "kv_norm", "w_ukv", "w_branch_a", "w_branch_b",
        "w_out", "ffn_norm", "w_gate", "w_up", "w_down", "final_norm", "attn_pre_norm_2", "w_in_2", "w_alpha_up_2",
        "b_alpha_2", "gla_norm_2", "lambda_q1_2", "lambda_k1_2", "lambda_q2_2", "lambda_k2_2", "diff_norm_2",
        "w_o_2", "attn_post_norm_2", "ffn_pre_norm_2", "w_ffn_in_2", "conv_w_2", "conv_b_2", "w_ffn_out_2",
        "ffn_post_norm_2"]


def kernel(**inputs):
    import concourse.bacc as _bacc
    from concourse.bass_utils import run_bass_kernel_spmd as _run

    nc = _bacc.Bacc("TRN2", target_bir_lowering=False, num_devices=1)
    arrays = {name: np.ascontiguousarray(inputs[name]) for name in _INS}
    arrays["inv_freq"] = (THETA ** (-np.arange(0, ROPE, 2, dtype=np.float64) / ROPE)).astype(np.float32)
    args = {name: nc.dram_tensor(f"in_{name}", v.shape, mybir.dt.from_np(v.dtype), kind="ExternalInput").ap()
            for name, v in arrays.items()}
    out = nc.dram_tensor("out", (1, T, D), F32, kind="ExternalOutput").ap()
    two_blocks(nc, args, out)
    r = _run(nc, [{f"in_{name}": v for name, v in arrays.items()}], core_ids=[0])
    return r.results[0]["out"]
```

```python
from contextlib import ExitStack

import numpy as np

import concourse.bass as bass
from concourse import mybir

F32 = mybir.dt.float32
F32R = mybir.dt.float32r
I32 = mybir.dt.int32
ALU = mybir.AluOpType
ACT = mybir.ActivationFunctionType
AX = mybir.AxisListType
ds = bass.ds

P = 128
TT = 2
T = P * TT
W = 512
CK = 2
RING = 4
LEAD = 3
D = 2048
KD = D // P
DT = D // W
DFF = 5632
KF = DFF // P
FT = DFF // W
EPS = 1e-6
NEG = -1e30

MH, MD = 8, 128
NOPE, ROPE, QR, KVR = 128, 64, 512, 256
MROPE = 32
QKV = 3 * MH * MD
C_CQ = QKV
C_CKV = C_CQ + QR
W_CKV = KVR + ROPE
C_GATE = C_CKV + W_CKV
UQ = MH * (NOPE + ROPE)
UKV = MH * (NOPE + MD)
THETA = 500000.0

GH, GK, GV, GR = 4, 128, 256, 16
LEVELS = 8
C2 = dict(gq=0, gk=512, gv=1024, gg=2048, ga=3072, dq=3088, dk=4112, dv=5136)
IN2 = 6160
BESIDE = [C2["gv"], C2["gv"] + W, C2["dq"], C2["dk"], C2["dv"], C2["dq"] + W, C2["dk"] + W, C2["dv"] + W,
          C2["gg"], C2["gg"] + W]
NB = len(BESIDE)
PERIOD = 7
MOBA_FIRST, MLA_FIRST = 4, 4
GLA_FIRST, GLA_PERIOD = 7, 9
DIFF_FIRST = 48
TWO_PI = (6.28125, 0.0019350051879882812, 3.0198494e-07)
MAGIC = 12582912.0
LAMBDA_INIT = 0.2

A0, E0, H0, B0, R0, M0 = 0, 8192, 22528, 26624, 34816, 47104
END = 53200

V_ATT, V_Q, V_KV, V_FFN, V_FIN, V_PRE2, V_PRE3, V_BAL, V_GLA, V_DIF, V_ROWS = 0, 16, 20, 22, 38, 54, 70, 86, 90, 92, 94
V_CW, V_CB = 94, 94 + 3 * KF
V_ALL = V_CB + KF


class Count:

    def __init__(self, start, i=0, per=0):
        self.start, self.i, self.per = start, i, per

    def at(self, k):
        if self.per == 0 or (isinstance(self.i, int) and self.i == 0):
            return self.start + k
        return self.i * self.per + (self.start + k)

    def low(self, k):
        return self.start + k + (self.per * self.i if isinstance(self.i, int) else self.per)


class Chain:

    def __init__(self, eng, sem):
        self.eng, self.sem, self.base, self.k = eng, sem, 0, 0
        self.i, self.i0, self.per = 0, 0, 0

    def loop(self, i, i0, per):
        self.base, self.k = self.base + self.k, 0
        self.i, self.i0, self.per = i, i0, per

    def end(self, turns):
        assert self.k == self.per, f"the body's chain has {self.k} steps, not {self.per}"
        self.base, self.k, self.per = self.base + turns * self.per, 0, 0

    def mark(self, ins):
        ins.then_inc(self.sem, 1)
        self.k += 1

    def join(self):
        value = self.base + self.k
        if self.per:
            value = self.i * self.per + (value - self.i0 * self.per)
        self.eng.wait_ge(self.sem, value)

    def step(self, ins):
        self.mark(ins)
        self.join()


def pairs(eng, n):
    yield 0
    if n > 1:
        with eng.Fori(1, n) as i:
            yield i


def due(g, first, period, step, n):
    turn, rest = divmod(g - first - step, period)
    return turn if rest == 0 and 0 <= turn < n else None


def landed(n, c):
    return Count(16 * ((n.start + c) // RING + 1), n.i, 16 * n.per // RING).at(0)


def rows_of(w):
    return w.rearrange("l (k p) n -> p (l k) n", p=P)


def two_blocks(nc, a, out):
    ctx = ExitStack()
    with ctx:
        base = -(-nc.sbuf_base // 64) * 64

        def psum(name, shape):
            return ctx.enter_context(nc.psum_tensor(name, shape, F32))

        def sem(name):
            return ctx.enter_context(nc.semaphore(name))

        def at(name, word, shape, dt=F32):
            return nc.alloc_sbuf_tensor_at(name, [P] + shape, dt, offset=base + 4 * word)

        xa = [at("xa_hi", A0, [KD, T], F32R), at("xa_lo", A0 + 4096, [KD, T], F32R)]
        xb = [at("xb_hi", B0, [KD, T], F32R), at("xb_lo", B0 + 4096, [KD, T], F32R)]
        ff = [at("ff_hi", A0, [KF, T], F32R), at("ff_lo", A0 + KF * T, [KF, T], F32R)]
        xin = at("xin", H0, [TT, D])
        hres = at("hres", H0, [TT, D])
        ct = [at("ct_hi", H0 + 1024, [6, T], F32R), at("ct_lo", H0 + 1024 + 6 * T, [6, T], F32R)]
        gates = at("gates", E0, [TT, 2 * D])
        qkv = at("qkv", E0 + 8192, [TT, QKV])
        qm = at("qm", E0 + 8192, [TT, UQ])
        kvm = at("kvm", E0 + 8192 + TT * UQ, [TT, UKV])
        proj2 = at("proj2", E0, [TT, IN2])
        g2bc = at("g2bc", E0 + 6144, [D])
        mres = at("mres", E0, [TT, D])
        frow = at("frow", B0, [TT, D])
        gfbc = at("gfbc", A0, [D])
        gf2bc = at("gf2bc", B0 + 4096, [D])
        sqx2 = at("sqx2", A0 + 2048, [TT, D])
        raw = at("raw", R0, [RING, CK, W])
        hi = at("hi", R0 + 4096, [RING, CK, W], F32R)
        lo = at("lo", R0 + 8192, [RING, CK, W], F32R)
        m = M0
        stg = at("stg", m, [TT, W]); m += 1024
        stg2 = at("stg2", m, [TT, W]); m += 1024
        res = at("res", m, [TT, W])
        conv = at("conv", m, [4, T]); m += 1024
        lmask = at("lmask", m, [LEVELS, P])
        turned_a = at("turned_a", m, [4, T]); m += 1024
        ident = at("ident", m, [P]); m += P
        vec = at("vec", m, [V_ALL]); m += V_ALL + (-V_ALL) % 8
        gfin = at("gfin", m, [KD]); m += KD
        cs = at("cs", m, [TT, 2, ROPE // 2]); m += 128
        causal = at("causal", m, [384]); m += 384
        kr = at("kr", m, [TT, ROPE]); m += 128
        small = at("small", m, [256]); m += 256
        assert m <= END, m
        rows = at("rows", E0, [3, P])
        ang = at("ang", E0 + 512, [TT, 32])
        trn = at("trn", E0 + 640, [2, TT, 32])
        rnd = at("rnd", E0 + 768, [2, TT, 32])
        invf = at("invf", E0 + 896, [32])
        posi = at("posi", E0 + 960, [TT], I32)
        posf = at("posf", E0 + 968, [TT])
        junk = at("junk", E0 + 1024, [TT, D])
        ab = dict(qk=[at(f"ab_qk{s}", M0 + 1024 + 512 * s, [2, T]) for s in range(2)],
                  p=[at(f"ab_p{s}", M0 + 2048 + 384 * s, [384]) for s in range(2)],
                  pt=[at(f"ab_pt{s}", M0 + 3072 + 384 * s, [384]) for s in range(2)])
        qr = at("qr", H0 + 1024, [TT, MH * ROPE])
        krz = at("krz", H0 + 2048, [TT, 2, P])
        qrt = at("qrt", H0 + 2560, [MH // 2, T])
        krt = at("krt", H0 + 3584, [2, T])
        rope_t = [at(f"rope_t{j}", B0 + 2048 + 512 * j, [512]) for j in range(4)]
        dbias = at("dbias", E0 + TT * IN2, [384])
        lamr = at("lamr", E0 + TT * IN2 + 384, [4, P])
        lamj = at("lamj", E0 + TT * IN2 + 896, [2, P])
        sq = at("sq", E0 + TT * IN2 + 1152, [TT, GV])
        db = dict(qk=[at(f"db_qk{s}", A0 + 3072 + 512 * s, [2, T]) for s in range(2)],
                  p=[at(f"db_p{s}", A0 + 7168 + 384 * s, [384]) for s in range(2)],
                  pt=[at("db_pt", A0 + 1024, [384])])
        g_qk = at("g_qk", A0, [2, T])
        g_z = at("g_z", A0 + 512, [T])
        g_e = at("g_e", A0 + 768, [T])
        g_b = at("g_b", A0 + 1408, [T])
        g_at = at("g_at", A0 + 1664, [3, P])
        g_chunk = at("g_chunk", A0 + 2048, [T])
        walpha = at("walpha", A0 + 2304, [GH * GK])
        gat = at("gat", A0 + 2816, [T])
        g_x = at("g_x", A0 + 4096, [LEVELS, T])
        g_m = at("g_m", A0 + 6144, [LEVELS, P])
        o_strips = [proj2[:, :, c:c + W] for c in (C2["gv"], C2["gv"] + W, C2["dv"], C2["dv"] + W)]
        sig = proj2[:, :, 0:GH * GV]

        def stat(k, n):
            return small[:, k:k + n]

        rs_x, ss_x = stat(0, 2), stat(2, 2)
        ss_c, rs_c = stat(4, 4), stat(8, 4)
        ss_h4, ss_h, rs_h = stat(12, 8), stat(20, 2), stat(22, 2)
        ss_f4, ss_f, rs_f = stat(24, 8), stat(32, 2), stat(34, 2)
        ss_x2, rs_x2, rs_in2 = stat(36, 2), stat(38, 2), stat(40, 2)
        ss_o, rs_o = stat(42, 16), stat(58, 16)
        ss_m4, ss_m, rs_m = stat(74, 8), stat(82, 2), stat(84, 2)
        ss_x3, rs_x3 = stat(94, 2), stat(96, 2)
        ss_g4, ss_g, rs_g = stat(98, 8), stat(106, 2), stat(108, 2)
        mx = [stat(110 + 2 * s, 2) for s in range(2)]
        sm = [stat(114 + 2 * s, 2) for s in range(2)]
        rc = [stat(118 + 2 * s, 2) for s in range(2)]
        lam2, lam = stat(122, 2), stat(124, 1)
        rs_tmp = stat(126, 16)

        acc = [psum(f"acc{j}", [P, TT, W]) for j in range(2)]
        mis = [psum(f"mis{j}", [P, 4, T]) for j in range(2)]
        misf = [x[:, :, :].rearrange("p a b -> p (a b)") for x in mis]
        accf = [x[:, :, :].rearrange("p a b -> p (a b)") for x in acc]

        raw_in = [sem(f"raw_in{j}") for j in range(RING)]
        hi_ready = sem("hi_ready")
        lo_ready = sem("lo_ready")
        chunk_used = sem("chunk_used")
        acc_free = [sem(f"acc_free{j}") for j in range(2)]
        staged = sem("staged")
        turned = sem("turned")
        hi_side = sem("hi_side")
        side = sem("side")
        x_in = sem("x_in")
        rows_in = sem("rows_in")
        tab_in = sem("tab_in")
        ident_ok = sem("ident_ok")
        masks_ok = sem("masks_ok")
        rows_turned = sem("rows_turned")
        vec_ok = sem("vec_ok")
        squares = sem("squares")
        var_ok = sem("var_ok")
        root_ok = sem("root_ok")
        rstd_ok = sem("rstd_ok")
        ang_ok = sem("ang_ok")
        cs_ok = sem("cs_ok")
        act_out = sem("act_out")
        dve_out = sem("dve_out")
        roped = sem("roped")
        head_in = sem("head_in")
        head_turned = sem("head_turned")
        head_qk = sem("head_qk")
        head_scores = sem("head_scores")
        head_masked = sem("head_masked")
        head_max = sem("head_max")
        head_exp = sem("head_exp")
        head_probs = sem("head_probs")
        probs_turned = sem("probs_turned")
        probs_in = sem("probs_in")
        head_y = sem("head_y")
        y_hi = sem("y_hi")
        y_done = sem("y_done")
        krz_ok = sem("krz_ok")
        krt_turned = sem("krt_turned")
        krt_in = sem("krt_in")
        bias_ok = sem("bias_ok")
        lam_in = sem("lam_in")
        lam_sum = sem("lam_sum")
        lam_exp = sem("lam_exp")
        lam_ok = sem("lam_ok")
        ga_turned = sem("ga_turned")
        ga_in = sem("ga_in")
        wa_in = sem("wa_in")
        tables_ok = sem("tables_ok")
        gl_turned = sem("gl_turned")
        gl_qk = sem("gl_qk")
        gl_z = sem("gl_z")
        gl_abs = sem("gl_abs")
        gl_ln = sem("gl_ln")
        gl_dec = sem("gl_dec")
        gl_exp = sem("gl_exp")
        gl_x = sem("gl_x")
        gl_lev = sem("gl_lev")
        gl_read = sem("gl_read")
        gl_at = sem("gl_at")
        gl_o = sem("gl_o")
        gl_sq = sem("gl_sq")
        gl_out = sem("gl_out")
        silu_ok = sem("silu_ok")
        res_in = sem("res_in")
        res_free = sem("res_free")
        h_in = sem("h_in")
        gbc_in = sem("gbc_in")
        x2_ok = sem("x2_ok")
        x3_ok = sem("x3_ok")
        conv_tap = sem("conv_tap")
        conv_ok = sem("conv_ok")
        gelu_ok = sem("gelu_ok")
        prod_ok = sem("prod_ok")
        fin_ok = sem("fin_ok")
        out_done = sem("out_done")
        act_chain = sem("act_chain")
        dve_chain = sem("dve_chain")
        pool_chain = sem("pool_chain")

        w_in, w_in2 = rows_of(a["w_in"]), rows_of(a["w_in_2"])
        w_uq, w_ukv = rows_of(a["w_uq"]), rows_of(a["w_ukv"])
        w_a, w_b, w_out = rows_of(a["w_branch_a"]), rows_of(a["w_branch_b"]), rows_of(a["w_out"])
        w_gate, w_up, w_down = rows_of(a["w_gate"]), rows_of(a["w_up"]), rows_of(a["w_down"])
        w_o2, w_f2, w_fo2 = rows_of(a["w_o_2"]), rows_of(a["w_ffn_in_2"]), rows_of(a["w_ffn_out_2"])

        PH = {}
        order = [
            ("qkv", 6, KD, 0), ("gate0", 4, KD, 0), ("cq", 1, KD, 1), ("ckv", 1, KD, 1), ("uq", 3, 4, 0), ("ukv", 4, 2, 0),
            ("gate1", 4, KD, 0), ("branch", 8, 8, 4), ("out", 4, KD, 4), ("ffn", 2 * FT, KD, FT),
            ("down", 4, KF, 4), ("in2a", 2, KD, 0), ("ga", 1, KD, 0), ("in2b", NB, KD, 4),
            ("o2", 4, KD, 4), ("ffn2", 2 * FT, KD, FT), ("down2", 4, KF, 0)]
        n_chunk = n_tile = 0
        n_item = 4
        for name, tiles, k, items in order:
            PH[name] = (n_chunk, n_tile, n_item, k // CK)
            n_chunk += tiles * k // CK
            n_tile += tiles
            n_item += items

        SQ = dict(x=1, c=2, h=6, f=10, x2=11, m=15, x3=16, g=20)

        def gains(row, n=4):
            return [vec[:, row + q:row + q + 1] for q in range(n)]

        def stages(item):
            return 2 * (item - 4 + 1)

        block = ctx.enter_context(nc.Block())

        @block.sync
        def _(sp):
            for t in range(TT):
                sp.dma_start(xin[:, t, :], a["x"][0, t * P:(t + 1) * P, :]).then_inc(x_in, 16)

            def load(n, c, src):
                slot = (n.start + c) % RING
                if n.low(c) >= RING:
                    sp.wait_ge(lo_ready, n.at(c - RING + 1))
                w = src.shape[2]
                sp.dma_start(raw[:, slot, :, 0:w], src).then_inc(raw_in[slot], 16)

            def tile(n, c0, w, col, k, width=W):
                for c in range(k // CK):
                    load(n, c0 + c, w[:, CK * c:CK * c + CK, ds(col, width)])

            def plain(phase, w, col, k, n_pairs):
                n0 = PH[phase][0]
                per = 2 * k // CK
                for i in pairs(sp, n_pairs):
                    n = Count(n0, i, per)
                    tile(n, 0, w, col + i * (2 * W), k)
                    tile(n, k // CK, w, (col + W) + i * (2 * W), k)

            def couple(phase, w1, w2, col1, col2, k, n_pairs):
                n0 = PH[phase][0]
                per = 2 * k // CK
                for i in pairs(sp, n_pairs):
                    n = Count(n0, i, per)
                    tile(n, 0, w1, col1 + i * W, k)
                    tile(n, k // CK, w2, col2 + i * W, k)

            plain("qkv", w_in, 0, KD, 3)
            plain("gate0", w_in, C_GATE, KD, 2)
            tile(Count(PH["cq"][0]), 0, w_in, C_CQ, KD)
            tile(Count(PH["ckv"][0]), 0, w_in, C_CKV, KD, W_CKV)
            for j in range(3):
                tile(Count(PH["uq"][0]), 2 * j, w_uq, j * W, 4)
            for j in range(4):
                tile(Count(PH["ukv"][0]), j, w_ukv, j * W, 2)
            plain("gate1", w_in, C_GATE + D, KD, 2)
            couple("branch", w_a, w_b, 0, 0, 8, DT)
            plain("out", w_out, 0, KD, 2)
            couple("ffn", w_gate, w_up, 0, 0, KD, FT)
            plain("down", w_down, 0, KF, 2)
            plain("in2a", w_in2, 0, KD, 1)
            tile(Count(PH["ga"][0]), 0, w_in2, C2["ga"], KD, GR)
            for j, col in enumerate(BESIDE):
                tile(Count(PH["in2b"][0]), j * PH["in2b"][3], w_in2, col, KD)
            plain("o2", w_o2, 0, KD, 2)
            couple("ffn2", w_f2, w_f2, 0, DFF, KD, FT)
            plain("down2", w_fo2, 0, KF, 2)
            for j in range(DT):
                sp.wait_ge(fin_ok, 2 * (j + 1))
                sp.dma_start(out[0].rearrange("(t p) n -> p t n", p=P)[:, :, j * W:(j + 1) * W],
                             frow[:, :, j * W:(j + 1) * W]).then_inc(out_done, 16)
            sp.wait_ge(out_done, 16 * DT)

        @block.tensor
        def _(pe):
            def turn(item, src, pair, blocks=4, wait=True):
                if wait:
                    pe.wait_ge(staged, stages(item))
                for kb in range(blocks):
                    for t in range(TT):
                        last = nc.tensor.transpose(mis[pair][:, kb, t * P:(t + 1) * P],
                                                   src[:, t, kb * P:(kb + 1) * P], ident[:, :])
                last.then_inc(turned, 1)

            def tile(n, c0, k, x, tile_no, par, width=W, k0=0, sides=None, hook=None, beside=None):
                for c in range(k // CK):
                    if hook and c in hook:
                        hook[c]()
                    if beside is not None:
                        beside(c)
                    if c == 0 and tile_no.low(0) >= 2:
                        pe.wait_ge(acc_free[par], tile_no.at(0))
                    if sides is not None and c % 2 == 0:
                        pe.wait_ge(side, sides + c // 2 + 1)
                    slot = (n.start + c0 + c) % RING
                    pe.wait_ge(lo_ready, n.at(c0 + c + 1))
                    for kk in range(CK):
                        kb = c * CK + kk
                        for t in range(TT):
                            xh = x[0][:, k0 + kb, t * P:(t + 1) * P]
                            xl = x[1][:, k0 + kb, t * P:(t + 1) * P]
                            o = acc[par][:, t, 0:width]
                            wh, wl = hi[:, slot, kk, 0:width], lo[:, slot, kk, 0:width]
                            nc.tensor.matmul(o, xh, wh, start=kb == 0, stop=False)
                            nc.tensor.matmul(o, xh, wl, start=False, stop=False)
                            last = nc.tensor.matmul(o, xl, wh, start=False, stop=kb == k - 1)
                    last.then_inc(chunk_used, 1)

            def tiles_of(tile0, i=0, per=0):
                return Count(tile0 - tile0 % 2, i, per)

            def plain(phase, k, x, n_pairs, sides=None, item=None):
                n0, t0, _, per = PH[phase]
                for i in pairs(pe, n_pairs):
                    n = Count(n0, i, 2 * per)
                    for j in range(2):
                        hook = None
                        if item is not None:
                            hook = {4: lambda j=j: turn(i * 2 + (item + j), stg, 0)}
                        tile(n, j * per, k, x, tiles_of(t0 + j, i, 2), (t0 + j) % 2,
                             sides=sides if j == 0 else None, hook=hook)

            def couple(phase, k, xs, n_pairs, hooks, sides=None, k0=(0, 0)):
                n0, t0, _, per = PH[phase]
                with pe.Fori(0, n_pairs) as i:
                    n = Count(n0, i, 2 * per)
                    for j in range(2):
                        tile(n, j * per, k, xs, tiles_of(t0 + j, i, 2), (t0 + j) % 2, k0=k0[j],
                             sides=sides if j == 0 else None,
                             hook={4: lambda: hooks(i)} if hooks and j == 0 else None)

            def attention_steps(g, first, head0, b, q, k, v, rope, diff, values_in=None):
                n = due(g, first, PERIOD, 0, GH)
                if n is not None:
                    if head0 + 2 * (n - 1) > 0 and n != 1:
                        pe.wait_ge(y_done, head0 + 2 * max(n - 1, 0))
                    for s in range(2):
                        for x, src in enumerate((q, k)):
                            for t in range(TT):
                                last = nc.tensor.transpose(misf[s][:, x * T + t * P:x * T + (t + 1) * P],
                                                           src(n, s, t), ident[:, :])
                        last.then_inc(head_turned, 1)
                n = due(g, first, PERIOD, 2, GH)
                if n is not None:
                    if n:
                        pe.wait_ge(probs_in, head0 + 2 * n)
                    for s in range(2):
                        pe.wait_ge(head_qk, head0 + 2 * n + s + 1)
                        for t in range(TT):
                            o = misf[s][:, W + t * P:W + t * P + (t + 1) * P]
                            last = nc.tensor.matmul(o, b["qk"][s][:, 0, t * P:(t + 1) * P],
                                                    b["qk"][s][:, 1, 0:(t + 1) * P], start=True, stop=not rope)
                            if rope:
                                last = nc.tensor.matmul(o, qrt[:, n, t * P:(t + 1) * P],
                                                        krt[:, s, 0:(t + 1) * P], start=False, stop=True)
                        last.then_inc(head_scores, 1)
                n = due(g, first, PERIOD, PERIOD + 2, GH)
                if n is not None:
                    if values_in:
                        values_in(n)
                    for s in range(1 if diff else 2):
                        pe.wait_ge(probs_in, head0 + 2 * n + (2 if diff else s + 1))
                        if diff:
                            o0, o1 = misf[0][:, 0:GV], misf[0][:, GV:2 * GV]
                            vv = [v(n, s, t) for t in range(TT)]
                            nc.tensor.matmul(o0, b["pt"][0][:, 0:P], vv[0], start=True, stop=True)
                            nc.tensor.matmul(o1, b["pt"][0][:, P:T], vv[0], start=True, stop=False)
                            nc.tensor.matmul(o1, b["pt"][0][:, T:T + P], vv[1], start=False, stop=True)\
                                .then_inc(head_y, 2)
                        else:
                            nc.tensor.matmul(misf[s][:, 0:T], v(n, s, 0), b["pt"][s][:, 0:T],
                                             start=True, stop=False)
                            nc.tensor.matmul(misf[s][:, P:T], v(n, s, 1), b["pt"][s][:, T:T + P],
                                             start=False, stop=True).then_inc(head_y, 1)
                n = due(g, first, PERIOD, 6, GH)
                if n is not None:
                    for s in range(1 if diff else 2):
                        pe.wait_ge(head_probs, head0 + 2 * n + (2 if diff else s + 1))
                        for x in range(3):
                            last = nc.tensor.transpose(misf[s][:, W + x * P:W + (x + 1) * P],
                                                       b["p"][s][:, x * P:(x + 1) * P], ident[:, :])
                        last.then_inc(probs_turned, 2 if diff else 1)

            def moba_steps(g):
                if g == MOBA_FIRST:
                    pe.wait_ge(roped, 1)
                attention_steps(g, MOBA_FIRST, 0, ab,
                                lambda n, s, t: qkv[:, t, (2 * n + s) * MD:(2 * n + s + 1) * MD],
                                lambda n, s, t: qkv[:, t, (MH + 2 * n + s) * MD:(MH + 2 * n + s + 1) * MD],
                                lambda n, s, t: qkv[:, t, (2 * MH + 2 * n + s) * MD:(2 * MH + 2 * n + s + 1) * MD],
                                False, False)

            def mla_steps(g):
                def keys(n, s):
                    return (2 * n + s) * (NOPE + MD)

                attention_steps(g, MLA_FIRST, MH, ab,
                                lambda n, s, t: qm[:, t, (2 * n + s) * (NOPE + ROPE):(2 * n + s) * (NOPE + ROPE) + NOPE],
                                lambda n, s, t: kvm[:, t, keys(n, s):keys(n, s) + NOPE],
                                lambda n, s, t: kvm[:, t, keys(n, s) + NOPE:keys(n, s) + NOPE + MD],
                                True, False)

            pe.wait_ge(ident_ok, 2)
            pe.wait_ge(rows_in, 16 * 14)
            for j, r in enumerate((V_ROWS, 2 * KF, 2 * KF)):
                last = nc.tensor.transpose(misf[1][:, j * P:j * P + r], rows[0:r, j, :], ident[0:r, 0:r])
            last.then_inc(rows_turned, 1)
            pe.wait_ge(x_in, 32)
            for j in range(4):
                if j == 1:
                    pe.wait_ge(vec_ok, 1)
                if j >= 2:
                    pe.wait_ge(side, j - 1)
                turn(j, xin[:, :, j * W:(j + 1) * W], j % 2, wait=False)
            plain("qkv", KD, xa, 3, sides=0)
            n0, t0, _, per = PH["gate0"]
            for j in range(4):
                tile(Count(n0), j * per, KD, xa, tiles_of(t0 + j), (t0 + j) % 2,
                     beside=lambda c, j=j: moba_steps(j * per + c))
            n0, t0, i0, per = PH["cq"]
            tile(Count(n0), 0, KD, xa, tiles_of(t0), t0 % 2, beside=lambda c: moba_steps(4 * per + c))
            n0, t0, _, per = PH["ckv"]
            tile(Count(n0), 0, KD, xa, tiles_of(t0), t0 % 2, width=W_CKV,
                 hook={4: lambda: turn(i0, stg, 0)})
            n0, t0, _, per = PH["uq"]
            for j in range(3):
                if j == 1:
                    turn(i0 + 1, stg, 0, blocks=2)
                if j == 0:
                    pe.wait_ge(side, i0 + 1)
                tile(Count(n0), 2 * j, 4, ct, tiles_of(t0 + j), (t0 + j) % 2)
            n0, t0, _, per = PH["ukv"]
            pe.wait_ge(side, i0 + 2)
            for j in range(4):
                tile(Count(n0), j, 2, ct, tiles_of(t0 + j), (t0 + j) % 2, k0=4)

            def mla_rope():
                pe.wait_ge(roped, 2)
                for hp in range(MH // 2):
                    for t in range(TT):
                        nc.tensor.transpose(mis[0][:, hp, t * P:(t + 1) * P], qr[:, t, hp * P:(hp + 1) * P], ident[:, :])
                for s in range(2):
                    for t in range(TT):
                        last = nc.tensor.transpose(mis[1][:, s, t * P:(t + 1) * P], krz[:, t, s, :], ident[:, :])
                last.then_inc(krt_turned, 1)
                pe.wait_ge(krt_in, 1)

            n0, t0, _, per = PH["gate1"]
            for j in range(4):
                def beside(c, j=j):
                    if j == 0 and c == MLA_FIRST - 1:
                        mla_rope()
                    mla_steps(j * per + c)

                tile(Count(n0), j * per, KD, xa, tiles_of(t0 + j), (t0 + j) % 2, beside=beside)
            i0 = PH["branch"][2]
            n0, t0, _, per = PH["branch"]
            for i in pairs(pe, DT):
                n = Count(n0, i, 2 * per)
                if isinstance(i, int):
                    pe.wait_ge(y_done, MH)
                    tile(n, 0, 8, xb, tiles_of(t0), t0 % 2, beside=lambda c: mla_steps(4 * KD // CK + c))
                    pe.wait_ge(y_done, 2 * MH)
                else:
                    tile(n, 0, 8, xb, tiles_of(t0, i, 2), t0 % 2)
                tile(n, per, 8, xb, tiles_of(t0 + 1, i, 2), (t0 + 1) % 2, k0=8,
                     hook=None if isinstance(i, int) else {0: lambda: turn(i + (i0 - 1), stg, 0)})
            i1 = PH["out"][2]
            n0, t0, _, per = PH["out"]
            tile(Count(n0), 0, KD, xa, tiles_of(t0), t0 % 2, sides=i0,
                 hook={4: lambda: turn(i1 - 1, stg, 0)})
            for j in range(1, DT):
                tile(Count(n0), j * per, KD, xa, tiles_of(t0 + j), (t0 + j) % 2,
                     hook={4: lambda j=j: turn(i1 + j - 1, stg, 0)})
            i2 = PH["ffn"][2]
            couple("ffn", KD, xb, FT, lambda i: turn(i + (i2 - 1), stg, 0), sides=i1)
            i3 = PH["down"][2]
            plain("down", KF, ff, 2, sides=i2, item=i3 - 1)
            i4 = PH["in2b"][2]
            n0, t0, _, per = PH["in2a"]
            tile(Count(n0), 0, KD, xb, tiles_of(t0), t0 % 2, sides=i3,
                 hook={4: lambda: turn(i4 - 1, stg, 0)})
            tile(Count(n0), per, KD, xb, tiles_of(t0 + 1), (t0 + 1) % 2)
            n0, t1, _, per = PH["ga"]
            tile(Count(n0), 0, KD, xb, tiles_of(t1), t1 % 2, width=GR)
            n0, t0, _, per = PH["in2b"]

            def evicted(tile_no):
                pe.wait_ge(acc_free[tile_no % 2], 2 * (tile_no // 2 + 1))

            def gla_steps(g):
                if g == 4:
                    evicted(t1 - 1)
                    evicted(t1)
                    for t in range(TT):
                        last = nc.tensor.transpose(misf[1][0:GR, t * P:(t + 1) * P], kr[:, t, 0:GR], ident[:, :])
                    last.then_inc(ga_turned, 1)
                h = due(g, GLA_FIRST, GLA_PERIOD, 0, GH)
                if h is not None:
                    if h == 0:
                        pe.wait_ge(side, i4)
                        pe.wait_ge(ga_in, 1)
                        pe.wait_ge(wa_in, 16)
                    else:
                        pe.wait_ge(gl_qk, h)
                        pe.wait_ge(gl_read, h)
                    for x, col in enumerate((C2["gq"], C2["gk"])):
                        for t in range(TT):
                            nc.tensor.transpose(misf[0][:, x * T + t * P:x * T + (t + 1) * P],
                                                proj2[:, t, col + h * GK:col + (h + 1) * GK], ident[:, :])
                    nc.tensor.matmul(misf[0][:, W:W + T], walpha[0:GR, h * GK:(h + 1) * GK], gat[0:GR, :],
                                     start=True, stop=True).then_inc(gl_turned, 1)

                def levels(t):
                    tt = slice(t * P, (t + 1) * P)
                    for lv in range(LEVELS - 1):
                        nc.tensor.matmul(misf[1][:, lv * P:(lv + 1) * P], g_x[:, lv, tt], g_x[:, lv, tt],
                                         start=True, stop=True)
                    return nc.tensor.matmul(misf[1][:, (LEVELS - 1) * P:], g_qk[:, 1, tt], g_qk[:, 0, tt],
                                            start=True, stop=True)

                h = due(g, GLA_FIRST, GLA_PERIOD, 6, GH)
                if h is not None:
                    pe.wait_ge(gl_x, h + 1)
                    if h:
                        pe.wait_ge(gl_out, h)
                    nc.tensor.matmul(misf[0][:, W + T:W + T + P], g_x[:, LEVELS - 1, 0:P],
                                     g_x[:, LEVELS - 1, P:T], start=True, stop=True)
                    levels(0).then_inc(gl_lev, 1)
                h = due(g, GLA_FIRST, GLA_PERIOD, 8, GH)
                if h is not None:
                    pe.wait_ge(gl_read, h + 1)
                    levels(1).then_inc(gl_lev, 1)
                h = due(g, GLA_FIRST, GLA_PERIOD, 11, GH)
                if h is not None:
                    evicted(t0 + h // 2)
                    pe.wait_ge(gl_at, h + 1)
                    v = [proj2[:, t, C2["gv"] + h * GV:C2["gv"] + (h + 1) * GV] for t in range(TT)]
                    nc.tensor.matmul(misf[1][:, 0:GV], g_at[:, 0, :], v[0], start=True, stop=True)
                    nc.tensor.matmul(misf[1][:, GV:2 * GV], g_at[:, 1, :], v[1], start=True, stop=False)
                    nc.tensor.matmul(misf[1][:, GV:2 * GV], g_at[:, 2, :], v[0], start=False, stop=True)\
                        .then_inc(gl_o, 1)

            dtile = [(t0 + 3, t0 + 4), (t0 + 6, t0 + 7)]

            def diff_steps(g):
                n = due(g, DIFF_FIRST, PERIOD, 0, GH)
                if n is not None:
                    if n == 0:
                        pe.wait_ge(gl_out, GH)
                    evicted(dtile[n // 2][0] - 1)
                    evicted(dtile[n // 2][0])
                attention_steps(g, DIFF_FIRST, 2 * MH, db,
                                lambda n, s, t: proj2[:, t, C2["dq"] + (2 * n + s) * GK:C2["dq"] + (2 * n + s + 1) * GK],
                                lambda n, s, t: proj2[:, t, C2["dk"] + (2 * n + s) * GK:C2["dk"] + (2 * n + s + 1) * GK],
                                lambda n, s, t: proj2[:, t, C2["dv"] + n * GV:C2["dv"] + (n + 1) * GV],
                                False, True, lambda n: evicted(dtile[n // 2][1]))

            for j in range(NB):
                def beside(c, j=j):
                    gla_steps(j * per + c)
                    diff_steps(j * per + c)

                tile(Count(n0), j * per, KD, xb, tiles_of(t0 + j), (t0 + j) % 2, beside=beside)
            diff_steps(NB * per)

            i4 = PH["in2b"][2]
            for j in range(4):
                if j >= 2:
                    pe.wait_ge(side, i4 + j - 1)
                turn(i4 + j, o_strips[j], j % 2)
            n0, t0, _, per = PH["o2"]
            with pe.Fori(0, 2) as i:
                n = Count(n0, i, 2 * per)
                for j in range(2):
                    tile(n, j * per, KD, xa, tiles_of(t0 + j, i, 2), (t0 + j) % 2, sides=i4 if j == 0 else None)
            i5 = PH["o2"][2]
            for j in range(4):
                if j >= 2:
                    pe.wait_ge(side, i5 + j - 1)
                turn(i5 + j, hres[:, :, j * W:(j + 1) * W], j % 2)
            i6 = PH["ffn2"][2]

            def turn_both(k, a_read):
                pe.wait_ge(staged, k)
                pe.wait_ge(acc_free[PH["ffn2"][1] % 2], a_read)
                for pair, src in ((0, stg), (1, stg2)):
                    for kb in range(4):
                        for t in range(TT):
                            last = nc.tensor.transpose(mis[pair][:, kb, t * P:(t + 1) * P],
                                                       src[:, t, kb * P:(kb + 1) * P], ident[:, :])
                last.then_inc(turned, 1)

            n0, t0, _, per = PH["ffn2"]
            tile(Count(n0), 0, KD, xb, tiles_of(t0), t0 % 2, sides=i5)
            tile(Count(n0), per, KD, xb, tiles_of(t0 + 1), (t0 + 1) % 2)
            with pe.Fori(1, FT) as i:
                n = Count(n0, i, 2 * per)
                tile(n, 0, KD, xb, tiles_of(t0, i, 2), t0 % 2,
                     hook={4: lambda: turn_both(i * 2 + (stages(i6) - 2), i * 2 + (t0 - t0 % 2))})
                tile(n, per, KD, xb, tiles_of(t0 + 1, i, 2), (t0 + 1) % 2)
            even = t0 - t0 % 2 + 2 * FT
            n0, t0, _, per = PH["down2"]
            tile(Count(n0), 0, KF, ff, tiles_of(t0), t0 % 2, sides=i6,
                 hook={4: lambda: turn_both(stages(i6 + FT - 1), even)})
            tile(Count(n0), per, KF, ff, tiles_of(t0 + 1), (t0 + 1) % 2)
            for j in range(2, 4):
                tile(Count(n0), j * per, KF, ff, tiles_of(t0 + j), (t0 + j) % 2)

        @block.scalar
        def _(act):
            chain = Chain(act, act_chain)

            for row, name, n in ((V_ATT, "attn_norm", 16), (V_Q, "q_norm", 4), (V_KV, "kv_norm", 2),
                                 (V_FFN, "ffn_norm", 16), (V_FIN, "final_norm", 16),
                                 (V_PRE2, "attn_pre_norm_2", 16), (V_PRE3, "ffn_pre_norm_2", 16),
                                 (V_BAL, "b_alpha_2", 4), (V_GLA, "gla_norm_2", 2), (V_DIF, "diff_norm_2", 2)):
                v = a[name]
                v = v.rearrange("l (k p) -> (l k) p", p=P) if len(v.shape) == 2 else v.rearrange("(k p) -> k p", p=P)
                act.dma_start(rows[row:row + n, 0, :], v).then_inc(rows_in, 16)
            cw = a["conv_w_2"][0].rearrange("w (k p) -> w k p", p=P)
            act.dma_start(rows[0:KF, 1, :], cw[0]).then_inc(rows_in, 16)
            act.dma_start(rows[KF:2 * KF, 1, :], cw[1]).then_inc(rows_in, 16)
            act.dma_start(rows[0:KF, 2, :], cw[2]).then_inc(rows_in, 16)
            act.dma_start(rows[KF:2 * KF, 2, :], a["conv_b_2"].rearrange("l (k p) -> (l k) p", p=P))\
                .then_inc(rows_in, 16)
            for t in range(TT):
                act.dma_start(posi[:, t:t + 1], a["positions"][0:1, t * P:(t + 1) * P].rearrange("b p -> p b"))\
                    .then_inc(tab_in, 16)
            act.dma_start(invf[:, :], a["inv_freq"].partition_broadcast(P)).then_inc(tab_in, 16)

            def split(n, c, width=W):
                slot = (n.start + c) % RING
                act.wait_ge(raw_in[slot], landed(n, c))
                if n.low(c) >= RING:
                    act.wait_ge(chunk_used, n.at(c - RING + 1))
                nc.scalar.activation(hi[:, slot, :, 0:width], raw[:, slot, :, 0:width], ACT.Copy)\
                    .then_inc(hi_ready, 1)

            def root(k, dst):
                act.wait_ge(var_ok, k + 1)
                nc.scalar.activation(dst, dst, ACT.Sqrt).then_inc(root_ok, 1)

            def side_hi(item, dst, kb, gain=None, pair=0, blocks=4):
                act.wait_ge(turned, item + 1)
                if gain is None:
                    for half in range(2):
                        last = nc.scalar.activation(dst[0][:, ds(kb + 2 * half, 2), :],
                                                    mis[pair][:, 2 * half:2 * half + 2, :], ACT.Copy)
                else:
                    for j in range(blocks):
                        last = nc.scalar.activation(dst[0][:, ds(kb + j, 1), :], mis[pair][:, j:j + 1, :],
                                                    ACT.Copy, scale=gain[j])
                last.then_inc(hi_side, 1)

            def results(n, c):
                act.wait_ge(chunk_used, n.at(c + 1))

            def ev(dst, par, scale, width=W):
                nc.scalar.activation(dst, acc[par][:, 0, 0:width], ACT.Copy, scale=scale)\
                    .then_inc(acc_free[par], 1)

            def square(src, dst, total):
                return nc.scalar.activation(dst, src, ACT.Square, accum_out=total)

            def keep(item, ss4, j):
                act.wait_ge(staged, stages(item) - 1)
                for t in range(TT):
                    last = square(stg[:, t, :], stg2[:, t, :], ss4[:, 4 * t + j:4 * t + j + 1])
                last.then_inc(squares, 1)
                nc.scalar.activation(hres[:, :, j * W:(j + 1) * W], stg[:, :, :], ACT.Copy).then_inc(staged, 1)

            act.wait_ge(vec_ok, 1)
            for j in range(4):
                side_hi(j, xa, 4 * j, gains(V_ATT + 4 * j), j % 2)

            def first_norm():
                act.wait_ge(x_in, 32)
                for t in range(TT):
                    last = square(xin[:, t, :], junk[:, t, :], ss_x[:, t:t + 1])
                last.then_inc(squares, 1)
                root(0, rs_x)
                act.wait_ge(ang_ok, 1)
                for t in range(TT):
                    last = nc.scalar.activation(cs[:, t, :, :], trn[:, :, t, :], ACT.Sin)
                last.then_inc(cs_ok, 1)
                act.wait_ge(rstd_ok, 1)

            n0, t0, _, per = PH["qkv"]
            for i in pairs(act, 3):
                n = Count(n0, i, 2 * per)
                for j in range(2):
                    for c in range(per):
                        if c == 6 and j == 0 and isinstance(i, int):
                            first_norm()
                        if c == LEAD and (j == 1 or not isinstance(i, int)):
                            results(n, j * per - 1)
                            ev(qkv[:, 0, ds(i * (2 * W) + (j - 1) * W, W)], (t0 + j - 1) % 2, rs_x[:, 0:1])
                        split(n, j * per + c)
            def attention_steps(g, first, head0, b, out, diff):
                n = due(g, first, PERIOD, 2, GH)
                if n is not None:
                    for s in range(2):
                        act.wait_ge(head_turned, head0 + 2 * n + s + 1)
                        if n:
                            act.wait_ge(head_scores, head0 + 2 * n + s - 1)
                        nc.scalar.activation(b["qk"][s][:, :, :].rearrange("p a b -> p (a b)"),
                                             misf[s][:, 0:W], ACT.Copy).then_inc(head_qk, 1)
                n = due(g, first, PERIOD, 5, GH)
                if n is not None:
                    for s in range(2):
                        act.wait_ge(head_max, head0 + 2 * n + s + 1)
                        p = b["p"][s]
                        nc.scalar.activation(p[:, 0:P], p[:, 0:P], ACT.Exp, bias=mx[s][:, 0:1],
                                             accum_out=sm[s][:, 0:1])
                        nc.scalar.activation(p[:, P:], p[:, P:], ACT.Exp, bias=mx[s][:, 1:2],
                                             accum_out=sm[s][:, 1:2]).then_inc(head_exp, 1)
                n = due(g, first, PERIOD, 8, GH)
                if n is not None:
                    for s in range(1 if diff else 2):
                        act.wait_ge(probs_turned, head0 + 2 * n + (2 if diff else s + 1))
                        if n:
                            act.wait_ge(head_y, head0 + 2 * n + (0 if diff else s - 1))
                        nc.scalar.activation(b["pt"][s][:, :], misf[s][:, W:W + 384], ACT.Copy)\
                            .then_inc(probs_in, 2 if diff else 1)
                n = due(g, first, PERIOD, 11, GH)
                if n is not None:
                    for s in range(1 if diff else 2):
                        act.wait_ge(head_y, head0 + 2 * n + (2 if diff else s + 1))
                        out(n, s)

            def head_out(n, s, head0=MH):
                nc.scalar.activation(xb[0][:, head0 + 2 * n + s, :], misf[s][:, 0:T], ACT.Copy).then_inc(y_hi, 1)

            def moba_out(n, s):
                head_out(n, s, 0)

            def sigmoid(par, col):
                for t in range(TT):
                    nc.scalar.activation(gates[:, t, col:col + W], acc[par][:, t, :], ACT.Sigmoid,
                                         scale=rs_x[:, t:t + 1]).then_inc(acc_free[par], 1)

            n0, t0, _, per = PH["gate0"]
            n = Count(n0)
            for c in range(5 * per):
                if c == LEAD:
                    results(n, -1)
                    ev(qkv[:, 0, 5 * W:], (t0 - 1) % 2, rs_x[:, 0:1])
                if c > per and c % per == LEAD:
                    results(n, c - LEAD - 1)
                    sigmoid((t0 + c // per - 1) % 2, (c // per - 1) * W)
                attention_steps(c, MOBA_FIRST, 0, ab, moba_out, False)
                split(n, c)
            n0, t0, i0, per = PH["cq"]
            n = Count(PH["ckv"][0])
            for c in range(per):
                if c == LEAD:
                    results(n, -1)
                    ev(stg[:, 0, :], t0 % 2, rs_x[:, 0:1])
                    act.wait_ge(acc_free[t0 % 2], 2 * (t0 // 2 + 1))
                    for t in range(TT):
                        square(stg[:, t, :], stg2[:, t, :], ss_c[:, t:t + 1]).then_inc(staged, 1)
                split(n, c, W_CKV)
            side_hi(i0, ct, 0, gains(V_Q))
            n, tu = Count(PH["uq"][0]), PH["uq"][1]
            for c in range(6):
                if c == LEAD:
                    results(n, -1)
                    ev(stg[:, 0, 0:W_CKV], (tu - 1) % 2, rs_x[:, 0:1], W_CKV)
                    act.wait_ge(acc_free[(tu - 1) % 2], 2 * ((tu - 1) // 2 + 1))
                    for t in range(TT):
                        square(stg[:, t, 0:KVR], stg2[:, t, 0:KVR], ss_c[:, 2 + t:3 + t]).then_inc(staged, 1)
                    nc.scalar.activation(kr[:, :, :], stg[:, :, KVR:W_CKV], ACT.Copy).then_inc(squares, 1)
                    root(1, rs_c)
                    side_hi(i0 + 1, ct, 4, gains(V_KV, 2), blocks=2)
                    act.wait_ge(rstd_ok, 2)
                    results(n, 1)
                    ev(qm[:, 0, 0:W], tu % 2, rs_c[:, 0:1])
                split(n, c)
            n, tk = Count(PH["ukv"][0]), PH["ukv"][1]
            split(n, 0)
            results(n, -3)
            ev(qm[:, 0, W:2 * W], (tu + 1) % 2, rs_c[:, 0:1])
            split(n, 1)
            results(n, -1)
            ev(qm[:, 0, 2 * W:3 * W], (tu + 2) % 2, rs_c[:, 0:1])
            for j in range(2):
                split(n, j + 2)
                results(n, j)
                ev(kvm[:, 0, j * W:(j + 1) * W], (tk + j) % 2, rs_c[:, 2:3])
            n0, t0, _, per = PH["gate1"]
            n = Count(n0)
            for c in range(4 * per):
                if c < 2:
                    results(Count(PH["ukv"][0]), c + 2)
                    ev(kvm[:, 0, (c + 2) * W:(c + 3) * W], (tk + c) % 2, rs_c[:, 2:3])
                if c > per and c % per == LEAD:
                    results(n, c - LEAD - 1)
                    sigmoid((t0 + c // per - 1) % 2, D + (c // per - 1) * W)
                if c == MLA_FIRST:
                    act.wait_ge(krt_turned, 1)
                    nc.scalar.activation(qrt[:, :, :], mis[0][:, :, :], ACT.Copy)
                    nc.scalar.activation(krt[:, :, :], mis[1][:, 0:2, :], ACT.Copy).then_inc(krt_in, 1)
                attention_steps(c, MLA_FIRST, MH, ab, head_out, False)
                split(n, c)
            n0, t0, i0, per = PH["branch"]
            for i in pairs(act, DT):
                n = Count(n0, i, 2 * per)
                first = isinstance(i, int)
                for c in range(2 * per):
                    if first and c == LEAD:
                        results(n, -1)
                        sigmoid((t0 - 1) % 2, 7 * W)
                    if first:
                        attention_steps(4 * KD // CK + c, MLA_FIRST, MH, ab, head_out, False)
                    if not first and c == 7:
                        side_hi(i + (i0 - 1), xa, i * 4 - 4)
                    split(n, c)
            i1 = PH["out"][2]
            n0, t0, _, per = PH["out"]
            for j in range(DT):
                for c in range(per):
                    if c == LEAD and j > 0:
                        keep(i1 + j - 1, ss_h4, j - 1)
                    if c == 7 and j == 0:
                        side_hi(i1 - 1, xa, 4 * (DT - 1))
                    if c == 7 and j > 0:
                        side_hi(i1 + j - 1, xb, 4 * (j - 1), gains(V_FFN + 4 * (j - 1)))
                    split(Count(n0), j * per + c)
            n0, t0, i2, per = PH["ffn"]
            for i in pairs(act, FT):
                n = Count(n0, i, 2 * per)
                first = isinstance(i, int)
                for c in range(2 * per):
                    if c == LEAD and first:
                        keep(i2 - 1, ss_h4, DT - 1)
                        root(2, rs_h)
                    if c == 7 and first:
                        side_hi(i2 - 1, xb, 4 * (DT - 1), gains(V_FFN + 12))
                        act.wait_ge(rstd_ok, 3)
                    if c == 7 and not first:
                        side_hi(i + (i2 - 1), ff, i * 4 - 4)
                    if c == per + LEAD:
                        results(n, per - 1)
                        for t in range(TT):
                            nc.scalar.activation(stg2[:, t, :], acc[t0 % 2][:, t, :], ACT.Silu,
                                                 scale=rs_h[:, t:t + 1]).then_inc(acc_free[t0 % 2], 1)
                    split(n, c)
            n0, t0, i3, per = PH["down"]
            for j in range(DT):
                for c in range(per):
                    if c == LEAD and j > 0:
                        keep(i3 + j - 1, ss_f4, j - 1)
                    if c == 7 and j == 0:
                        side_hi(i3 - 1, ff, 4 * (FT - 1))
                    if c == 7 and j > 0:
                        side_hi(i3 + j - 1, xb, 4 * (j - 1), [gfin[:, 4 * j - 4 + q:4 * j - 3 + q] for q in range(4)])
                    split(Count(n0), j * per + c)
            n0, t0, _, per = PH["in2a"]
            n = Count(n0)
            for c in range(2 * per):
                if c == LEAD:
                    keep(i3 + DT - 1, ss_f4, DT - 1)
                    root(3, rs_f)
                if c == 7:
                    side_hi(i3 + DT - 1, xb, 12, [gfin[:, q:q + 1] for q in range(12, 16)])
                if c == per + 1:
                    act.wait_ge(x2_ok, 1)
                    for t in range(TT):
                        last = square(hres[:, t, :], sqx2[:, t, :], ss_x2[:, t:t + 1])
                    last.then_inc(squares, 1)
                    root(4, rs_x2)
                    act.wait_ge(rstd_ok, 5)
                if c == per + LEAD:
                    results(n, per - 1)
                    ev(proj2[:, 0, 0:W], t0 % 2, rs_in2[:, 0:1])
                split(n, c)
            n, t1 = Count(PH["ga"][0]), PH["ga"][1]
            for c in range(per):
                if c == LEAD:
                    results(n, -1)
                    ev(proj2[:, 0, W:2 * W], (t1 - 1) % 2, rs_in2[:, 0:1])
                split(n, c, GR)
            n0, t0, i4, per = PH["in2b"]

            def gla_steps(g):
                if g == 6:
                    act.wait_ge(ga_turned, 1)
                    nc.scalar.activation(gat[0:GR, :], misf[1][0:GR, 0:T], ACT.Copy).then_inc(ga_in, 1)
                h = due(g, GLA_FIRST, GLA_PERIOD, 13, GH)
                if h is not None:
                    act.wait_ge(gl_o, h + 1)
                    for t in range(TT):
                        last = square(misf[1][:, t * GV:(t + 1) * GV], sq[:, t, :], ss_o[:, 4 * t + h:4 * t + h + 1])
                    last.then_inc(gl_sq, 1)
                h = due(g, GLA_FIRST, GLA_PERIOD, 2, GH)
                if h is not None:
                    act.wait_ge(gl_turned, h + 1)
                    if h:
                        act.wait_ge(gl_lev, 2 * h)
                    nc.scalar.activation(g_qk[:, :, :].rearrange("p a b -> p (a b)"), misf[0][:, 0:W], ACT.Copy)\
                        .then_inc(gl_qk, 1)
                h = due(g, GLA_FIRST, GLA_PERIOD, 3, GH)
                if h is not None:
                    act.wait_ge(gl_z, h + 1)
                    chain.step(nc.scalar.activation(g_e[:, :], g_z[:, :], ACT.Abs))
                    chain.step(nc.scalar.activation(g_e[:, :], g_e[:, :], ACT.Exp, scale=-1.0))
                    nc.scalar.activation(g_e[:, :], g_e[:, :], ACT.Ln, bias=1.0).then_inc(gl_ln, 1)
                h = due(g, GLA_FIRST, GLA_PERIOD, 5, GH)
                if h is not None:
                    act.wait_ge(gl_dec, h + 1)
                    gx = g_x[:, :, :].rearrange("p a b -> p (a b)")
                    chain.step(nc.scalar.activation(gx, gx, ACT.Abs))
                    nc.scalar.activation(gx, gx, ACT.Exp, scale=-1.0 / 16.0).then_inc(gl_exp, 1)

            def diff_out(n, s):
                for t in range(TT):
                    last = square(misf[0][:, t * GV:(t + 1) * GV], sq[:, t, :], ss_o[:, 8 + 4 * t + n:9 + 4 * t + n])
                last.then_inc(y_hi, 2)

            def silu(par, col):
                for t in range(TT):
                    nc.scalar.activation(sig[:, t, col:col + W], acc[par][:, t, :], ACT.Silu,
                                         scale=rs_in2[:, t:t + 1]).then_inc(acc_free[par], 1)

            for j in range(NB):
                for c in range(per):
                    if c == LEAD:
                        results(Count(n0), j * per - 1)
                        if j == 0:
                            ev(kr[:, 0, 0:GR], t1 % 2, rs_in2[:, 0:1], GR)
                        elif BESIDE[j - 1] == C2["gg"]:
                            silu((t0 + j - 1) % 2, 0)
                        else:
                            ev(proj2[:, 0, BESIDE[j - 1]:BESIDE[j - 1] + W], (t0 + j - 1) % 2, rs_in2[:, 0:1])
                    if j == 4 and c == 0:
                        act.wait_ge(lam_sum, 1)
                        nc.scalar.activation(lam2, lam2, ACT.Exp).then_inc(lam_exp, 1)
                    gla_steps(j * per + c)
                    attention_steps(j * per + c, DIFF_FIRST, 2 * MH, db, diff_out, True)
                    split(Count(n0), j * per + c)
            attention_steps(NB * per, DIFF_FIRST, 2 * MH, db, diff_out, True)
            results(Count(n0), NB * per - 1)
            silu((t0 + NB - 1) % 2, W)
            root(5, rs_o)
            for j in range(4):
                g0 = V_GLA if j < 2 else V_DIF
                side_hi(i4 + j, xa, 4 * j, gains(g0, 2) * 2, j % 2)

            n0, t0, i5, per = PH["o2"]

            def result_squares(par, ss4, j):
                for t in range(TT):
                    last = square(acc[par][:, t, :], stg2[:, t, :], ss4[:, 4 * t + j:4 * t + j + 1])
                    last.then_inc(squares if t == 0 else acc_free[par], 1)

            for j in range(DT):
                for c in range(per):
                    if c == LEAD and j > 0:
                        results(Count(n0), j * per - 1)
                        result_squares((t0 + j - 1) % 2, ss_m4, j - 1)
                    split(Count(n0), j * per + c)
            n0, t0, i6, per = PH["ffn2"]
            for c in range(LEAD):
                split(Count(n0), c)
            results(Count(n0), -1)
            result_squares((t0 - 1) % 2, ss_m4, DT - 1)
            root(6, rs_m)
            for j in range(DT):
                side_hi(i5 + j, xb, 4 * j, gains(V_PRE3 + 4 * j), j % 2)

            def conv_act(c, item, kb):
                if c == 7:
                    act.wait_ge(turned, item + 1)
                    for q in range(4):
                        last = nc.scalar.activation(conv[:, q, :], mis[0][:, q, :], ACT.Identity,
                                                    bias=vec[:, ds(kb + (V_CB + q), 1)],
                                                    scale=vec[:, ds(kb + (V_CW + 2 * KF + q), 1)])
                    last.then_inc(conv_tap, 1)
                if c == 9:
                    act.wait_ge(conv_ok, item + (1 - i6))
                    nc.scalar.activation(turned_a[:, :, :], conv[:, :, :], ACT.Gelu_apprx_tanh).then_inc(gelu_ok, 1)
                if c == 12:
                    act.wait_ge(prod_ok, item + (1 - i6))
                    nc.scalar.activation(ff[0][:, ds(kb, 4), :], conv[:, :, :], ACT.Copy).then_inc(hi_side, 1)

            for i in pairs(act, FT):
                n = Count(n0, i, 2 * per)
                first = isinstance(i, int)
                for c in range(2 * per):
                    if not first:
                        conv_act(c, i + (i6 - 1), i * 4 - 4)
                    if first and c == 5:
                        act.wait_ge(staged, stages(i5 + DT - 1))
                        for t in range(TT):
                            last = square(hres[:, t, :], mres[:, t, :], ss_x3[:, t:t + 1])
                        last.then_inc(squares, 1)
                    if first and c == 7:
                        root(7, rs_x3)
                        act.wait_ge(rstd_ok, 8)
                    if c == per + LEAD:
                        results(n, per - 1)
                        for t in range(TT):
                            nc.scalar.activation(stg[:, t, :], acc[t0 % 2][:, t, :], ACT.Copy,
                                                 scale=rs_x3[:, t:t + 1]).then_inc(acc_free[t0 % 2], 1)
                    if not (first and c < LEAD):
                        split(n, c)
            n0, t0, _, per = PH["down2"]
            for j in range(DT):
                for c in range(per):
                    if j == 0:
                        conv_act(c, i6 + FT - 1, 4 * (FT - 1))
                    if c == LEAD and j > 0:
                        results(Count(n0), j * per - 1)
                        result_squares((t0 + j - 1) % 2, ss_g4, j - 1)
                    split(Count(n0), j * per + c)
            results(Count(n0), DT * per - 1)
            result_squares((t0 + 3) % 2, ss_g4, DT - 1)
            root(8, rs_g)

        @block.vector
        def _(dve):
            chain = Chain(dve, dve_chain)
            V = nc.vector

            def split(n, c, width=W):
                slot = (n.start + c) % RING
                dve.wait_ge(hi_ready, n.at(c + 1))
                V.tensor_tensor(lo[:, slot, :, 0:width], raw[:, slot, :, 0:width],
                                hi[:, slot, :, 0:width].bitcast(F32), ALU.subtract).then_inc(lo_ready, 1)

            def norm(k, ss, rs, count, after):
                if after:
                    dve.wait_ge(squares, after)
                V.tensor_scalar(rs, ss, 1.0 / count, EPS, ALU.mult, ALU.add).then_inc(var_ok, 1)
                dve.wait_ge(root_ok, k + 1)
                V.reciprocal(rs, rs).then_inc(rstd_ok, 1)
                dve.wait_ge(rstd_ok, k + 1)

            def norm4(k, ss4, ss, rs, after):
                dve.wait_ge(squares, after)
                chain.step(V.tensor_reduce(ss, ss4.rearrange("p (t j) -> p t j", t=TT), AX.X, ALU.add))
                norm(k, ss, rs, D, 0)

            def side_lo(item, dst, kb, gain=None, pair=0, blocks=4):
                dve.wait_ge(hi_side, item + 1)
                if gain is None:
                    for half in range(2):
                        last = V.tensor_tensor(dst[1][:, ds(kb + 2 * half, 2), :],
                                               mis[pair][:, 2 * half:2 * half + 2, :],
                                               dst[0][:, ds(kb + 2 * half, 2), :].bitcast(F32), ALU.subtract)
                else:
                    for j in range(blocks):
                        last = V.scalar_tensor_tensor(dst[1][:, ds(kb + j, 1), :], mis[pair][:, j:j + 1, :], gain[j],
                                                      dst[0][:, ds(kb + j, 1), :].bitcast(F32), ALU.mult, ALU.subtract)
                last.then_inc(side, 1)

            def results(n, c):
                dve.wait_ge(chunk_used, n.at(c + 1))

            def ev(dst, par, scale, width=W):
                V.tensor_scalar(dst, acc[par][:, 1, 0:width], scale, None, ALU.mult).then_inc(acc_free[par], 1)

            dve.wait_ge(rows_turned, 1)
            V.tensor_copy(vec[:, 0:V_ROWS], misf[1][:, 0:V_ROWS])
            V.tensor_copy(vec[:, V_CW:V_CW + 2 * KF], misf[1][:, P:P + 2 * KF])
            V.tensor_copy(vec[:, V_CW + 2 * KF:V_ALL], misf[1][:, 2 * P:2 * P + 2 * KF]).then_inc(vec_ok, 1)
            dve.wait_ge(vec_ok, 1)
            chain.mark(V.tensor_tensor(gfin[:, :], vec[:, V_FIN:V_FIN + KD], vec[:, V_PRE2:V_PRE2 + KD], ALU.mult))
            dve.wait_ge(tab_in, 48)
            chain.step(V.tensor_copy(posf[:, :], posi[:, :]))
            for t in range(TT):
                chain.mark(V.tensor_scalar(ang[:, t, :], invf[:, :], posf[:, t:t + 1], None, ALU.mult))
            chain.join()
            chain.mark(V.tensor_scalar(trn[:, 0, :, :], ang[:, :, :], 1.0 / (2 * np.pi), 0.25, ALU.mult, ALU.add))
            chain.step(V.tensor_scalar(trn[:, 1, :, :], ang[:, :, :], 1.0 / (2 * np.pi), None, ALU.mult))
            chain.step(V.tensor_scalar(rnd[:, :, :, :], trn[:, :, :, :], MAGIC, None, ALU.add))
            chain.step(V.tensor_scalar(rnd[:, :, :, :], rnd[:, :, :, :], MAGIC, None, ALU.subtract))
            for k, part in enumerate(TWO_PI):
                for f in range(2):
                    chain.mark(V.scalar_tensor_tensor(trn[:, f, :, :], rnd[:, f, :, :], -part,
                                                      ang[:, :, :] if k == 0 else trn[:, f, :, :], ALU.mult, ALU.add))
                chain.join()
            chain.step(V.tensor_scalar(trn[:, 0, :, :], trn[:, 0, :, :], float(np.pi / 2), None, ALU.add))
            V.tensor_scalar(trn[:, :, :, :], trn[:, :, :, :], 3.1415925, -3.1415925, ALU.min, ALU.max)\
                .then_inc(ang_ok, 1)
            for j in range(4):
                side_lo(j, xa, 4 * j, gains(V_ATT + 4 * j), j % 2)
            n0, t0, _, per = PH["qkv"]
            for i in pairs(dve, 3):
                n = Count(n0, i, 2 * per)
                for j in range(2):
                    for c in range(per):
                        if c == 6 and j == 0 and isinstance(i, int):
                            norm(0, ss_x, rs_x, D, SQ["x"])
                        if c == LEAD and (j == 1 or not isinstance(i, int)):
                            results(n, j * per - 1)
                            ev(qkv[:, 1, ds(i * (2 * W) + (j - 1) * W, W)], (t0 + j - 1) % 2, rs_x[:, 1:2])
                        split(n, j * per + c)
            def rotate(x, t, heads, half, step, outs=None):
                outs = outs or [x]
                x1, x2 = x[:, :, 0:half], x[:, :, half:2 * half]
                co, si = (cs[:, t, f, ::step].unsqueeze(1).to_broadcast([P, heads, half]) for f in range(2))
                b = [r[:, 0:heads * half].rearrange("p (h f) -> p h f", h=heads) for r in rope_t]
                chain.mark(V.tensor_tensor(b[0], x1, co, ALU.mult))
                chain.mark(V.tensor_tensor(b[1], x2, si, ALU.mult))
                chain.mark(V.tensor_tensor(b[2], x2, co, ALU.mult))
                chain.step(V.tensor_tensor(b[3], x1, si, ALU.mult))
                for y in outs:
                    chain.mark(V.tensor_tensor(y[:, :, 0:half], b[0], b[1], ALU.subtract))
                    chain.mark(V.tensor_tensor(y[:, :, half:2 * half], b[2], b[3], ALU.add))
                chain.join()

            def attention_steps(g, first, head0, b, scale, bias, out, diff):
                n = due(g, first, PERIOD, 11, GH)
                if n is not None:
                    for s in range(1 if diff else 2):
                        dve.wait_ge(y_hi, head0 + 2 * n + (2 if diff else s + 1))
                        out(n, s)
                n = due(g, first, PERIOD, 4, GH)
                if n is not None:
                    for s in range(2):
                        dve.wait_ge(head_scores, head0 + 2 * n + s + 1)
                        if n:
                            dve.wait_ge(probs_turned, head0 + 2 * n + (0 if diff else s - 1))
                        p = b["p"][s]
                        chain.step(V.scalar_tensor_tensor(p[:, :], misf[s][:, W:W + 384], scale, bias[:, :],
                                                          ALU.mult, ALU.add))
                        V.tensor_reduce(mx[s][:, 0:1], p[:, 0:P], AX.X, ALU.max, negate=True)
                        V.tensor_reduce(mx[s][:, 1:2], p[:, P:384], AX.X, ALU.max, negate=True).then_inc(head_max, 1)
                    if diff:
                        chain.step(V.tensor_scalar(bias[:, :], bias[:, :], 0.25, None, ALU.mult))
                n = due(g, first, PERIOD, 6, GH)
                if n is None:
                    return
                for s in range(2):
                    dve.wait_ge(head_exp, head0 + 2 * n + s + 1)
                    p = b["p"][s]
                    chain.step(V.reciprocal(rc[s][:, :], sm[s][:, :]))
                    if diff and s == 1:
                        chain.step(V.tensor_scalar(rc[s][:, :], rc[s][:, :], lam[:, 0:1], -1.0, ALU.mult, ALU.mult))
                        dve.wait_ge(head_probs, head0 + 2 * n + 1)
                        p0 = b["p"][0]
                        V.scalar_tensor_tensor(p0[:, 0:P], p[:, 0:P], rc[1][:, 0:1], p0[:, 0:P], ALU.mult, ALU.add)
                        V.scalar_tensor_tensor(p0[:, P:384], p[:, P:384], rc[1][:, 1:2], p0[:, P:384],
                                               ALU.mult, ALU.add).then_inc(head_probs, 1)
                    else:
                        chain.mark(V.tensor_scalar(p[:, 0:P], p[:, 0:P], rc[s][:, 0:1], None, ALU.mult))
                        V.tensor_scalar(p[:, P:384], p[:, P:384], rc[s][:, 1:2], None, ALU.mult)\
                            .then_inc(head_probs, 1)

            def moba_out(n, s):
                V.tensor_tensor(xb[1][:, 2 * n + s, :], misf[s][:, 0:T], xb[0][:, 2 * n + s, :].bitcast(F32),
                                ALU.subtract).then_inc(y_done, 1)

            n0, t0, _, per = PH["gate0"]
            n = Count(n0)
            for c in range(5 * per):
                if c == LEAD:
                    results(n, -1)
                    ev(qkv[:, 1, 5 * W:], (t0 - 1) % 2, rs_x[:, 1:2])
                    for par in range(2):
                        dve.wait_ge(acc_free[par], 2 * ((t0 + 1 - par) // 2))
                    dve.wait_ge(cs_ok, 1)
                    for t in range(TT):
                        rotate(qkv[:, t, 0:2 * MH * MD].rearrange("p (h f) -> p h f", f=MD)[:, :, 0:MROPE], t,
                               2 * MH, MROPE // 2, 2)
                    V.engine_nop().then_inc(roped, 1)
                    dve.wait_ge(masks_ok, 1)
                attention_steps(c, MOBA_FIRST, 0, ab, float(MD) ** -0.5, causal, moba_out, False)
                split(n, c)
            n0, t0, i0, per = PH["cq"]
            n = Count(PH["ckv"][0])
            for c in range(per):
                if c == LEAD:
                    results(n, -1)
                    ev(stg[:, 1, :], t0 % 2, rs_x[:, 1:2])
                split(n, c, W_CKV)
            side_lo(i0, ct, 0, gains(V_Q))
            n, tu = Count(PH["uq"][0]), PH["uq"][1]
            for c in range(6):
                if c == LEAD:
                    results(n, -1)
                    ev(stg[:, 1, 0:W_CKV], (tu - 1) % 2, rs_x[:, 1:2], W_CKV)
                    dve.wait_ge(squares, SQ["c"])
                    chain.mark(V.tensor_scalar(rs_c[:, 0:2], ss_c[:, 0:2], 1.0 / QR, EPS, ALU.mult, ALU.add))
                    V.tensor_scalar(rs_c[:, 2:4], ss_c[:, 2:4], 1.0 / KVR, EPS, ALU.mult, ALU.add).then_inc(var_ok, 1)
                    dve.wait_ge(root_ok, 2)
                    V.reciprocal(rs_c, rs_c).then_inc(rstd_ok, 1)
                    side_lo(i0 + 1, ct, 4, gains(V_KV, 2), blocks=2)
                    dve.wait_ge(rstd_ok, 2)
                    results(n, 1)
                    ev(qm[:, 1, 0:W], tu % 2, rs_c[:, 1:2])
                split(n, c)
            n, tk = Count(PH["ukv"][0]), PH["ukv"][1]
            split(n, 0)
            results(n, -3)
            ev(qm[:, 1, W:2 * W], (tu + 1) % 2, rs_c[:, 1:2])
            split(n, 1)
            results(n, -1)
            ev(qm[:, 1, 2 * W:3 * W], (tu + 2) % 2, rs_c[:, 1:2])
            for j in range(2):
                split(n, j + 2)
                results(n, j)
                ev(kvm[:, 1, j * W:(j + 1) * W], (tk + j) % 2, rs_c[:, 3:4])

            def mla_rotate():
                for par in range(2):
                    dve.wait_ge(acc_free[par], 2 * ((tk + 4 + 1 - par) // 2))
                dve.wait_ge(krz_ok, 1)
                for t in range(TT):
                    rotate(kr[:, t, :].unsqueeze(1), t, 1, ROPE // 2, 1,
                           [krz[:, t, s:s + 1, s * ROPE:(s + 1) * ROPE] for s in range(2)])
                    rotate(qm[:, t, :].rearrange("p (h f) -> p h f", f=NOPE + ROPE)[:, :, NOPE:], t,
                           MH, ROPE // 2, 1, [qr[:, t, :].rearrange("p (h f) -> p h f", f=ROPE)])
                V.engine_nop().then_inc(roped, 1)

            def head_out(n, s, head0=MH):
                y = head0 + 2 * n + s
                V.tensor_tensor(xb[1][:, y, :], misf[s][:, 0:T], xb[0][:, y, :].bitcast(F32), ALU.subtract)\
                    .then_inc(y_done, 1)

            def mla_steps(g):
                attention_steps(g, MLA_FIRST, MH, ab, float(NOPE + ROPE) ** -0.5, causal, head_out, False)

            n0, t0, _, per = PH["gate1"]
            n = Count(n0)
            for c in range(4 * per):
                if c < 2:
                    results(Count(PH["ukv"][0]), c + 2)
                    ev(kvm[:, 1, (c + 2) * W:(c + 3) * W], (tk + c) % 2, rs_c[:, 3:4])
                if c == 2:
                    mla_rotate()
                mla_steps(c)
                split(n, c)
            n0, t0, i0, per = PH["branch"]

            def gated(par, dst, col):
                for t in range(TT):
                    V.tensor_tensor(dst[:, t, :], acc[par][:, t, :], gates[:, t, ds(col, W)], ALU.mult)\
                        .then_inc(acc_free[par], 1)

            def mix(tile_b, col):
                par = (t0 + 1) % 2
                gated(par, stg2, col)
                dve.wait_ge(acc_free[par], tile_b.at(2))
                V.tensor_tensor(stg[:, :, :], stg[:, :, :], stg2[:, :, :], ALU.add).then_inc(staged, 2)

            even = t0 - t0 % 2
            odd = (t0 + 1) - (t0 + 1) % 2
            for i in pairs(dve, DT):
                n = Count(n0, i, 2 * per)
                first = isinstance(i, int)
                for c in range(2 * per):
                    if first:
                        mla_steps(4 * KD // CK + c)
                    if c == LEAD and not first:
                        results(n, -1)
                        mix(Count(odd - 2, i, 2), i * W + (D - W))
                    if not first and c == 7:
                        side_lo(i + (i0 - 1), xa, i * 4 - 4)
                    if c == 7:
                        if first:
                            for par in range(2):
                                dve.wait_ge(acc_free[par], 2 * ((t0 + 1 - par) // 2))
                        results(n, per - 1)
                        gated(t0 % 2, stg, i * W)
                    split(n, c)

            def add(item, n, c, par, old):
                results(n, c)
                for t in range(TT):
                    V.tensor_tensor(stg[:, t, :], acc[par][:, t, :], old[:, t, :], ALU.add).then_inc(acc_free[par], 1)
                V.engine_nop().then_inc(staged, 1)

            i1 = PH["out"][2]
            n0, t1, _, per = PH["out"]
            for j in range(DT):
                for c in range(per):
                    if c == LEAD and j == 0:
                        results(Count(n0), -1)
                        mix(Count(odd + 2 * (DT - 1)), D + (DT - 1) * W)
                    if c == LEAD and j > 0:
                        dve.wait_ge(res_in, 16 * j)
                        add(i1 + j - 1, Count(n0), j * per - 1, (t1 + j - 1) % 2, res)
                    if c == 7 and j == 0:
                        side_lo(i1 - 1, xa, 4 * (DT - 1))
                    if c == 7 and j > 0:
                        side_lo(i1 + j - 1, xb, 4 * (j - 1), gains(V_FFN + 4 * (j - 1)))
                    split(Count(n0), j * per + c)
            n0, t0, i2, per = PH["ffn"]

            def swiglu(n, gate_tiles):
                par = (t0 + 1) % 2
                dve.wait_ge(acc_free[t0 % 2], gate_tiles)
                results(n, -1)
                for t in range(TT):
                    V.scalar_tensor_tensor(stg[:, t, :], acc[par][:, t, :], rs_h[:, t:t + 1], stg2[:, t, :],
                                           ALU.mult, ALU.mult).then_inc(acc_free[par], 1)
                V.engine_nop().then_inc(staged, 2)

            for i in pairs(dve, FT):
                n = Count(n0, i, 2 * per)
                first = isinstance(i, int)
                for c in range(2 * per):
                    if c == LEAD and first:
                        dve.wait_ge(res_in, 16 * DT)
                        add(i2 - 1, n, -1, (t0 - 1) % 2, res)
                        norm4(2, ss_h4, ss_h, rs_h, SQ["h"])
                    if c == LEAD and not first:
                        swiglu(n, i * 2 + (t0 - t0 % 2))
                    if c == 7 and first:
                        side_lo(i2 - 1, xb, 4 * (DT - 1), gains(V_FFN + 12))
                    if c == 7 and not first:
                        side_lo(i + (i2 - 1), ff, i * 4 - 4)
                    split(n, c)
            tg = t0 - t0 % 2 + 2 * FT
            n0, t1, i3, per = PH["down"]
            for j in range(DT):
                for c in range(per):
                    if c == LEAD and j == 0:
                        swiglu(Count(n0), tg)
                    if c == LEAD and j > 0:
                        add(i3 + j - 1, Count(n0), j * per - 1, (t1 + j - 1) % 2, hres[:, :, (j - 1) * W:j * W])
                    if c == 7 and j == 0:
                        side_lo(i3 - 1, ff, 4 * (FT - 1))
                    if c == 7 and j > 0:
                        side_lo(i3 + j - 1, xb, 4 * (j - 1), [gfin[:, 4 * j - 4 + q:4 * j - 3 + q] for q in range(4)])
                    split(Count(n0), j * per + c)
            n0, t0, _, per = PH["in2a"]
            n = Count(n0)
            for c in range(2 * per):
                if c == LEAD:
                    add(i3 + DT - 1, n, -1, (t0 - 1) % 2, hres[:, :, (DT - 1) * W:])
                    norm4(3, ss_f4, ss_f, rs_f, SQ["f"])
                if c == 7:
                    side_lo(i3 + DT - 1, xb, 12, [gfin[:, q:q + 1] for q in range(12, 16)])
                if c == per:
                    dve.wait_ge(gbc_in, 16)
                    dve.wait_ge(staged, stages(i3 + DT - 1))
                    for t in range(TT):
                        last = V.scalar_tensor_tensor(hres[:, t, :], hres[:, t, :], rs_f[:, t:t + 1],
                                                      gfbc[:, :], ALU.mult, ALU.mult)
                    last.then_inc(x2_ok, 1)
                if c == per + 1:
                    dve.wait_ge(squares, SQ["x2"])
                    V.tensor_scalar(rs_x2, ss_x2, 1.0 / D, EPS, ALU.mult, ALU.add).then_inc(var_ok, 1)
                    dve.wait_ge(root_ok, 5)
                    chain.step(V.reciprocal(rs_x2, rs_x2))
                    V.tensor_tensor(rs_in2, rs_x2, rs_f, ALU.mult).then_inc(rstd_ok, 1)
                    dve.wait_ge(rstd_ok, 5)
                if c == per + LEAD:
                    results(n, per - 1)
                    ev(proj2[:, 1, 0:W], t0 % 2, rs_in2[:, 1:2])
                split(n, c)
            n, t1 = Count(PH["ga"][0]), PH["ga"][1]
            for c in range(per):
                if c == LEAD:
                    results(n, -1)
                    ev(proj2[:, 1, W:2 * W], (t1 - 1) % 2, rs_in2[:, 1:2])
                split(n, c, GR)
            n0, t0, i4, per = PH["in2b"]

            def gla_steps(g):
                h = due(g, GLA_FIRST, GLA_PERIOD, 13, GH)
                if h is not None:
                    dve.wait_ge(gl_sq, h + 1)
                    V.tensor_copy(proj2[:, :, C2["gv"] + h * GV:C2["gv"] + (h + 1) * GV],
                                  misf[1][:, 0:2 * GV].rearrange("p (t e) -> p t e", t=TT)).then_inc(gl_out, 1)
                h = due(g, GLA_FIRST, GLA_PERIOD, 2, GH)
                if h is not None:
                    dve.wait_ge(gl_turned, h + 1)
                    V.tensor_scalar(g_z[:, :], misf[0][:, W:W + T], vec[:, V_BAL + h:V_BAL + h + 1], None, ALU.add)\
                        .then_inc(gl_z, 1)
                h = due(g, GLA_FIRST, GLA_PERIOD, 4, GH)
                if h is not None:
                    if h == 0:
                        dve.wait_ge(tables_ok, 1)
                    dve.wait_ge(gl_ln, h + 1)
                    chain.step(V.scalar_tensor_tensor(g_z[:, :], g_z[:, :], 0.0, g_e[:, :], ALU.min, ALU.subtract))
                    chain.step(V.tensor_tensor_scan(g_b[:, :], g_chunk[:, :], g_z[:, :], 0.0, ALU.mult, ALU.add))
                    if h:
                        dve.wait_ge(gl_lev, 2 * h)
                    for lv in range(6):
                        s = 1 << lv
                        b = g_b[:, :].rearrange("p (n s) -> p n s", s=2 * s)
                        V.tensor_tensor(g_x[:, lv, :].rearrange("p (n s) -> p n s", s=2 * s), b,
                                        b[:, :, s - 1:s].to_broadcast([P, T // (2 * s), 2 * s]), ALU.subtract)
                    b = g_b[:, :].rearrange("p (n s) -> p n s", s=64)
                    x6 = g_x[:, 6, :].rearrange("p (n s) -> p n s", s=64)
                    x7 = g_x[:, 7, :].rearrange("p (n s) -> p n s", s=64)
                    for k in range(4):
                        if k % 2 == 0:
                            V.tensor_scalar(x6[:, k, :], b[:, k, :], b[:, k, 63:64], None, ALU.subtract)
                        else:
                            V.tensor_copy(x6[:, k, :], b[:, k, :])
                    V.tensor_scalar(x7[:, 0, :], b[:, 0, :], b[:, 0, 63:64], b[:, 1, 63:64], ALU.subtract, ALU.subtract)
                    V.tensor_scalar(x7[:, 1, :], b[:, 1, :], b[:, 1, 63:64], None, ALU.subtract)
                    V.tensor_copy(x7[:, 2, :], b[:, 2, :])
                    V.tensor_scalar(x7[:, 3, :], b[:, 3, :], b[:, 2, 63:64], None, ALU.add).then_inc(gl_dec, 1)
                h = due(g, GLA_FIRST, GLA_PERIOD, 7, GH)
                if h is not None:
                    dve.wait_ge(gl_exp, h + 1)
                    dve.wait_ge(gl_qk, h + 1)
                    for lv in range(LEVELS):
                        s = 1 << lv
                        for half, x in ((0, 1), (1, 0)):
                            o = g_x[:, lv, :].rearrange("p (n h s) -> p n h s", h=2, s=s)[:, :, half, :]
                            v = g_qk[:, x, :].rearrange("p (n h s) -> p n h s", h=2, s=s)[:, :, half, :]
                            last = V.tensor_tensor(o, o, v, ALU.mult)
                    last.then_inc(gl_x, 1)
                gm, levels = g_m[:, :, :].rearrange("p a b -> p (a b)"), lmask[:, :, :].rearrange("p a b -> p (a b)")
                h = due(g, GLA_FIRST, GLA_PERIOD, 8, GH)
                if h is not None:
                    dve.wait_ge(gl_lev, 2 * h + 1)
                    if h:
                        dve.wait_ge(gl_o, h)
                    V.tensor_scalar(g_at[:, 2, :], misf[0][:, W + T:W + T + P], float(GK) ** -0.5, None, ALU.mult)
                    V.tensor_tensor(gm, misf[1], levels, ALU.mult).then_inc(gl_read, 1)
                    dve.wait_ge(gl_read, h + 1)
                    chain.step(V.tensor_reduce(g_at[:, 0, :], g_m[:, :, :].rearrange("p l i -> p i l"), AX.X, ALU.add))
                h = due(g, GLA_FIRST, GLA_PERIOD, 10, GH)
                if h is not None:
                    dve.wait_ge(gl_lev, 2 * h + 2)
                    chain.step(V.tensor_tensor(gm, misf[1], levels, ALU.mult))
                    V.tensor_reduce(g_at[:, 1, :], g_m[:, :, :].rearrange("p l i -> p i l"), AX.X, ALU.add)\
                        .then_inc(gl_at, 1)

            def diff_out(n, s):
                V.tensor_copy(proj2[:, :, C2["dv"] + n * GV:C2["dv"] + (n + 1) * GV],
                              misf[0][:, 0:2 * GV].rearrange("p (t e) -> p t e", t=TT)).then_inc(y_done, 2)

            def diff_steps(g):
                attention_steps(g, DIFF_FIRST, 2 * MH, db, float(GK) ** -0.5, dbias, diff_out, True)

            for j in range(NB):
                for c in range(per):
                    if c == LEAD and (j == 0 or BESIDE[j - 1] != C2["gg"]):
                        results(Count(n0), j * per - 1)
                        if j == 0:
                            ev(kr[:, 1, 0:GR], t1 % 2, rs_in2[:, 1:2], GR)
                        else:
                            ev(proj2[:, 1, BESIDE[j - 1]:BESIDE[j - 1] + W], (t0 + j - 1) % 2, rs_in2[:, 1:2])
                    if j == 4 and c == 0:
                        dve.wait_ge(lam_in, 64)
                        chain.step(V.tensor_tensor(lamj[:, :, :], lamr[:, 0:2, :], lamr[:, 2:4, :], ALU.mult))
                        V.tensor_reduce(lam2, lamj[:, :, :], AX.X, ALU.add).then_inc(lam_sum, 1)
                    if j == 4 and c == 4:
                        dve.wait_ge(lam_exp, 1)
                        chain.step(V.tensor_tensor(lam, lam2[:, 0:1], lam2[:, 1:2], ALU.subtract))
                        chain.step(V.tensor_scalar(lam, lam, LAMBDA_INIT, None, ALU.add))
                        dve.wait_ge(bias_ok, 1)
                    gla_steps(j * per + c)
                    diff_steps(j * per + c)
                    split(Count(n0), j * per + c)
            diff_steps(NB * per)
            dve.wait_ge(gl_sq, GH)
            dve.wait_ge(y_done, 4 * MH - 2 * MH + 2 * GH)
            norm(5, ss_o, rs_o, GV, 0)
            for par in range(2):
                dve.wait_ge(acc_free[par], 2 * ((t0 + NB + 1 - par) // 2))

            def strip_o(j):
                for t in range(TT):
                    for g in range(2):
                        h = (2 * j + g) % GH
                        o = o_strips[j][:, t, g * GV:(g + 1) * GV]
                        if j < 2:
                            V.scalar_tensor_tensor(o, o, rs_o[:, 4 * t + h:4 * t + h + 1],
                                                   sig[:, t, h * GV:(h + 1) * GV], ALU.mult, ALU.mult)
                        else:
                            V.tensor_scalar(o, o, rs_o[:, 8 + 4 * t + h:9 + 4 * t + h], 1.0 - LAMBDA_INIT,
                                            ALU.mult, ALU.mult)
                V.engine_nop().then_inc(staged, 2)

            strip_o(0)
            strip_o(1)
            for j in range(4):
                g0 = V_GLA if j < 2 else V_DIF
                side_lo(i4 + j, xa, 4 * j, gains(g0, 2) * 2, j % 2)
                if j + 2 < 4:
                    strip_o(j + 2)
            n0, t0, i5, per = PH["o2"]

            def gained(dst, tile_no, gain, squared):
                par = tile_no % 2
                dve.wait_ge(squares, squared)
                V.tensor_tensor(dst[:, 0, :], acc[par][:, 0, :], gain, ALU.mult)
                dve.wait_ge(acc_free[par], 2 * (tile_no // 2) + 1)
                V.tensor_tensor(dst[:, 1, :], acc[par][:, 1, :], gain, ALU.mult).then_inc(acc_free[par], 1)

            for j in range(DT):
                for c in range(per):
                    if c == LEAD and j > 0:
                        results(Count(n0), j * per - 1)
                        dve.wait_ge(gbc_in, 32)
                        gained(mres[:, :, (j - 1) * W:j * W], t0 + j - 1, g2bc[:, (j - 1) * W:j * W],
                               SQ["x2"] + j)
                    split(Count(n0), j * per + c)
            t_last = t0 + DT - 1
            n0, t0, i6, per = PH["ffn2"]
            for c in range(LEAD):
                split(Count(n0), c)
            results(Count(n0), -1)
            gained(mres[:, :, (DT - 1) * W:], t_last, g2bc[:, (DT - 1) * W:], SQ["m"])
            dve.wait_ge(acc_free[t_last % 2], 2 * (t_last // 2 + 1))
            norm4(6, ss_m4, ss_m, rs_m, SQ["m"])

            def strip_x3(j):
                for t in range(TT):
                    x = hres[:, t, j * W:(j + 1) * W]
                    V.scalar_tensor_tensor(x, mres[:, t, j * W:(j + 1) * W], rs_m[:, t:t + 1], x, ALU.mult, ALU.add)
                V.engine_nop().then_inc(staged, 2)

            strip_x3(0)
            strip_x3(1)
            for j in range(DT):
                side_lo(i5 + j, xb, 4 * j, gains(V_PRE3 + 4 * j), j % 2)
                if j + 2 < DT:
                    strip_x3(j + 2)

            def conv_dve(c, item, kb):
                if c == 8:
                    dve.wait_ge(conv_tap, item + (1 - i6))
                    for shift in (1, 2):
                        for q in range(4):
                            last = V.scalar_tensor_tensor(
                                conv[:, q, shift:T], mis[0][:, q, 0:T - shift],
                                vec[:, ds(kb + (V_CW + (2 - shift) * KF + q), 1)], conv[:, q, shift:T],
                                ALU.mult, ALU.add)
                            if shift == 1:
                                chain.mark(last)
                        if shift == 1:
                            chain.join()
                    last.then_inc(conv_ok, 1)
                if c == 10:
                    dve.wait_ge(gelu_ok, item + (1 - i6))
                    V.tensor_tensor(conv[:, :, :], turned_a[:, :, :], mis[1][:, :, :], ALU.mult).then_inc(prod_ok, 1)
                if c == 13:
                    dve.wait_ge(hi_side, item + 1)
                    V.tensor_tensor(ff[1][:, ds(kb, 4), :], conv[:, :, :], ff[0][:, ds(kb, 4), :].bitcast(F32),
                                    ALU.subtract).then_inc(side, 1)

            def stage_b(n):
                results(n, -1)
                for t in range(TT):
                    V.tensor_scalar(stg2[:, t, :], acc[(t0 + 1) % 2][:, t, :], rs_x3[:, t:t + 1], None, ALU.mult)\
                        .then_inc(acc_free[(t0 + 1) % 2], 1)
                V.engine_nop().then_inc(staged, 2)

            for i in pairs(dve, FT):
                n = Count(n0, i, 2 * per)
                first = isinstance(i, int)
                if not first:
                    chain.loop(i, 1, 4)
                for c in range(2 * per):
                    if not first:
                        if c == LEAD:
                            stage_b(n)
                        conv_dve(c, i + (i6 - 1), i * 4 - 4)
                    if first and c == 7:
                        norm(7, ss_x3, rs_x3, D, SQ["x3"])
                    if not (first and c < LEAD):
                        split(n, c)
            chain.end(FT - 1)
            n0, t1, _, per = PH["down2"]
            for j in range(DT):
                for c in range(per):
                    if j == 0:
                        if c == LEAD:
                            stage_b(Count(n0))
                        conv_dve(c, i6 + FT - 1, 4 * (FT - 1))
                    if c == LEAD and j > 0:
                        results(Count(n0), j * per - 1)
                        dve.wait_ge(gbc_in, 48)
                        gained(frow[:, :, (j - 1) * W:j * W], t1 + j - 1, gf2bc[:, (j - 1) * W:j * W],
                               SQ["x3"] + j)
                    split(Count(n0), j * per + c)
            results(Count(n0), DT * per - 1)
            gained(frow[:, :, (DT - 1) * W:], t1 + 3, gf2bc[:, (DT - 1) * W:], SQ["g"])
            dve.wait_ge(acc_free[(t1 + 3) % 2], 2 * ((t1 + 3) // 2 + 1))
            norm4(8, ss_g4, ss_g, rs_g, SQ["g"])
            for j in range(DT):
                for t in range(TT):
                    x = frow[:, t, j * W:(j + 1) * W]
                    V.scalar_tensor_tensor(x, x, rs_g[:, t:t + 1], hres[:, t, j * W:(j + 1) * W], ALU.mult, ALU.add)\
                        .then_inc(fin_ok, 1)

        @block.gpsimd
        def _(pool):
            chain = Chain(pool, pool_chain)
            G_ = nc.gpsimd

            def select(out, pattern, base, mult, compare, fill):
                return G_.affine_select(out=out, in_=out, compare_op=compare, fill=fill, base=base,
                                        pattern=pattern, channel_multiplier=mult)

            G_.memset(ident[:, :], 0.0).then_inc(ident_ok, 1)
            pool.wait_ge(ident_ok, 1)
            select(ident[:, :], [[-1, P]], 0, 1, ALU.not_equal, 1.0).then_inc(ident_ok, 1)
            chain.step(G_.memset(causal[:, :], 0.0))
            select(causal[:, 0:P], [[-1, P]], 0, 1, ALU.is_ge, NEG)
            select(causal[:, P:384], [[-1, T]], P, 1, ALU.is_ge, NEG).then_inc(masks_ok, 1)

            pool.wait_ge(chunk_used, PH["gate1"][0])
            G_.memset(krz[:, :, :, :], 0.0).then_inc(krz_ok, 1)
            pool.wait_ge(y_done, 2 * MH)
            for j in range(DT):
                if j:
                    pool.wait_ge(staged, stages(PH["out"][2] + j - 1) - 1)
                pool.dma_start(res[:, :, :], a["x"][0].rearrange("(t p) n -> p t n", p=P)[:, :, j * W:(j + 1) * W])\
                    .then_inc(res_in, 16)
            pool.wait_ge(chunk_used, PH["in2a"][0])
            pool.dma_start(gfbc[:, :], a["final_norm"].partition_broadcast(P)).then_inc(gbc_in, 16)
            for k, name in enumerate(("lambda_q1_2", "lambda_q2_2", "lambda_k1_2", "lambda_k2_2")):
                pool.dma_start(lamr[:, k, :], a[name][0].partition_broadcast(P)).then_inc(lam_in, 16)
            chain.step(G_.iota(dbias[:, 0:P], [[-1, P]], base=0, channel_multiplier=1,
                               allow_small_or_imprecise_dtypes=True))
            chain.step(G_.iota(dbias[:, P:384], [[-1, T]], base=P, channel_multiplier=1,
                               allow_small_or_imprecise_dtypes=True))
            chain.step(select(dbias[:, 0:P], [[-1, P]], 0, 1, ALU.is_ge, -NEG))
            chain.step(select(dbias[:, P:384], [[-1, T]], P, 1, ALU.is_ge, -NEG))
            G_.tensor_scalar(dbias[:, :], dbias[:, :], -0.25, None, ALU.mult).then_inc(bias_ok, 1)
            pool.wait_ge(rstd_ok, 5)
            pool.dma_start(walpha[0:GR, :], a["w_alpha_up_2"][0]).then_inc(wa_in, 16)
            chain.step(G_.memset(g_chunk[:, :], 1.0))
            chain.step(G_.memset(g_chunk[:, ::64], 0.0))
            sc = float(GK) ** -0.5
            chain.step(G_.memset(lmask[:, :, :], 0.0))
            for lv in range(LEVELS - 1):
                s = 1 << lv
                mk = lmask[:, lv, :].rearrange("p (n h s) -> p n h s", h=2, s=s)
                chain.step(G_.memset(mk[:, :, 1, :], sc))
                nb = P // (2 * s)
                flat = lmask[:, lv, :].rearrange("p (n s) -> p n s", s=2 * s)
                chain.step(select(flat, [[-2 * s, nb], [0, 2 * s]], 0, 1, ALU.is_ge, 0.0))
                chain.step(select(flat, [[2 * s, nb], [0, 2 * s]], s - 1, -1, ALU.is_ge, 0.0))
            select(lmask[:, LEVELS - 1, :], [[-1, P]], 0, 1, ALU.not_equal, sc).then_inc(tables_ok, 1)
            pool.wait_ge(turned, PH["in2b"][2] + 4)
            pool.dma_start(g2bc[:, :], a["attn_post_norm_2"][0].partition_broadcast(P)).then_inc(gbc_in, 16)
            pool.wait_ge(chunk_used, PH["down2"][0])
            pool.dma_start(gf2bc[:, :], a["ffn_post_norm_2"][0].partition_broadcast(P)).then_inc(gbc_in, 16)


_INS = ["x", "positions", "attn_norm", "w_in", "q_norm", "w_uq", "kv_norm", "w_ukv", "w_branch_a", "w_branch_b",
        "w_out", "ffn_norm", "w_gate", "w_up", "w_down", "final_norm", "attn_pre_norm_2", "w_in_2", "w_alpha_up_2",
        "b_alpha_2", "gla_norm_2", "lambda_q1_2", "lambda_k1_2", "lambda_q2_2", "lambda_k2_2", "diff_norm_2",
        "w_o_2", "attn_post_norm_2", "ffn_pre_norm_2", "w_ffn_in_2", "conv_w_2", "conv_b_2", "w_ffn_out_2",
        "ffn_post_norm_2"]


def kernel(**inputs):
    import concourse.bacc as _bacc
    from concourse.bass_utils import run_bass_kernel_spmd as _run

    nc = _bacc.Bacc("TRN2", target_bir_lowering=False, num_devices=1)
    arrays = {name: np.ascontiguousarray(inputs[name]) for name in _INS}
    arrays["inv_freq"] = (THETA ** (-np.arange(0, ROPE, 2, dtype=np.float64) / ROPE)).astype(np.float32)
    args = {name: nc.dram_tensor(f"in_{name}", v.shape, mybir.dt.from_np(v.dtype), kind="ExternalInput").ap()
            for name, v in arrays.items()}
    out = nc.dram_tensor("out", (1, T, D), F32, kind="ExternalOutput").ap()
    two_blocks(nc, args, out)
    r = _run(nc, [{f"in_{name}": v for name, v in arrays.items()}], core_ids=[0])
    return r.results[0]["out"]
```

```python
from contextlib import ExitStack

import numpy as np

import concourse.bass as bass
from concourse import mybir

F32 = mybir.dt.float32
F32R = mybir.dt.float32r
I32 = mybir.dt.int32
ALU = mybir.AluOpType
ACT = mybir.ActivationFunctionType
AX = mybir.AxisListType
ds = bass.ds

P = 128
TT = 2
T = P * TT
W = 512
CK = 2
RING = 4
LEAD = 3
D = 2048
KD = D // P
DT = D // W
DFF = 5632
KF = DFF // P
FT = DFF // W
EPS = 1e-6
NEG = -1e30

MH, MD = 8, 128
NOPE, ROPE, QR, KVR = 128, 64, 512, 256
MROPE = 32
QKV = 3 * MH * MD
C_CQ = QKV
C_CKV = C_CQ + QR
W_CKV = KVR + ROPE
C_GATE = C_CKV + W_CKV
UQ = MH * (NOPE + ROPE)
UKV = MH * (NOPE + MD)
THETA = 500000.0

GH, GK, GV, GR = 4, 128, 256, 16
LEVELS = 8
C2 = dict(gq=0, gk=512, gv=1024, gg=2048, ga=3072, dq=3088, dk=4112, dv=5136)
IN2 = 6160
BESIDE = [C2["gv"], C2["gv"] + W, C2["dq"], C2["dk"], C2["dv"], C2["dq"] + W, C2["dk"] + W, C2["dv"] + W,
          C2["gg"], C2["gg"] + W]
NB = len(BESIDE)
O2_ROWS = (8, 0, 12, 4)
PERIOD = 7
MOBA_FIRST, MLA_FIRST = 4, 4
GLA_FIRST, GLA_PERIOD = 6, 9
DIFF_FIRST = 48
TWO_PI = (6.28125, 0.0019350051879882812, 3.0198494e-07)
MAGIC = 12582912.0
LAMBDA_INIT = 0.2

A0, E0, H0, B0, R0, M0 = 0, 8192, 22528, 26624, 34816, 47104
END = 53200

V_ATT, V_Q, V_KV, V_FFN, V_FIN, V_PRE2, V_PRE3, V_BAL, V_GLA, V_DIF, V_ROWS = 0, 16, 20, 22, 38, 54, 70, 86, 90, 92, 94
V_CW, V_CB = 94, 94 + 3 * KF
V_ALL = V_CB + KF


class Count:

    def __init__(self, start, i=0, per=0):
        self.start, self.i, self.per = start, i, per

    def at(self, k):
        if self.per == 0 or (isinstance(self.i, int) and self.i == 0):
            return self.start + k
        return self.i * self.per + (self.start + k)

    def low(self, k):
        return self.start + k + (self.per * self.i if isinstance(self.i, int) else self.per)


class Chain:

    def __init__(self, eng, sem):
        self.eng, self.sem, self.base, self.k = eng, sem, 0, 0
        self.i, self.i0, self.per = 0, 0, 0

    def loop(self, i, i0, per):
        self.base, self.k = self.base + self.k, 0
        self.i, self.i0, self.per = i, i0, per

    def end(self, turns):
        assert self.k == self.per, f"the body's chain has {self.k} steps, not {self.per}"
        self.base, self.k, self.per = self.base + turns * self.per, 0, 0

    def mark(self, ins):
        ins.then_inc(self.sem, 1)
        self.k += 1

    def join(self):
        value = self.base + self.k
        if self.per:
            value = self.i * self.per + (value - self.i0 * self.per)
        self.eng.wait_ge(self.sem, value)

    def step(self, ins):
        self.mark(ins)
        self.join()


def pairs(eng, n):
    yield 0
    if n > 1:
        with eng.Fori(1, n) as i:
            yield i


def due(g, first, period, step, n):
    turn, rest = divmod(g - first - step, period)
    return turn if rest == 0 and 0 <= turn < n else None


def landed(n, c):
    return Count(16 * ((n.start + c) // RING + 1), n.i, 16 * n.per // RING).at(0)


def rows_of(w):
    return w.rearrange("l (k p) n -> p (l k) n", p=P)


def two_blocks(nc, a, out):
    ctx = ExitStack()
    with ctx:
        base = -(-nc.sbuf_base // 64) * 64

        def psum(name, shape):
            return ctx.enter_context(nc.psum_tensor(name, shape, F32))

        def sem(name):
            return ctx.enter_context(nc.semaphore(name))

        def at(name, word, shape, dt=F32):
            return nc.alloc_sbuf_tensor_at(name, [P] + shape, dt, offset=base + 4 * word)

        xa = [at("xa_hi", A0, [KD, T], F32R), at("xa_lo", A0 + 4096, [KD, T], F32R)]
        xb = [at("xb_hi", B0, [KD, T], F32R), at("xb_lo", B0 + 4096, [KD, T], F32R)]
        ff = [at("ff_hi", A0, [KF, T], F32R), at("ff_lo", A0 + KF * T, [KF, T], F32R)]
        xin = at("xin", H0, [TT, D])
        hres = at("hres", H0, [TT, D])
        ct = [at("ct_hi", H0 + 1024, [6, T], F32R), at("ct_lo", H0 + 1024 + 6 * T, [6, T], F32R)]
        gates = at("gates", E0, [TT, 2 * D])
        qkv = at("qkv", E0 + 8192, [TT, QKV])
        qm = at("qm", E0 + 8192, [TT, UQ])
        kvm = at("kvm", E0 + 8192 + TT * UQ, [TT, UKV])
        proj2 = at("proj2", E0, [TT, IN2])
        g2bc = at("g2bc", E0 + 6144, [D])
        mres = at("mres", E0, [TT, D])
        frow = at("frow", B0, [TT, D])
        gfbc = at("gfbc", A0, [D])
        gf2bc = at("gf2bc", B0 + 4096, [D])
        sqx2 = at("sqx2", A0 + 2048, [TT, D])
        raw = at("raw", R0, [RING, CK, W])
        raw_ga, hi_ga, lo_ga = (at(f"{x}_ga", R0 + w0, [RING, KD, GR * 4], dt)
                                for x, w0, dt in (("raw", 0, F32), ("hi", 4096, F32R), ("lo", 8192, F32R)))
        hi = at("hi", R0 + 4096, [RING, CK, W], F32R)
        lo = at("lo", R0 + 8192, [RING, CK, W], F32R)
        m = M0
        stg = at("stg", m, [TT, W]); m += 1024
        stg2 = at("stg2", m, [TT, W]); m += 1024
        res = at("res", m, [TT, W])
        conv = at("conv", m, [4, T]); m += 1024
        lmask = at("lmask", m, [LEVELS, P])
        turned_a = at("turned_a", m, [4, T]); m += 1024
        ident = at("ident", m, [P]); m += P
        vec = at("vec", m, [V_ALL]); m += V_ALL + (-V_ALL) % 8
        gfin = at("gfin", m, [KD]); m += KD
        cs = at("cs", m, [TT, 2, ROPE // 2]); m += 128
        causal = at("causal", m, [384]); m += 384
        kr = at("kr", m, [TT, ROPE]); m += 128
        small = at("small", m, [256]); m += 256
        assert m <= END, m
        rows = at("rows", E0, [3, P])
        ang = at("ang", E0 + 512, [TT, 32])
        trn = at("trn", E0 + 640, [2, TT, 32])
        rnd = at("rnd", E0 + 768, [2, TT, 32])
        invf = at("invf", E0 + 896, [32])
        posi = at("posi", E0 + 960, [TT], I32)
        posf = at("posf", E0 + 968, [TT])
        junk = at("junk", E0 + 1024, [TT, D])
        ab = dict(qk=[at(f"ab_qk{s}", M0 + 1024 + 512 * s, [2, T]) for s in range(2)],
                  p=[at(f"ab_p{s}", M0 + 2048 + 384 * s, [384]) for s in range(2)],
                  pt=[at(f"ab_pt{s}", M0 + 3072 + 384 * s, [384]) for s in range(2)])
        qr = at("qr", E0 + 2048, [TT, MH * ROPE])
        krz = at("krz", E0 + 3072, [TT, 2, P])
        qrt = at("qrt", H0 + 2560, [MH // 2, T])
        krt = at("krt", H0 + 3584, [2, T])
        rope_t = [at(f"rope_t{j}", B0 + 2048 + 512 * j, [512]) for j in range(4)]
        dbias = at("dbias", E0 + TT * IN2, [384])
        lamr = at("lamr", E0 + TT * IN2 + 384, [4, P])
        lamj = at("lamj", E0 + TT * IN2 + 896, [2, P])
        sq = at("sq", E0 + TT * IN2 + 1152, [TT, GV])
        db = dict(qk=[at(f"db_qk{s}", A0 + 3072 + 512 * s, [2, T]) for s in range(2)],
                  p=[at(f"db_p{s}", A0 + 7168 + 384 * s, [384]) for s in range(2)],
                  pt=[at("db_pt", A0 + 2432, [384])])
        g_qk = at("g_qk", A0, [2, T])
        g_z = at("g_z", A0 + 512, [T])
        g_e = at("g_e", A0 + 768, [T])
        g_b = at("g_b", A0 + 1024, [T])
        g_at = at("g_at", A0 + 1280, [3, P])
        g_chunk = at("g_chunk", A0 + 1664, [T])
        walpha = at("walpha", A0 + 1920, [GH * GK])
        gat = at("gat", A0 + 2816, [T])
        g_x = at("g_x", A0 + 4096, [LEVELS, T])
        g_m = at("g_m", A0 + 6144, [LEVELS, P])
        o_strips = [proj2[:, :, c:c + W] for c in (C2["dv"], C2["gv"], C2["dv"] + W, C2["gv"] + W)]
        sig = proj2[:, :, 0:GH * GV]

        def stat(k, n):
            return small[:, k:k + n]

        rs_x, ss_x = stat(0, 2), stat(2, 2)
        ss_c, rs_c = stat(4, 4), stat(8, 4)
        ss_h4, ss_h, rs_h = stat(12, 8), stat(20, 2), stat(22, 2)
        ss_f4, ss_f, rs_f = stat(24, 8), stat(32, 2), stat(34, 2)
        ss_x2, rs_x2, rs_in2 = stat(36, 2), stat(38, 2), stat(40, 2)
        ss_o, rs_o = stat(42, 16), stat(58, 16)
        ss_m4, ss_m, rs_m = stat(74, 8), stat(82, 2), stat(84, 2)
        ss_x3, rs_x3 = stat(94, 2), stat(96, 2)
        ss_g4, ss_g, rs_g = stat(98, 8), stat(106, 2), stat(108, 2)
        mx = [stat(110 + 2 * s, 2) for s in range(2)]
        sm = [stat(114 + 2 * s, 2) for s in range(2)]
        rc = [stat(118 + 2 * s, 2) for s in range(2)]
        lam2, lam = stat(122, 2), stat(124, 1)
        rs_tmp = stat(126, 16)

        acc = [psum(f"acc{j}", [P, TT, W]) for j in range(2)]
        mis = [psum(f"mis{j}", [P, 4, T]) for j in range(2)]
        misf = [x[:, :, :].rearrange("p a b -> p (a b)") for x in mis]
        accf = [x[:, :, :].rearrange("p a b -> p (a b)") for x in acc]

        raw_in = [sem(f"raw_in{j}") for j in range(RING)]
        hi_ready = sem("hi_ready")
        lo_ready = sem("lo_ready")
        chunk_used = sem("chunk_used")
        acc_free = [sem(f"acc_free{j}") for j in range(2)]
        staged = sem("staged")
        turned = sem("turned")
        hi_side = sem("hi_side")
        side = sem("side")
        x_in = [sem(f"x_in{j}") for j in range(4)]
        att_in = sem("att_in")
        att_turned = sem("att_turned")
        rows_in = sem("rows_in")
        tab_in = sem("tab_in")
        ident_ok = sem("ident_ok")
        masks_ok = sem("masks_ok")
        rows_turned = sem("rows_turned")
        vec_ok = sem("vec_ok")
        squares = sem("squares")
        var_ok = sem("var_ok")
        root_ok = sem("root_ok")
        rstd_ok = sem("rstd_ok")
        ang_ok = sem("ang_ok")
        cs_ok = sem("cs_ok")
        roped = sem("roped")
        head_turned = sem("head_turned")
        head_qk = sem("head_qk")
        head_scores = sem("head_scores")
        head_max = sem("head_max")
        head_exp = sem("head_exp")
        head_probs = sem("head_probs")
        probs_turned = sem("probs_turned")
        probs_in = sem("probs_in")
        head_y = sem("head_y")
        y_hi = sem("y_hi")
        y_done = sem("y_done")
        krt_turned = sem("krt_turned")
        krt_in = sem("krt_in")
        bias_ok = sem("bias_ok")
        lam_in = sem("lam_in")
        lam_sum = sem("lam_sum")
        lam_exp = sem("lam_exp")
        scales_ok = sem("scales_ok")
        scales_turned = sem("scales_turned")
        scales_in = sem("scales_in")
        ga_in = sem("ga_in")
        wa_in = sem("wa_in")
        tables_ok = sem("tables_ok")
        gl_turned = sem("gl_turned")
        gl_qk = sem("gl_qk")
        gl_z = sem("gl_z")
        gl_ln = sem("gl_ln")
        gl_dec = sem("gl_dec")
        gl_exp = sem("gl_exp")
        gl_x = sem("gl_x")
        gl_lev = sem("gl_lev")
        gl_read = sem("gl_read")
        gl_at = sem("gl_at")
        gl_o = sem("gl_o")
        gl_sq = sem("gl_sq")
        gl_out = sem("gl_out")
        res_in = sem("res_in")
        gbc_in = sem("gbc_in")
        x2_ok = sem("x2_ok")
        half_gained = sem("half_gained")
        conv_tap = sem("conv_tap")
        conv_ok = sem("conv_ok")
        gelu_ok = sem("gelu_ok")
        prod_ok = sem("prod_ok")
        fin_ok = sem("fin_ok")
        out_done = sem("out_done")
        act_chain = sem("act_chain")
        dve_chain = sem("dve_chain")
        pool_chain = sem("pool_chain")

        w_in, w_in2 = rows_of(a["w_in"]), rows_of(a["w_in_2"])
        w_uq, w_ukv = rows_of(a["w_uq"]), rows_of(a["w_ukv"])
        w_a, w_b, w_out = rows_of(a["w_branch_a"]), rows_of(a["w_branch_b"]), rows_of(a["w_out"])
        w_gate, w_up, w_down = rows_of(a["w_gate"]), rows_of(a["w_up"]), rows_of(a["w_down"])
        w_o2, w_f2, w_fo2 = rows_of(a["w_o_2"]), rows_of(a["w_ffn_in_2"]), rows_of(a["w_ffn_out_2"])

        PH = {}
        order = [
            ("qkv", 6, KD, 0), ("gate0", 4, KD, 0), ("cq", 1, KD, 1), ("ckv", 1, KD, 1),
            ("uq", 3, 4, 0), ("ukv", 4, 2, 0),
            ("gate1", 4, KD, 0), ("branch", 8, 8, 4), ("out", 4, KD, 4), ("ffn", 2 * FT, KD, FT),
            ("down", 4, KF, 4), ("in2a", 2, KD, 0), ("ga", 1, CK, 0), ("in2b", NB, KD, 4),
            ("o2", 4, KD, 4), ("ffn2", 2 * FT, KD, FT), ("down2", 4, KF, 0)]
        n_chunk = n_tile = 0
        n_item = 4
        for name, tiles, k, items in order:
            PH[name] = (n_chunk, n_tile, n_item, k // CK)
            n_chunk += tiles * k // CK
            n_tile += tiles if name != "ga" else 0
            n_item += items

        SQ = dict(x=2, c=3, h=7, f=11, x2=13, m=17, x3=19, g=23)

        def gains(row, n=4):
            return [vec[:, row + q:row + q + 1] for q in range(n)]

        def stages(item):
            return 2 * (item - 4 + 1)

        block = ctx.enter_context(nc.Block())

        @block.sync
        def _(sp):
            def x_strip(j):
                sp.dma_start(xin[:, :, j * W:(j + 1) * W],
                             a["x"][0].rearrange("(t p) n -> p t n", p=P)[:, :, j * W:(j + 1) * W])\
                    .then_inc(x_in[j], 16)

            def load(n, c, src):
                slot = (n.start + c) % RING
                if n.low(c) >= RING:
                    sp.wait_ge(lo_ready, n.at(c - RING + 1))
                w = src.shape[2]
                sp.dma_start(raw[:, slot, :, 0:w], src).then_inc(raw_in[slot], 16)

            def tile(n, c0, w, col, k, width=W):
                for c in range(k // CK):
                    load(n, c0 + c, w[:, CK * c:CK * c + CK, ds(col, width)])

            def plain(phase, w, col, k, n_pairs):
                n0 = PH[phase][0]
                per = 2 * k // CK
                for i in pairs(sp, n_pairs):
                    n = Count(n0, i, per)
                    if phase == "qkv" and isinstance(i, int):
                        for c in range(k // CK):
                            if c < 4:
                                x_strip(c)
                            load(n, c, w[:, CK * c:CK * c + CK, ds(col, W)])
                    else:
                        tile(n, 0, w, col + i * (2 * W), k)
                    tile(n, k // CK, w, (col + W) + i * (2 * W), k)

            def couple(phase, w1, w2, col1, col2, k, n_pairs):
                n0 = PH[phase][0]
                per = 2 * k // CK
                for i in pairs(sp, n_pairs):
                    n = Count(n0, i, per)
                    tile(n, 0, w1, col1 + i * W, k)
                    tile(n, k // CK, w2, col2 + i * W, k)

            plain("qkv", w_in, 0, KD, 3)
            plain("gate0", w_in, C_GATE, KD, 2)
            tile(Count(PH["cq"][0]), 0, w_in, C_CQ, KD)
            tile(Count(PH["ckv"][0]), 0, w_in, C_CKV, KD, W_CKV)
            for j in range(3):
                tile(Count(PH["uq"][0]), 2 * j, w_uq, j * W, 4)
            for j in range(4):
                tile(Count(PH["ukv"][0]), j, w_ukv, j * W, 2)
            plain("gate1", w_in, C_GATE + D, KD, 2)
            couple("branch", w_a, w_b, 0, 0, 8, DT)
            plain("out", w_out, 0, KD, 2)
            couple("ffn", w_gate, w_up, 0, 0, KD, FT)
            plain("down", w_down, 0, KF, 2)
            plain("in2a", w_in2, 0, KD, 1)
            slot = PH["ga"][0] % RING
            sp.wait_ge(lo_ready, PH["ga"][0] - RING + 1)
            sp.dma_start(raw_ga[:, slot, :, 0:GR], w_in2[:, :, C2["ga"]:C2["ga"] + GR]).then_inc(raw_in[slot], 16)
            for j, col in enumerate(BESIDE):
                tile(Count(PH["in2b"][0]), j * PH["in2b"][3], w_in2, col, KD)
            for i in pairs(sp, DT // 2):
                n = Count(PH["o2"][0], i, 2 * KD // CK)
                for j in range(2):
                    col = j * W + i * (2 * W)
                    for c in range(KD // CK):
                        row = O2_ROWS[c // 2] + c % 2 * CK
                        load(n, j * KD // CK + c, w_o2[:, row:row + CK, ds(col, W)])
            couple("ffn2", w_f2, w_f2, 0, DFF, KD, FT)
            plain("down2", w_fo2, 0, KF, 2)
            for j in range(DT):
                for t in range(TT):
                    sp.wait_ge(fin_ok, 2 * j + t + 1)
                    sp.dma_start(out[0, t * P:(t + 1) * P, j * W:(j + 1) * W],
                                 frow[:, t, j * W:(j + 1) * W]).then_inc(out_done, 16)
            sp.wait_ge(out_done, 16 * DT * TT)

        @block.tensor
        def _(pe):
            def turn(item, src, pair, blocks=4, wait=True):
                if wait:
                    pe.wait_ge(staged, stages(item))
                for kb in range(blocks):
                    for t in range(TT):
                        last = nc.tensor.transpose(mis[pair][:, kb, t * P:(t + 1) * P],
                                                   src[:, t, kb * P:(kb + 1) * P], ident[:, :])
                last.then_inc(turned, 1)

            def tile(n, c0, k, x, tile_no, par, width=W, k0=0, sides=None, hook=None, beside=None):
                for c in range(k // CK):
                    if hook and c in hook:
                        hook[c]()
                    if beside is not None:
                        beside(c)
                    if c == 0 and tile_no.low(0) >= 2:
                        pe.wait_ge(acc_free[par], tile_no.at(0))
                    if sides is not None and c % 2 == 0:
                        pe.wait_ge(side, sides + c // 2 + 1)
                    slot = (n.start + c0 + c) % RING
                    pe.wait_ge(lo_ready, n.at(c0 + c + 1))
                    for kk in range(CK):
                        kb = c * CK + kk
                        for t in range(TT):
                            xh = x[0][:, k0 + kb, t * P:(t + 1) * P]
                            xl = x[1][:, k0 + kb, t * P:(t + 1) * P]
                            o = acc[par][:, t, 0:width]
                            wh, wl = hi[:, slot, kk, 0:width], lo[:, slot, kk, 0:width]
                            nc.tensor.matmul(o, xh, wh, start=kb == 0, stop=False)
                            nc.tensor.matmul(o, xh, wl, start=False, stop=False)
                            last = nc.tensor.matmul(o, xl, wh, start=False, stop=kb == k - 1)
                    last.then_inc(chunk_used, 1)

            def tiles_of(tile0, i=0, per=0):
                return Count(tile0 - tile0 % 2, i, per)

            def plain(phase, k, x, n_pairs, sides=None, item=None):
                n0, t0, _, per = PH[phase]
                with pe.Fori(0, n_pairs) as i:
                    n = Count(n0, i, 2 * per)
                    for j in range(2):
                        hook = None
                        if item is not None:
                            hook = {4: lambda j=j: turn(i * 2 + (item + j), stg, 0)}
                        tile(n, j * per, k, x, tiles_of(t0 + j, i, 2), (t0 + j) % 2,
                             sides=sides if j == 0 else None, hook=hook)

            def couple(phase, k, xs, n_pairs, hooks, sides=None, k0=(0, 0)):
                n0, t0, _, per = PH[phase]
                with pe.Fori(0, n_pairs) as i:
                    n = Count(n0, i, 2 * per)
                    for j in range(2):
                        tile(n, j * per, k, xs, tiles_of(t0 + j, i, 2), (t0 + j) % 2, k0=k0[j],
                             sides=sides if j == 0 else None,
                             hook={4: lambda: hooks(i)} if hooks and j == 0 else None)

            def attention_steps(g, first, head0, b, q, k, v, rope, diff, values_in=None):
                n = due(g, first, PERIOD, 0, GH)
                if n is not None:
                    if head0 + 2 * (n - 1) > 0 and n != 1:
                        pe.wait_ge(y_done, head0 + 2 * max(n - 1, 0))
                    for s in range(2):
                        for x, src in enumerate((q, k)):
                            for t in range(TT):
                                last = nc.tensor.transpose(misf[s][:, x * T + t * P:x * T + (t + 1) * P],
                                                           src(n, s, t), ident[:, :])
                        last.then_inc(head_turned, 1)
                n = due(g, first, PERIOD, 2, GH)
                if n is not None:
                    if n:
                        pe.wait_ge(probs_in, head0 + 2 * n)
                    for s in range(2):
                        pe.wait_ge(head_qk, head0 + 2 * n + s + 1)
                        for t in range(TT):
                            o = misf[s][:, W + t * P:W + t * P + (t + 1) * P]
                            last = nc.tensor.matmul(o, b["qk"][s][:, 0, t * P:(t + 1) * P],
                                                    b["qk"][s][:, 1, 0:(t + 1) * P], start=True, stop=not rope)
                            if rope:
                                last = nc.tensor.matmul(o, qrt[:, n, t * P:(t + 1) * P],
                                                        krt[:, s, 0:(t + 1) * P], start=False, stop=True)
                        last.then_inc(head_scores, 1)
                n = due(g, first, PERIOD, PERIOD + 2, GH)
                if n is not None:
                    if values_in:
                        values_in(n)
                    for s in range(1 if diff else 2):
                        pe.wait_ge(probs_in, head0 + 2 * n + (2 if diff else s + 1))
                        if diff:
                            o0, o1 = misf[0][:, 0:GV], misf[0][:, GV:2 * GV]
                            vv = [v(n, s, t) for t in range(TT)]
                            nc.tensor.matmul(o0, b["pt"][0][:, 0:P], vv[0], start=True, stop=True)
                            nc.tensor.matmul(o1, b["pt"][0][:, P:T], vv[0], start=True, stop=False)
                            nc.tensor.matmul(o1, b["pt"][0][:, T:T + P], vv[1], start=False, stop=True)\
                                .then_inc(head_y, 2)
                        else:
                            nc.tensor.matmul(misf[s][:, 0:T], v(n, s, 0), b["pt"][s][:, 0:T],
                                             start=True, stop=False)
                            nc.tensor.matmul(misf[s][:, P:T], v(n, s, 1), b["pt"][s][:, T:T + P],
                                             start=False, stop=True).then_inc(head_y, 1)
                n = due(g, first, PERIOD, 6, GH)
                if n is not None:
                    for s in range(1 if diff else 2):
                        pe.wait_ge(head_probs, head0 + 2 * n + (2 if diff else s + 1))
                        for x in range(3):
                            last = nc.tensor.transpose(misf[s][:, W + x * P:W + (x + 1) * P],
                                                       b["p"][s][:, x * P:(x + 1) * P], ident[:, :])
                        last.then_inc(probs_turned, 2 if diff else 1)

            def moba_steps(g):
                if g == MOBA_FIRST:
                    pe.wait_ge(roped, 1)
                attention_steps(g, MOBA_FIRST, 0, ab,
                                lambda n, s, t: qkv[:, t, (2 * n + s) * MD:(2 * n + s + 1) * MD],
                                lambda n, s, t: qkv[:, t, (MH + 2 * n + s) * MD:(MH + 2 * n + s + 1) * MD],
                                lambda n, s, t: qkv[:, t, (2 * MH + 2 * n + s) * MD:(2 * MH + 2 * n + s + 1) * MD],
                                False, False)

            def mla_steps(g):
                def queries(n, s):
                    return (2 * n + s) * (NOPE + ROPE)

                def keys(n, s):
                    return (2 * n + s) * (NOPE + MD)

                attention_steps(g, MLA_FIRST, MH, ab,
                                lambda n, s, t: qm[:, t, queries(n, s):queries(n, s) + NOPE],
                                lambda n, s, t: kvm[:, t, keys(n, s):keys(n, s) + NOPE],
                                lambda n, s, t: kvm[:, t, keys(n, s) + NOPE:keys(n, s) + NOPE + MD],
                                True, False)

            pe.wait_ge(ident_ok, 2)

            def x_item(j):
                if j >= 2:
                    pe.wait_ge(side, j - 1)
                pe.wait_ge(x_in[j], 16)
                turn(j, xin[:, :, j * W:(j + 1) * W], j % 2, wait=False)

            def gain_vectors():
                pe.wait_ge(rows_in, 16 * 13)
                pe.wait_ge(side, 3)
                for j, r in enumerate((V_ROWS, 2 * KF, 2 * KF)):
                    last = nc.tensor.transpose(misf[0][:, j * P:j * P + r], rows[0:r, j, :], ident[0:r, 0:r])
                last.then_inc(rows_turned, 1)

            x_item(0)
            pe.wait_ge(att_in, 16)
            nc.tensor.transpose(accf[1][:, 0:KD], rows[0:KD, 0, :], ident[0:KD, 0:KD]).then_inc(att_turned, 1)
            x_item(1)
            n0, t0, _, per = PH["qkv"]
            tile(Count(n0), 0, KD, xa, tiles_of(t0), t0 % 2, sides=0,
                 hook={1: lambda: x_item(2), 3: lambda: x_item(3), 7: gain_vectors})
            pe.wait_ge(vec_ok, 1)
            tile(Count(n0), per, KD, xa, tiles_of(t0 + 1), (t0 + 1) % 2)
            with pe.Fori(1, 3) as i:
                for j in range(2):
                    tile(Count(n0, i, 2 * per), j * per, KD, xa, tiles_of(t0 + j, i, 2), (t0 + j) % 2)
            n0, t0, _, per = PH["gate0"]
            for j in range(4):
                tile(Count(n0), j * per, KD, xa, tiles_of(t0 + j), (t0 + j) % 2,
                     beside=lambda c, j=j: moba_steps(j * per + c))
            n0, t0, i0, per = PH["cq"]
            tile(Count(n0), 0, KD, xa, tiles_of(t0), t0 % 2, beside=lambda c: moba_steps(4 * per + c))
            n0, t0, _, per = PH["ckv"]
            tile(Count(n0), 0, KD, xa, tiles_of(t0), t0 % 2, width=W_CKV,
                 hook={4: lambda: turn(i0, stg, 0)})
            n0, t0, _, per = PH["uq"]
            for j in range(3):
                if j == 1:
                    turn(i0 + 1, stg, 0, blocks=2)
                if j == 0:
                    pe.wait_ge(side, i0 + 1)
                tile(Count(n0), 2 * j, 4, ct, tiles_of(t0 + j), (t0 + j) % 2)
            n0, t0, _, per = PH["ukv"]
            pe.wait_ge(side, i0 + 2)
            for j in range(4):
                tile(Count(n0), j, 2, ct, tiles_of(t0 + j), (t0 + j) % 2, k0=4)

            def mla_rope():
                pe.wait_ge(roped, 2)
                for tile_no in (t0 - 2, t0 - 1):
                    pe.wait_ge(acc_free[tile_no % 2], 2 * (tile_no // 2 + 1))
                for hp in range(MH // 2):
                    for t in range(TT):
                        nc.tensor.transpose(mis[0][:, hp, t * P:(t + 1) * P],
                                            qr[:, t, hp * P:(hp + 1) * P], ident[:, :])
                for s in range(2):
                    for t in range(TT):
                        last = nc.tensor.transpose(mis[1][:, s, t * P:(t + 1) * P], krz[:, t, s, :], ident[:, :])
                last.then_inc(krt_turned, 1)
                pe.wait_ge(krt_in, 1)

            n0, t0, _, per = PH["gate1"]
            for j in range(4):
                def beside(c, j=j):
                    if j == 0 and c == MLA_FIRST - 1:
                        mla_rope()
                    mla_steps(j * per + c)

                tile(Count(n0), j * per, KD, xa, tiles_of(t0 + j), (t0 + j) % 2, beside=beside)
            i0 = PH["branch"][2]
            n0, t0, _, per = PH["branch"]
            for i in pairs(pe, DT):
                n = Count(n0, i, 2 * per)
                if isinstance(i, int):
                    pe.wait_ge(y_done, MH)
                    tile(n, 0, 8, xb, tiles_of(t0), t0 % 2, beside=lambda c: mla_steps(4 * KD // CK + c))
                    pe.wait_ge(y_done, 2 * MH)
                else:
                    tile(n, 0, 8, xb, tiles_of(t0, i, 2), t0 % 2)
                tile(n, per, 8, xb, tiles_of(t0 + 1, i, 2), (t0 + 1) % 2, k0=8,
                     hook=None if isinstance(i, int) else {0: lambda: turn(i + (i0 - 1), stg, 0)})
            i1 = PH["out"][2]
            n0, t0, _, per = PH["out"]
            tile(Count(n0), 0, KD, xa, tiles_of(t0), t0 % 2, sides=i0,
                 hook={4: lambda: turn(i1 - 1, stg, 0)})
            for j in range(1, DT):
                tile(Count(n0), j * per, KD, xa, tiles_of(t0 + j), (t0 + j) % 2,
                     hook={4: lambda j=j: turn(i1 + j - 1, stg, 0)})
            i2 = PH["ffn"][2]
            couple("ffn", KD, xb, FT, lambda i: turn(i + (i2 - 1), stg, 0), sides=i1)
            i3 = PH["down"][2]
            plain("down", KF, ff, 2, sides=i2, item=i3 - 1)
            i4 = PH["in2b"][2]
            n0, t0, _, per = PH["in2a"]
            tile(Count(n0), 0, KD, xb, tiles_of(t0), t0 % 2, sides=i3,
                 hook={4: lambda: turn(i4 - 1, stg, 0)})
            tile(Count(n0), per, KD, xb, tiles_of(t0 + 1), (t0 + 1) % 2)
            n1 = PH["ga"][0]
            pe.wait_ge(lo_ready, n1 + 1)
            for kb in range(KD):
                o = misf[1][0:GR, 0:T]
                wh, wl = (x[:, n1 % RING, kb, 0:GR] for x in (hi_ga, lo_ga))
                nc.tensor.matmul(o, wh, xb[0][:, kb, :], start=kb == 0, stop=False)
                nc.tensor.matmul(o, wl, xb[0][:, kb, :], start=False, stop=False)
                last = nc.tensor.matmul(o, wh, xb[1][:, kb, :], start=False, stop=kb == KD - 1)
            last.then_inc(chunk_used, 1)
            pe.wait_ge(scales_ok, 1)
            for t in range(TT):
                last = nc.tensor.matmul(misf[1][0:GR, W + t * P:W + (t + 1) * P], kr[:, t, 0:GR], ident[:, :],
                                        start=True, stop=True)
            last.then_inc(scales_turned, 1)
            n0, t0, _, per = PH["in2b"]

            def evicted(tile_no):
                pe.wait_ge(acc_free[tile_no % 2], 2 * (tile_no // 2 + 1))

            def gla_steps(g):
                h = due(g, GLA_FIRST, GLA_PERIOD, 0, GH)
                if h is not None:
                    if h == 0:
                        pe.wait_ge(side, i4)
                        evicted(t0 - 2)
                        evicted(t0 - 1)
                        pe.wait_ge(ga_in, 1)
                        pe.wait_ge(wa_in, 16)
                    else:
                        pe.wait_ge(gl_qk, h)
                        pe.wait_ge(gl_read, h)
                    for x, col in enumerate((C2["gq"], C2["gk"])):
                        for t in range(TT):
                            nc.tensor.transpose(misf[0][:, x * T + t * P:x * T + (t + 1) * P],
                                                proj2[:, t, col + h * GK:col + (h + 1) * GK], ident[:, :])
                    nc.tensor.matmul(misf[0][:, W:W + T], walpha[0:GR, h * GK:(h + 1) * GK], gat[0:GR, :],
                                     start=True, stop=True).then_inc(gl_turned, 1)

                def levels(t):
                    tt = slice(t * P, (t + 1) * P)
                    for lv in range(LEVELS - 1):
                        nc.tensor.matmul(misf[1][:, lv * P:(lv + 1) * P], g_x[:, lv, tt], g_x[:, lv, tt],
                                         start=True, stop=True)
                    return nc.tensor.matmul(misf[1][:, (LEVELS - 1) * P:], g_qk[:, 1, tt], g_qk[:, 0, tt],
                                            start=True, stop=True)

                h = due(g, GLA_FIRST, GLA_PERIOD, 7, GH)
                if h is not None:
                    pe.wait_ge(gl_x, h + 1)
                    if h:
                        pe.wait_ge(gl_out, h)
                    nc.tensor.matmul(misf[0][:, W + T:W + T + P], g_x[:, LEVELS - 1, 0:P],
                                     g_x[:, LEVELS - 1, P:T], start=True, stop=True)
                    levels(0).then_inc(gl_lev, 1)
                h = due(g, GLA_FIRST, GLA_PERIOD, 9, GH)
                if h is not None:
                    pe.wait_ge(gl_read, h + 1)
                    levels(1).then_inc(gl_lev, 1)
                h = due(g, GLA_FIRST, GLA_PERIOD, 12, GH)
                if h is not None:
                    evicted(t0 + h // 2)
                    pe.wait_ge(gl_at, h + 1)
                    v = [proj2[:, t, C2["gv"] + h * GV:C2["gv"] + (h + 1) * GV] for t in range(TT)]
                    nc.tensor.matmul(misf[1][:, 0:GV], g_at[:, 0, :], v[0], start=True, stop=True)
                    nc.tensor.matmul(misf[1][:, GV:2 * GV], g_at[:, 1, :], v[1], start=True, stop=False)
                    nc.tensor.matmul(misf[1][:, GV:2 * GV], g_at[:, 2, :], v[0], start=False, stop=True)\
                        .then_inc(gl_o, 1)

            dtile = [(t0 + 3, t0 + 4), (t0 + 6, t0 + 7)]

            def diff_steps(g):
                n = due(g, DIFF_FIRST, PERIOD, 0, GH)
                if n is not None:
                    if n == 0:
                        pe.wait_ge(gl_out, GH)
                    evicted(dtile[n // 2][0] - 1)
                    evicted(dtile[n // 2][0])
                attention_steps(g, DIFF_FIRST, 2 * MH, db,
                                lambda n, s, t: proj2[:, t, ds(C2["dq"] + (2 * n + s) * GK, GK)],
                                lambda n, s, t: proj2[:, t, ds(C2["dk"] + (2 * n + s) * GK, GK)],
                                lambda n, s, t: proj2[:, t, C2["dv"] + n * GV:C2["dv"] + (n + 1) * GV],
                                False, True, lambda n: evicted(dtile[n // 2][1]))

            for j in range(NB):
                def beside(c, j=j):
                    gla_steps(j * per + c)
                    diff_steps(j * per + c)
                    if j == NB - 1 and c == 3:
                        pe.wait_ge(head_max, 2 * MH + 2 * GH)
                        turn(i4, o_strips[0], 1)
                    if j == NB - 1 and c == 7:
                        pe.wait_ge(side, i4 + 1)
                        turn(i4 + 1, o_strips[1], 1)

                tile(Count(n0), j * per, KD, xb, tiles_of(t0 + j), (t0 + j) % 2, beside=beside)

            def last_items(c):
                if c == 3:
                    turn(i4 + 2, o_strips[2], 0)
                if c == 4:
                    pe.wait_ge(side, i4 + 2)
                    turn(i4 + 3, o_strips[3], 1)

            n0, t0, _, per = PH["o2"]
            tile(Count(n0), 0, KD, xa, tiles_of(t0), t0 % 2, sides=i4, beside=last_items)
            for j in range(1, DT):
                tile(Count(n0), j * per, KD, xa, tiles_of(t0 + j), (t0 + j) % 2)
            i5 = PH["o2"][2]

            def x3_item(j):
                if j >= 2:
                    pe.wait_ge(side, i5 + j - 1)
                turn(i5 + j, hres[:, :, j * W:(j + 1) * W], j % 2)

            x3_item(0)
            x3_item(1)
            i6 = PH["ffn2"][2]

            def turn_both(k, a_read):
                pe.wait_ge(staged, k)
                pe.wait_ge(acc_free[PH["ffn2"][1] % 2], a_read)
                for pair, src in ((0, stg), (1, stg2)):
                    for kb in range(4):
                        for t in range(TT):
                            last = nc.tensor.transpose(mis[pair][:, kb, t * P:(t + 1) * P],
                                                       src[:, t, kb * P:(kb + 1) * P], ident[:, :])
                last.then_inc(turned, 1)

            n0, t0, _, per = PH["ffn2"]
            tile(Count(n0), 0, KD, xb, tiles_of(t0), t0 % 2, sides=i5,
                 hook={1: lambda: x3_item(2), 3: lambda: x3_item(3)})
            tile(Count(n0), per, KD, xb, tiles_of(t0 + 1), (t0 + 1) % 2)
            with pe.Fori(1, FT) as i:
                n = Count(n0, i, 2 * per)
                tile(n, 0, KD, xb, tiles_of(t0, i, 2), t0 % 2,
                     hook={4: lambda: turn_both(i * 2 + (stages(i6) - 2), i * 2 + (t0 - t0 % 2))})
                tile(n, per, KD, xb, tiles_of(t0 + 1, i, 2), (t0 + 1) % 2)
            even = t0 - t0 % 2 + 2 * FT
            n0, t0, _, per = PH["down2"]
            tile(Count(n0), 0, KF, ff, tiles_of(t0), t0 % 2, sides=i6,
                 hook={4: lambda: turn_both(stages(i6 + FT - 1), even)})
            tile(Count(n0), per, KF, ff, tiles_of(t0 + 1), (t0 + 1) % 2)
            for j in range(2, 4):
                tile(Count(n0), j * per, KF, ff, tiles_of(t0 + j), (t0 + j) % 2)

        @block.scalar
        def _(act):
            chain = Chain(act, act_chain)

            act.dma_start(rows[V_ATT:V_ATT + KD, 0, :], a["attn_norm"].rearrange("l (k p) -> (l k) p", p=P))\
                .then_inc(att_in, 16)

            def split(n, c, width=W):
                slot = (n.start + c) % RING
                act.wait_ge(raw_in[slot], landed(n, c))
                if n.low(c) >= RING:
                    act.wait_ge(chunk_used, n.at(c - RING + 1))
                nc.scalar.activation(hi[:, slot, :, 0:width], raw[:, slot, :, 0:width], ACT.Copy)\
                    .then_inc(hi_ready, 1)

            def root(k, dst):
                act.wait_ge(var_ok, k + 1)
                nc.scalar.activation(dst, dst, ACT.Sqrt).then_inc(root_ok, 1)

            def side_hi(item, dst, kb, gain=None, pair=0, blocks=4):
                act.wait_ge(turned, item + 1)
                if gain is None:
                    for half in range(2):
                        last = nc.scalar.activation(dst[0][:, ds(kb + 2 * half, 2), :],
                                                    mis[pair][:, 2 * half:2 * half + 2, :], ACT.Copy)
                else:
                    for j in range(blocks):
                        last = nc.scalar.activation(dst[0][:, ds(kb + j, 1), :], mis[pair][:, j:j + 1, :],
                                                    ACT.Copy, scale=gain[j])
                last.then_inc(hi_side, 1)

            def results(n, c):
                act.wait_ge(chunk_used, n.at(c + 1))

            def ev(dst, par, scale, width=W):
                nc.scalar.activation(dst, acc[par][:, 0, 0:width], ACT.Copy, scale=scale)\
                    .then_inc(acc_free[par], 1)

            def square(src, dst, total):
                return nc.scalar.activation(dst, src, ACT.Square, accum_out=total)

            def keep(item, ss4, j):
                act.wait_ge(staged, stages(item) - 1)
                for t in range(TT):
                    last = square(stg[:, t, :], stg2[:, t, :], ss4[:, 4 * t + j:4 * t + j + 1])
                last.then_inc(squares, 1)
                nc.scalar.activation(hres[:, :, j * W:(j + 1) * W], stg[:, :, :], ACT.Copy).then_inc(staged, 1)

            def x_hi(j):
                side_hi(j, xa, 4 * j, gains(V_ATT + 4 * j), j % 2)

            act.wait_ge(vec_ok, 1)
            x_hi(0)

            n0, t0, _, per = PH["qkv"]
            for i in pairs(act, 3):
                n = Count(n0, i, 2 * per)
                for j in range(2):
                    for c in range(per):
                        if isinstance(i, int) and j == 0:
                            if c in (1, 3, 5):
                                x_hi((c + 1) // 2)
                            if c >= 6:
                                t = c - 6
                                square(xin[:, t, :], junk[:, t, :], ss_x[:, t:t + 1]).then_inc(squares, 1)
                        if isinstance(i, int) and j == 1 and c == 2:
                            root(0, rs_x)
                            act.wait_ge(rstd_ok, 1)
                            act.wait_ge(ang_ok, 1)
                            for t in range(TT):
                                last = nc.scalar.activation(cs[:, t, :, :], trn[:, :, t, :], ACT.Sin)
                            last.then_inc(cs_ok, 1)
                        if c == LEAD and (j == 1 or not isinstance(i, int)):
                            results(n, j * per - 1)
                            ev(qkv[:, 0, ds(i * (2 * W) + (j - 1) * W, W)], (t0 + j - 1) % 2, rs_x[:, 0:1])
                        split(n, j * per + c)
            def attention_steps(g, first, head0, b, out, diff):
                n = due(g, first, PERIOD, 2, GH)
                if n is not None:
                    for s in range(2):
                        act.wait_ge(head_turned, head0 + 2 * n + s + 1)
                        if n:
                            act.wait_ge(head_scores, head0 + 2 * n + s - 1)
                        nc.scalar.activation(b["qk"][s][:, :, :].rearrange("p a b -> p (a b)"),
                                             misf[s][:, 0:W], ACT.Copy).then_inc(head_qk, 1)
                n = due(g, first, PERIOD, 5, GH)
                if n is not None:
                    for s in range(2):
                        act.wait_ge(head_max, head0 + 2 * n + s + 1)
                        p = b["p"][s]
                        nc.scalar.activation(p[:, 0:P], p[:, 0:P], ACT.Exp, bias=mx[s][:, 0:1],
                                             accum_out=sm[s][:, 0:1])
                        nc.scalar.activation(p[:, P:], p[:, P:], ACT.Exp, bias=mx[s][:, 1:2],
                                             accum_out=sm[s][:, 1:2]).then_inc(head_exp, 1)
                n = due(g, first, PERIOD, 8, GH)
                if n is not None:
                    for s in range(1 if diff else 2):
                        act.wait_ge(probs_turned, head0 + 2 * n + (2 if diff else s + 1))
                        if n:
                            act.wait_ge(head_y, head0 + 2 * n + (0 if diff else s - 1))
                        nc.scalar.activation(b["pt"][s][:, :], misf[s][:, W:W + 384], ACT.Copy)\
                            .then_inc(probs_in, 2 if diff else 1)
                n = due(g, first, PERIOD, 11, GH)
                if n is not None:
                    for s in range(1 if diff else 2):
                        act.wait_ge(head_y, head0 + 2 * n + (2 if diff else s + 1))
                        out(n, s)

            def head_out(n, s, head0=MH):
                nc.scalar.activation(xb[0][:, head0 + 2 * n + s, :], misf[s][:, 0:T], ACT.Copy).then_inc(y_hi, 1)

            def moba_out(n, s):
                head_out(n, s, 0)

            def sigmoid(par, col):
                for t in range(TT):
                    nc.scalar.activation(gates[:, t, col:col + W], acc[par][:, t, :], ACT.Sigmoid,
                                         scale=rs_x[:, t:t + 1]).then_inc(acc_free[par], 1)

            n0, t0, _, per = PH["gate0"]
            n = Count(n0)
            for c in range(5 * per):
                if c == LEAD:
                    results(n, -1)
                    ev(qkv[:, 0, 5 * W:], (t0 - 1) % 2, rs_x[:, 0:1])
                if c > per and c % per == LEAD:
                    results(n, c - LEAD - 1)
                    sigmoid((t0 + c // per - 1) % 2, (c // per - 1) * W)
                attention_steps(c, MOBA_FIRST, 0, ab, moba_out, False)
                split(n, c)
            n0, t0, i0, per = PH["cq"]
            n = Count(PH["ckv"][0])
            for c in range(per):
                if c == LEAD:
                    results(n, -1)
                    ev(stg[:, 0, :], t0 % 2, rs_x[:, 0:1])
                    act.wait_ge(acc_free[t0 % 2], 2 * (t0 // 2 + 1))
                    for t in range(TT):
                        square(stg[:, t, :], stg2[:, t, :], ss_c[:, t:t + 1]).then_inc(staged, 1)
                split(n, c, W_CKV)
            side_hi(i0, ct, 0, gains(V_Q))
            n, tu = Count(PH["uq"][0]), PH["uq"][1]
            for c in range(6):
                if c == LEAD:
                    results(n, -1)
                    ev(stg[:, 0, 0:W_CKV], (tu - 1) % 2, rs_x[:, 0:1], W_CKV)
                    act.wait_ge(acc_free[(tu - 1) % 2], 2 * ((tu - 1) // 2 + 1))
                    for t in range(TT):
                        square(stg[:, t, 0:KVR], stg2[:, t, 0:KVR], ss_c[:, 2 + t:3 + t]).then_inc(staged, 1)
                    nc.scalar.activation(kr[:, :, :], stg[:, :, KVR:W_CKV], ACT.Copy).then_inc(squares, 1)
                    root(1, rs_c)
                    side_hi(i0 + 1, ct, 4, gains(V_KV, 2), blocks=2)
                    act.wait_ge(rstd_ok, 2)
                    results(n, 1)
                    ev(qm[:, 0, 0:W], tu % 2, rs_c[:, 0:1])
                split(n, c)
            n, tk = Count(PH["ukv"][0]), PH["ukv"][1]
            split(n, 0)
            results(n, -3)
            ev(qm[:, 0, W:2 * W], (tu + 1) % 2, rs_c[:, 0:1])
            split(n, 1)
            results(n, -1)
            ev(qm[:, 0, 2 * W:3 * W], (tu + 2) % 2, rs_c[:, 0:1])
            for j in range(2):
                split(n, j + 2)
                results(n, j)
                ev(kvm[:, 0, j * W:(j + 1) * W], (tk + j) % 2, rs_c[:, 2:3])
            n0, t0, _, per = PH["gate1"]
            n = Count(n0)
            for c in range(4 * per):
                if c < 2:
                    results(Count(PH["ukv"][0]), c + 2)
                    ev(kvm[:, 0, (c + 2) * W:(c + 3) * W], (tk + c) % 2, rs_c[:, 2:3])
                if c > per and c % per == LEAD:
                    results(n, c - LEAD - 1)
                    sigmoid((t0 + c // per - 1) % 2, D + (c // per - 1) * W)
                if c == MLA_FIRST:
                    act.wait_ge(krt_turned, 1)
                    nc.scalar.activation(qrt[:, :, :], mis[0][:, :, :], ACT.Copy)
                    nc.scalar.activation(krt[:, :, :], mis[1][:, 0:2, :], ACT.Copy).then_inc(krt_in, 1)
                attention_steps(c, MLA_FIRST, MH, ab, head_out, False)
                split(n, c)
            n0, t0, i0, per = PH["branch"]
            for i in pairs(act, DT):
                n = Count(n0, i, 2 * per)
                first = isinstance(i, int)
                for c in range(2 * per):
                    if first and c == LEAD:
                        results(n, -1)
                        sigmoid((t0 - 1) % 2, 7 * W)
                    if first:
                        attention_steps(4 * KD // CK + c, MLA_FIRST, MH, ab, head_out, False)
                    if not first and c == 7:
                        side_hi(i + (i0 - 1), xa, i * 4 - 4)
                    split(n, c)
            i1 = PH["out"][2]
            n0, t0, _, per = PH["out"]
            for j in range(DT):
                for c in range(per):
                    if c == LEAD and j > 0:
                        keep(i1 + j - 1, ss_h4, j - 1)
                    if c == 7 and j == 0:
                        side_hi(i1 - 1, xa, 4 * (DT - 1))
                    if c == 7 and j > 0:
                        side_hi(i1 + j - 1, xb, 4 * (j - 1), gains(V_FFN + 4 * (j - 1)))
                    split(Count(n0), j * per + c)
            n0, t0, i2, per = PH["ffn"]
            for i in pairs(act, FT):
                n = Count(n0, i, 2 * per)
                first = isinstance(i, int)
                for c in range(2 * per):
                    if c == LEAD and first:
                        keep(i2 - 1, ss_h4, DT - 1)
                        root(2, rs_h)
                    if c == 7 and first:
                        side_hi(i2 - 1, xb, 4 * (DT - 1), gains(V_FFN + 12))
                        act.wait_ge(rstd_ok, 3)
                    if c == 7 and not first:
                        side_hi(i + (i2 - 1), ff, i * 4 - 4)
                    if c == per + LEAD:
                        results(n, per - 1)
                        for t in range(TT):
                            nc.scalar.activation(stg2[:, t, :], acc[t0 % 2][:, t, :], ACT.Silu,
                                                 scale=rs_h[:, t:t + 1]).then_inc(acc_free[t0 % 2], 1)
                    split(n, c)
            n0, t0, i3, per = PH["down"]
            for j in range(DT):
                for c in range(per):
                    if c == LEAD and j > 0:
                        keep(i3 + j - 1, ss_f4, j - 1)
                    if c == 7 and j == 0:
                        side_hi(i3 - 1, ff, 4 * (FT - 1))
                    if c == 7 and j > 0:
                        side_hi(i3 + j - 1, xb, 4 * (j - 1), [gfin[:, 4 * j - 4 + q:4 * j - 3 + q] for q in range(4)])
                    split(Count(n0), j * per + c)
            n0, t0, _, per = PH["in2a"]
            n = Count(n0)
            for c in range(2 * per):
                if c == LEAD:
                    keep(i3 + DT - 1, ss_f4, DT - 1)
                    root(3, rs_f)
                if c == 7:
                    side_hi(i3 + DT - 1, xb, 12, [gfin[:, q:q + 1] for q in range(12, 16)])
                for t in range(TT):
                    if c == per + 1 + t:
                        act.wait_ge(x2_ok, t + 1)
                        square(hres[:, t, :], sqx2[:, t, :], ss_x2[:, t:t + 1]).then_inc(squares, 1)
                if c == per + 4:
                    root(4, rs_x2)
                    act.wait_ge(rstd_ok, 5)
                    results(n, per - 1)
                    ev(proj2[:, 0, 0:W], t0 % 2, rs_in2[:, 0:1])
                split(n, c)
            n1 = PH["ga"][0]
            act.wait_ge(raw_in[n1 % RING], landed(Count(n1), 0))
            act.wait_ge(chunk_used, n1 - RING + 1)
            nc.scalar.activation(hi_ga[:, n1 % RING, :, 0:GR], raw_ga[:, n1 % RING, :, 0:GR], ACT.Copy)\
                .then_inc(hi_ready, 1)
            n0, t0, i4, per = PH["in2b"]

            def gla_steps(g):
                h = due(g, GLA_FIRST, GLA_PERIOD, 14, GH)
                if h is not None:
                    act.wait_ge(gl_o, h + 1)
                    for t in range(TT):
                        last = square(misf[1][:, t * GV:(t + 1) * GV], sq[:, t, :], ss_o[:, 4 * t + h:4 * t + h + 1])
                    last.then_inc(gl_sq, 1)
                h = due(g, GLA_FIRST, GLA_PERIOD, 2, GH)
                if h is not None:
                    act.wait_ge(gl_turned, h + 1)
                    if h:
                        act.wait_ge(gl_lev, 2 * h)
                    nc.scalar.activation(g_qk[:, :, :].rearrange("p a b -> p (a b)"), misf[0][:, 0:W], ACT.Copy)\
                        .then_inc(gl_qk, 1)
                h = due(g, GLA_FIRST, GLA_PERIOD, 3, GH)
                if h is not None:
                    act.wait_ge(gl_z, h + 1)
                    chain.step(nc.scalar.activation(g_e[:, :], g_z[:, :], ACT.Abs))
                    chain.step(nc.scalar.activation(g_e[:, :], g_e[:, :], ACT.Exp, scale=-1.0))
                    nc.scalar.activation(g_e[:, :], g_e[:, :], ACT.Ln, bias=1.0).then_inc(gl_ln, 1)
                for half in range(2):
                    h = due(g, GLA_FIRST, GLA_PERIOD, 5 + half, GH)
                    if h is not None:
                        act.wait_ge(gl_dec, 2 * h + half + 1)
                        gx = g_x[:, 4 * half:4 * half + 4, :].rearrange("p a b -> p (a b)")
                        chain.step(nc.scalar.activation(gx, gx, ACT.Abs))
                        nc.scalar.activation(gx, gx, ACT.Exp, scale=-1.0 / 16.0).then_inc(gl_exp, 1)

            def diff_out(n, s):
                for t in range(TT):
                    last = square(misf[0][:, t * GV:(t + 1) * GV], sq[:, t, :], ss_o[:, 8 + 2 * n + t:9 + 2 * n + t])
                last.then_inc(y_hi, 2)

            def silu(par, col):
                for t in range(TT):
                    nc.scalar.activation(sig[:, t, col:col + W], acc[par][:, t, :], ACT.Silu,
                                         scale=rs_in2[:, t:t + 1]).then_inc(acc_free[par], 1)

            for j in range(NB):
                for c in range(per):
                    if c == LEAD:
                        results(Count(n0), j * per - 1)
                        if j == 0:
                            ev(proj2[:, 0, W:2 * W], (t0 - 1) % 2, rs_in2[:, 0:1])
                            act.wait_ge(scales_turned, 1)
                            nc.scalar.activation(gat[0:GR, :], misf[1][0:GR, W:W + T], ACT.Copy).then_inc(scales_in, 1)
                        elif BESIDE[j - 1] == C2["gg"]:
                            silu((t0 + j - 1) % 2, 0)
                        else:
                            ev(proj2[:, 0, BESIDE[j - 1]:BESIDE[j - 1] + W], (t0 + j - 1) % 2, rs_in2[:, 0:1])
                    if j == 4 and c == 0:
                        act.wait_ge(lam_sum, 1)
                        nc.scalar.activation(lam2, lam2, ACT.Exp).then_inc(lam_exp, 1)
                    g = j * per + c
                    gla_steps(g)
                    attention_steps(g, DIFF_FIRST, 2 * MH, db, diff_out, True)
                    if g == 64:
                        root(5, rs_o[:, 0:8])
                    if g == 69:
                        root(6, rs_o[:, 8:12])
                    if g == 77:
                        side_hi(i4, xa, 0, gains(V_DIF, 2) * 2, 1)
                    split(Count(n0), g)

            def last_heads(c):
                attention_steps(NB * KD // CK + c, DIFF_FIRST, 2 * MH, db, diff_out, True)
                if c == 1:
                    side_hi(i4 + 1, xa, 4, gains(V_GLA, 2) * 2, 1)
                    root(7, rs_o[:, 12:16])
                if c == 2:
                    results(Count(PH["o2"][0]), -1)
                    silu((PH["o2"][1] - 1) % 2, W)
                if c == 4:
                    side_hi(i4 + 2, xa, 8, gains(V_DIF, 2) * 2, 0)
                if c == 6:
                    side_hi(i4 + 3, xa, 12, gains(V_GLA, 2) * 2, 1)

            n0, t0, i5, per = PH["o2"]

            def result_squares(par, ss4, j):
                square(acc[par][:, 0, :], stg2[:, 0, :], ss4[:, j:j + 1]).then_inc(squares, 1)
                act.wait_ge(half_gained, j + 1 + (0 if ss4 is ss_m4 else DT))
                square(acc[par][:, 1, :], stg2[:, 1, :], ss4[:, 4 + j:5 + j]).then_inc(acc_free[par], 1)

            for j in range(DT):
                for c in range(per):
                    if c == LEAD and j > 0:
                        results(Count(n0), j * per - 1)
                        result_squares((t0 + j - 1) % 2, ss_m4, j - 1)
                    if j == 0:
                        last_heads(c)
                    split(Count(n0), j * per + c)
            n0, t0, i6, per = PH["ffn2"]
            for c in range(LEAD):
                split(Count(n0), c)
            results(Count(n0), -1)
            result_squares((t0 - 1) % 2, ss_m4, DT - 1)
            root(8, rs_m)

            def x3_hi(j):
                side_hi(i5 + j, xb, 4 * j, gains(V_PRE3 + 4 * j), j % 2)

            x3_hi(0)
            x3_hi(1)

            def conv_act(c, item, kb):
                if c == 7:
                    act.wait_ge(turned, item + 1)
                    for q in range(4):
                        last = nc.scalar.activation(conv[:, q, :], mis[0][:, q, :], ACT.Identity,
                                                    bias=vec[:, ds(kb + (V_CB + q), 1)],
                                                    scale=vec[:, ds(kb + (V_CW + 2 * KF + q), 1)])
                    last.then_inc(conv_tap, 1)
                if c == 9:
                    act.wait_ge(conv_ok, item + (1 - i6))
                    nc.scalar.activation(turned_a[:, :, :], conv[:, :, :], ACT.Gelu_apprx_tanh).then_inc(gelu_ok, 1)
                if c == 12:
                    act.wait_ge(prod_ok, item + (1 - i6))
                    nc.scalar.activation(ff[0][:, ds(kb, 4), :], conv[:, :, :], ACT.Copy).then_inc(hi_side, 1)

            for i in pairs(act, FT):
                n = Count(n0, i, 2 * per)
                first = isinstance(i, int)
                for c in range(2 * per):
                    if not first:
                        conv_act(c, i + (i6 - 1), i * 4 - 4)
                    if first and c in (3, 5):
                        x3_hi(2 + (c - 3) // 2)
                    if first and c in (6, 7):
                        act.wait_ge(staged, stages(i5 + DT - 1))
                        t = c - 6
                        square(hres[:, t, :], mres[:, t, :], ss_x3[:, t:t + 1]).then_inc(squares, 1)
                    if first and c == 9:
                        root(9, rs_x3)
                        act.wait_ge(rstd_ok, 10)
                    if c == per + LEAD:
                        results(n, per - 1)
                        for t in range(TT):
                            nc.scalar.activation(stg[:, t, :], acc[t0 % 2][:, t, :], ACT.Copy,
                                                 scale=rs_x3[:, t:t + 1]).then_inc(acc_free[t0 % 2], 1)
                    if not (first and c < LEAD):
                        split(n, c)
            n0, t0, _, per = PH["down2"]
            for j in range(DT):
                for c in range(per):
                    if j == 0:
                        conv_act(c, i6 + FT - 1, 4 * (FT - 1))
                    if c == LEAD and j > 0:
                        results(Count(n0), j * per - 1)
                        result_squares((t0 + j - 1) % 2, ss_g4, j - 1)
                    split(Count(n0), j * per + c)
            results(Count(n0), DT * per - 1)
            result_squares((t0 + 3) % 2, ss_g4, DT - 1)
            root(10, rs_g)

        @block.vector
        def _(dve):
            chain = Chain(dve, dve_chain)
            V = nc.vector

            def split(n, c, width=W):
                slot = (n.start + c) % RING
                dve.wait_ge(hi_ready, n.at(c + 1))
                V.tensor_tensor(lo[:, slot, :, 0:width], raw[:, slot, :, 0:width],
                                hi[:, slot, :, 0:width].bitcast(F32), ALU.subtract).then_inc(lo_ready, 1)

            def norm(k, ss, rs, count, after):
                if after:
                    dve.wait_ge(squares, after)
                V.tensor_scalar(rs, ss, 1.0 / count, EPS, ALU.mult, ALU.add).then_inc(var_ok, 1)
                dve.wait_ge(root_ok, k + 1)
                V.reciprocal(rs, rs).then_inc(rstd_ok, 1)
                dve.wait_ge(rstd_ok, k + 1)

            def norm4(k, ss4, ss, rs, after):
                dve.wait_ge(squares, after)
                chain.step(V.tensor_reduce(ss, ss4.rearrange("p (t j) -> p t j", t=TT), AX.X, ALU.add))
                norm(k, ss, rs, D, 0)

            def side_lo(item, dst, kb, gain=None, pair=0, blocks=4):
                dve.wait_ge(hi_side, item + 1)
                if gain is None:
                    for half in range(2):
                        last = V.tensor_tensor(dst[1][:, ds(kb + 2 * half, 2), :],
                                               mis[pair][:, 2 * half:2 * half + 2, :],
                                               dst[0][:, ds(kb + 2 * half, 2), :].bitcast(F32), ALU.subtract)
                else:
                    for j in range(blocks):
                        last = V.scalar_tensor_tensor(dst[1][:, ds(kb + j, 1), :], mis[pair][:, j:j + 1, :], gain[j],
                                                      dst[0][:, ds(kb + j, 1), :].bitcast(F32), ALU.mult, ALU.subtract)
                last.then_inc(side, 1)

            def results(n, c):
                dve.wait_ge(chunk_used, n.at(c + 1))

            def ev(dst, par, scale, width=W):
                V.tensor_scalar(dst, acc[par][:, 1, 0:width], scale, None, ALU.mult).then_inc(acc_free[par], 1)

            def angles():
                dve.wait_ge(tab_in, 48)
                chain.step(V.tensor_copy(posf[:, :], posi[:, :]))
                for t in range(TT):
                    chain.mark(V.tensor_scalar(ang[:, t, :], invf[:, :], posf[:, t:t + 1], None, ALU.mult))
                chain.join()
                chain.mark(V.tensor_scalar(trn[:, 0, :, :], ang[:, :, :], 1.0 / (2 * np.pi), 0.25, ALU.mult, ALU.add))
                chain.step(V.tensor_scalar(trn[:, 1, :, :], ang[:, :, :], 1.0 / (2 * np.pi), None, ALU.mult))
                chain.step(V.tensor_scalar(rnd[:, :, :, :], trn[:, :, :, :], MAGIC, None, ALU.add))
                chain.step(V.tensor_scalar(rnd[:, :, :, :], rnd[:, :, :, :], MAGIC, None, ALU.subtract))
                for k, part in enumerate(TWO_PI):
                    for f in range(2):
                        chain.mark(V.scalar_tensor_tensor(trn[:, f, :, :], rnd[:, f, :, :], -part,
                                                          ang[:, :, :] if k == 0 else trn[:, f, :, :],
                                                               ALU.mult, ALU.add))
                    chain.join()
                chain.step(V.tensor_scalar(trn[:, 0, :, :], trn[:, 0, :, :], float(np.pi / 2), None, ALU.add))
                V.tensor_scalar(trn[:, :, :, :], trn[:, :, :, :], 3.1415925, -3.1415925, ALU.min, ALU.max)\
                    .then_inc(ang_ok, 1)
            def gain_vectors():
                dve.wait_ge(rows_turned, 1)
                V.tensor_copy(vec[:, KD:V_ROWS], misf[0][:, KD:V_ROWS])
                V.tensor_copy(vec[:, V_CW:V_CW + 2 * KF], misf[0][:, P:P + 2 * KF])
                V.tensor_copy(vec[:, V_CW + 2 * KF:V_ALL], misf[0][:, 2 * P:2 * P + 2 * KF]).then_inc(vec_ok, 1)
                dve.wait_ge(vec_ok, 2)
                V.tensor_tensor(gfin[:, :], vec[:, V_FIN:V_FIN + KD], vec[:, V_PRE2:V_PRE2 + KD], ALU.mult)\
                    .then_inc(vec_ok, 1)

            def x_lo(j):
                side_lo(j, xa, 4 * j, gains(V_ATT + 4 * j), j % 2)

            dve.wait_ge(att_turned, 1)
            V.tensor_copy(vec[:, V_ATT:V_ATT + KD], accf[1][:, 0:KD]).then_inc(vec_ok, 1)
            dve.wait_ge(vec_ok, 1)
            x_lo(0)
            n0, t0, _, per = PH["qkv"]
            for i in pairs(dve, 3):
                n = Count(n0, i, 2 * per)
                for j in range(2):
                    for c in range(per):
                        if isinstance(i, int) and j == 0:
                            if c in (1, 3, 5):
                                x_lo((c + 1) // 2)
                            if c == 7:
                                angles()
                        if isinstance(i, int) and j == 1 and c == 2:
                            norm(0, ss_x, rs_x, D, SQ["x"])
                            gain_vectors()
                        if c == LEAD and (j == 1 or not isinstance(i, int)):
                            results(n, j * per - 1)
                            ev(qkv[:, 1, ds(i * (2 * W) + (j - 1) * W, W)], (t0 + j - 1) % 2, rs_x[:, 1:2])
                        split(n, j * per + c)
            def rotate(x, t, heads, half, step):
                x1, x2 = x[:, :, 0:half], x[:, :, half:2 * half]
                co, si = (cs[:, t, f, ::step].unsqueeze(1).to_broadcast([P, heads, half]) for f in range(2))
                b = [r[:, 0:heads * half].rearrange("p (h f) -> p h f", h=heads) for r in rope_t]
                chain.mark(V.tensor_tensor(b[0], x1, co, ALU.mult))
                chain.mark(V.tensor_tensor(b[1], x2, si, ALU.mult))
                chain.mark(V.tensor_tensor(b[2], x2, co, ALU.mult))
                chain.step(V.tensor_tensor(b[3], x1, si, ALU.mult))
                chain.mark(V.tensor_tensor(x1, b[0], b[1], ALU.subtract))
                chain.step(V.tensor_tensor(x2, b[2], b[3], ALU.add))

            def attention_steps(g, first, head0, b, scale, bias, out, diff):
                n = due(g, first, PERIOD, 11, GH)
                if n is not None:
                    for s in range(1 if diff else 2):
                        dve.wait_ge(y_hi, head0 + 2 * n + (2 if diff else s + 1))
                        out(n, s)
                n = due(g, first, PERIOD, 4, GH)
                if n is not None:
                    for s in range(2):
                        dve.wait_ge(head_scores, head0 + 2 * n + s + 1)
                        if n:
                            dve.wait_ge(probs_turned, head0 + 2 * n + (0 if diff else s - 1))
                        p = b["p"][s]
                        chain.step(V.scalar_tensor_tensor(p[:, :], misf[s][:, W:W + 384], scale, bias[:, :],
                                                          ALU.mult, ALU.add))
                        V.tensor_reduce(mx[s][:, 0:1], p[:, 0:P], AX.X, ALU.max, negate=True)
                        V.tensor_reduce(mx[s][:, 1:2], p[:, P:384], AX.X, ALU.max, negate=True).then_inc(head_max, 1)
                    if diff:
                        chain.step(V.tensor_scalar(bias[:, :], bias[:, :], 0.25, None, ALU.mult))
                n = due(g, first, PERIOD, 6, GH)
                if n is None:
                    return
                for s in range(2):
                    dve.wait_ge(head_exp, head0 + 2 * n + s + 1)
                    p = b["p"][s]
                    chain.step(V.reciprocal(rc[s][:, :], sm[s][:, :]))
                    if diff and s == 1:
                        chain.step(V.tensor_scalar(rc[s][:, :], rc[s][:, :], lam[:, 0:1], -1.0, ALU.mult, ALU.mult))
                        dve.wait_ge(head_probs, head0 + 2 * n + 1)
                        p0 = b["p"][0]
                        V.scalar_tensor_tensor(p0[:, 0:P], p[:, 0:P], rc[1][:, 0:1], p0[:, 0:P], ALU.mult, ALU.add)
                        V.scalar_tensor_tensor(p0[:, P:384], p[:, P:384], rc[1][:, 1:2], p0[:, P:384],
                                               ALU.mult, ALU.add).then_inc(head_probs, 1)
                    else:
                        chain.mark(V.tensor_scalar(p[:, 0:P], p[:, 0:P], rc[s][:, 0:1], None, ALU.mult))
                        V.tensor_scalar(p[:, P:384], p[:, P:384], rc[s][:, 1:2], None, ALU.mult)\
                            .then_inc(head_probs, 1)

            def moba_out(n, s):
                V.tensor_tensor(xb[1][:, 2 * n + s, :], misf[s][:, 0:T], xb[0][:, 2 * n + s, :].bitcast(F32),
                                ALU.subtract).then_inc(y_done, 1)

            n0, t0, _, per = PH["gate0"]
            n = Count(n0)
            for c in range(5 * per):
                if c == LEAD:
                    results(n, -1)
                    ev(qkv[:, 1, 5 * W:], (t0 - 1) % 2, rs_x[:, 1:2])
                    for par in range(2):
                        dve.wait_ge(acc_free[par], 2 * ((t0 + 1 - par) // 2))
                    dve.wait_ge(cs_ok, 1)
                    for t in range(TT):
                        rotate(qkv[:, t, 0:2 * MH * MD].rearrange("p (h f) -> p h f", f=MD)[:, :, 0:MROPE], t,
                               2 * MH, MROPE // 2, 2)
                    V.engine_nop().then_inc(roped, 1)
                    dve.wait_ge(masks_ok, 1)
                attention_steps(c, MOBA_FIRST, 0, ab, float(MD) ** -0.5, causal, moba_out, False)
                split(n, c)
            n0, t0, i0, per = PH["cq"]
            n = Count(PH["ckv"][0])
            for c in range(per):
                if c == LEAD:
                    results(n, -1)
                    ev(stg[:, 1, :], t0 % 2, rs_x[:, 1:2])
                split(n, c, W_CKV)
            side_lo(i0, ct, 0, gains(V_Q))
            n, tu = Count(PH["uq"][0]), PH["uq"][1]
            for c in range(6):
                if c == LEAD:
                    results(n, -1)
                    ev(stg[:, 1, 0:W_CKV], (tu - 1) % 2, rs_x[:, 1:2], W_CKV)
                    dve.wait_ge(squares, SQ["c"])
                    chain.mark(V.tensor_scalar(rs_c[:, 0:2], ss_c[:, 0:2], 1.0 / QR, EPS, ALU.mult, ALU.add))
                    V.tensor_scalar(rs_c[:, 2:4], ss_c[:, 2:4], 1.0 / KVR, EPS, ALU.mult, ALU.add).then_inc(var_ok, 1)
                    dve.wait_ge(root_ok, 2)
                    V.reciprocal(rs_c, rs_c).then_inc(rstd_ok, 1)
                    side_lo(i0 + 1, ct, 4, gains(V_KV, 2), blocks=2)
                    dve.wait_ge(rstd_ok, 2)
                    results(n, 1)
                    ev(qm[:, 1, 0:W], tu % 2, rs_c[:, 1:2])
                split(n, c)
            n, tk = Count(PH["ukv"][0]), PH["ukv"][1]
            split(n, 0)
            results(n, -3)
            ev(qm[:, 1, W:2 * W], (tu + 1) % 2, rs_c[:, 1:2])
            split(n, 1)
            results(n, -1)
            ev(qm[:, 1, 2 * W:3 * W], (tu + 2) % 2, rs_c[:, 1:2])
            for j in range(2):
                split(n, j + 2)
                results(n, j)
                ev(kvm[:, 1, j * W:(j + 1) * W], (tk + j) % 2, rs_c[:, 3:4])

            def head_out(n, s, head0=MH):
                y = head0 + 2 * n + s
                V.tensor_tensor(xb[1][:, y, :], misf[s][:, 0:T], xb[0][:, y, :].bitcast(F32), ALU.subtract)\
                    .then_inc(y_done, 1)

            def mla_steps(g):
                attention_steps(g, MLA_FIRST, MH, ab, float(NOPE + ROPE) ** -0.5, causal, head_out, False)

            n0, t0, _, per = PH["gate1"]
            n = Count(n0)
            for c in range(4 * per):
                if c < 2:
                    results(Count(PH["ukv"][0]), c + 2)
                    ev(kvm[:, 1, (c + 2) * W:(c + 3) * W], (tk + c) % 2, rs_c[:, 3:4])
                mla_steps(c)
                split(n, c)
            n0, t0, i0, per = PH["branch"]

            def gated(par, dst, col):
                for t in range(TT):
                    V.tensor_tensor(dst[:, t, :], acc[par][:, t, :], gates[:, t, ds(col, W)], ALU.mult)\
                        .then_inc(acc_free[par], 1)

            def mix(tile_b, col):
                par = (t0 + 1) % 2
                gated(par, stg2, col)
                dve.wait_ge(acc_free[par], tile_b.at(2))
                V.tensor_tensor(stg[:, :, :], stg[:, :, :], stg2[:, :, :], ALU.add).then_inc(staged, 2)

            even = t0 - t0 % 2
            odd = (t0 + 1) - (t0 + 1) % 2
            for i in pairs(dve, DT):
                n = Count(n0, i, 2 * per)
                first = isinstance(i, int)
                for c in range(2 * per):
                    if first:
                        mla_steps(4 * KD // CK + c)
                    if c == LEAD and not first:
                        results(n, -1)
                        mix(Count(odd - 2, i, 2), i * W + (D - W))
                    if not first and c == 7:
                        side_lo(i + (i0 - 1), xa, i * 4 - 4)
                    if c == 7:
                        if first:
                            for par in range(2):
                                dve.wait_ge(acc_free[par], 2 * ((t0 + 1 - par) // 2))
                        results(n, per - 1)
                        gated(t0 % 2, stg, i * W)
                    split(n, c)

            def add(item, n, c, par, old):
                results(n, c)
                for t in range(TT):
                    V.tensor_tensor(stg[:, t, :], acc[par][:, t, :], old[:, t, :], ALU.add).then_inc(acc_free[par], 1)
                V.engine_nop().then_inc(staged, 1)

            i1 = PH["out"][2]
            n0, t1, _, per = PH["out"]
            for j in range(DT):
                for c in range(per):
                    if c == LEAD and j == 0:
                        results(Count(n0), -1)
                        mix(Count(odd + 2 * (DT - 1)), D + (DT - 1) * W)
                    if c == LEAD and j > 0:
                        dve.wait_ge(res_in, 16 * j)
                        add(i1 + j - 1, Count(n0), j * per - 1, (t1 + j - 1) % 2, res)
                    if c == 7 and j == 0:
                        side_lo(i1 - 1, xa, 4 * (DT - 1))
                    if c == 7 and j > 0:
                        side_lo(i1 + j - 1, xb, 4 * (j - 1), gains(V_FFN + 4 * (j - 1)))
                    split(Count(n0), j * per + c)
            n0, t0, i2, per = PH["ffn"]

            def swiglu(n, gate_tiles):
                par = (t0 + 1) % 2
                dve.wait_ge(acc_free[t0 % 2], gate_tiles)
                results(n, -1)
                for t in range(TT):
                    V.scalar_tensor_tensor(stg[:, t, :], acc[par][:, t, :], rs_h[:, t:t + 1], stg2[:, t, :],
                                           ALU.mult, ALU.mult).then_inc(acc_free[par], 1)
                V.engine_nop().then_inc(staged, 2)

            for i in pairs(dve, FT):
                n = Count(n0, i, 2 * per)
                first = isinstance(i, int)
                for c in range(2 * per):
                    if c == LEAD and first:
                        dve.wait_ge(res_in, 16 * DT)
                        add(i2 - 1, n, -1, (t0 - 1) % 2, res)
                        norm4(2, ss_h4, ss_h, rs_h, SQ["h"])
                    if c == LEAD and not first:
                        swiglu(n, i * 2 + (t0 - t0 % 2))
                    if c == 7 and first:
                        side_lo(i2 - 1, xb, 4 * (DT - 1), gains(V_FFN + 12))
                    if c == 7 and not first:
                        side_lo(i + (i2 - 1), ff, i * 4 - 4)
                    split(n, c)
            tg = t0 - t0 % 2 + 2 * FT
            n0, t1, i3, per = PH["down"]
            for j in range(DT):
                for c in range(per):
                    if c == LEAD and j == 0:
                        swiglu(Count(n0), tg)
                    if c == LEAD and j > 0:
                        add(i3 + j - 1, Count(n0), j * per - 1, (t1 + j - 1) % 2, hres[:, :, (j - 1) * W:j * W])
                    if c == 7 and j == 0:
                        side_lo(i3 - 1, ff, 4 * (FT - 1))
                    if c == 7 and j > 0:
                        side_lo(i3 + j - 1, xb, 4 * (j - 1), [gfin[:, 4 * j - 4 + q:4 * j - 3 + q] for q in range(4)])
                    split(Count(n0), j * per + c)
            n0, t0, _, per = PH["in2a"]
            n = Count(n0)
            for c in range(2 * per):
                if c == LEAD:
                    add(i3 + DT - 1, n, -1, (t0 - 1) % 2, hres[:, :, (DT - 1) * W:])
                    norm4(3, ss_f4, ss_f, rs_f, SQ["f"])
                if c == 7:
                    side_lo(i3 + DT - 1, xb, 12, [gfin[:, q:q + 1] for q in range(12, 16)])
                for t in range(TT):
                    if c == per + t:
                        dve.wait_ge(gbc_in, 16)
                        dve.wait_ge(staged, stages(i3 + DT - 1))
                        V.scalar_tensor_tensor(hres[:, t, :], hres[:, t, :], rs_f[:, t:t + 1],
                                               gfbc[:, :], ALU.mult, ALU.mult).then_inc(x2_ok, 1)
                if c == per + 4:
                    dve.wait_ge(squares, SQ["x2"])
                    V.tensor_scalar(rs_x2, ss_x2, 1.0 / D, EPS, ALU.mult, ALU.add).then_inc(var_ok, 1)
                    dve.wait_ge(root_ok, 5)
                    chain.step(V.reciprocal(rs_x2, rs_x2))
                    V.tensor_tensor(rs_in2, rs_x2, rs_f, ALU.mult).then_inc(rstd_ok, 1)
                    dve.wait_ge(rstd_ok, 5)
                    V.tensor_copy(kr[:, :, 0:GR], rs_in2.unsqueeze(2).to_broadcast([P, TT, GR])).then_inc(scales_ok, 1)
                    results(n, per - 1)
                    ev(proj2[:, 1, 0:W], t0 % 2, rs_in2[:, 1:2])
                split(n, c)
            n1 = PH["ga"][0]
            dve.wait_ge(hi_ready, n1 + 1)
            V.tensor_tensor(lo_ga[:, n1 % RING, :, 0:GR], raw_ga[:, n1 % RING, :, 0:GR],
                            hi_ga[:, n1 % RING, :, 0:GR].bitcast(F32), ALU.subtract).then_inc(lo_ready, 1)
            n0, t0, i4, per = PH["in2b"]

            def gla_steps(g):
                h = due(g, GLA_FIRST, GLA_PERIOD, 14, GH)
                if h is not None:
                    dve.wait_ge(gl_sq, h + 1)
                    V.tensor_copy(proj2[:, :, C2["gv"] + h * GV:C2["gv"] + (h + 1) * GV],
                                  misf[1][:, 0:2 * GV].rearrange("p (t e) -> p t e", t=TT)).then_inc(gl_out, 1)
                h = due(g, GLA_FIRST, GLA_PERIOD, 2, GH)
                if h is not None:
                    dve.wait_ge(gl_turned, h + 1)
                    V.tensor_scalar(g_z[:, :], misf[0][:, W:W + T], vec[:, V_BAL + h:V_BAL + h + 1], None, ALU.add)\
                        .then_inc(gl_z, 1)
                h = due(g, GLA_FIRST, GLA_PERIOD, 4, GH)
                if h is not None:
                    if h == 0:
                        dve.wait_ge(tables_ok, 1)
                    dve.wait_ge(gl_ln, h + 1)
                    chain.step(V.scalar_tensor_tensor(g_z[:, :], g_z[:, :], 0.0, g_e[:, :], ALU.min, ALU.subtract))
                    chain.step(V.tensor_tensor_scan(g_b[:, :], g_chunk[:, :], g_z[:, :], 0.0, ALU.mult, ALU.add))
                    if h:
                        dve.wait_ge(gl_lev, 2 * h)
                    for lv in range(6):
                        s = 1 << lv
                        b = g_b[:, :].rearrange("p (n s) -> p n s", s=2 * s)
                        last = V.tensor_tensor(g_x[:, lv, :].rearrange("p (n s) -> p n s", s=2 * s), b,
                                               b[:, :, s - 1:s].to_broadcast([P, T // (2 * s), 2 * s]), ALU.subtract)
                        if lv == 3:
                            last.then_inc(gl_dec, 1)
                    b = g_b[:, :].rearrange("p (n s) -> p n s", s=64)
                    x6 = g_x[:, 6, :].rearrange("p (n s) -> p n s", s=64)
                    x7 = g_x[:, 7, :].rearrange("p (n s) -> p n s", s=64)
                    for k in range(4):
                        if k % 2 == 0:
                            V.tensor_scalar(x6[:, k, :], b[:, k, :], b[:, k, 63:64], None, ALU.subtract)
                        else:
                            V.tensor_copy(x6[:, k, :], b[:, k, :])
                    V.tensor_scalar(x7[:, 0, :], b[:, 0, :], b[:, 0, 63:64], b[:, 1, 63:64], ALU.subtract, ALU.subtract)
                    V.tensor_scalar(x7[:, 1, :], b[:, 1, :], b[:, 1, 63:64], None, ALU.subtract)
                    V.tensor_copy(x7[:, 2, :], b[:, 2, :])
                    V.tensor_scalar(x7[:, 3, :], b[:, 3, :], b[:, 2, 63:64], None, ALU.add).then_inc(gl_dec, 1)
                for part in range(2):
                    h = due(g, GLA_FIRST, GLA_PERIOD, 6 + part, GH)
                    if h is not None:
                        dve.wait_ge(gl_exp, 2 * h + part + 1)
                        dve.wait_ge(gl_qk, h + 1)
                        for lv in range(4 * part, 4 * part + 4):
                            s = 1 << lv
                            for half, x in ((0, 1), (1, 0)):
                                o = g_x[:, lv, :].rearrange("p (n h s) -> p n h s", h=2, s=s)[:, :, half, :]
                                v = g_qk[:, x, :].rearrange("p (n h s) -> p n h s", h=2, s=s)[:, :, half, :]
                                last = V.tensor_tensor(o, o, v, ALU.mult)
                        if part:
                            last.then_inc(gl_x, 1)
                gm, levels = g_m[:, :, :].rearrange("p a b -> p (a b)"), lmask[:, :, :].rearrange("p a b -> p (a b)")
                h = due(g, GLA_FIRST, GLA_PERIOD, 9, GH)
                if h is not None:
                    dve.wait_ge(gl_lev, 2 * h + 1)
                    if h:
                        dve.wait_ge(gl_o, h)
                    V.tensor_scalar(g_at[:, 2, :], misf[0][:, W + T:W + T + P], float(GK) ** -0.5, None, ALU.mult)
                    V.tensor_tensor(gm, misf[1], levels, ALU.mult).then_inc(gl_read, 1)
                    dve.wait_ge(gl_read, h + 1)
                    chain.step(V.tensor_reduce(g_at[:, 0, :], g_m[:, :, :].rearrange("p l i -> p i l"), AX.X, ALU.add))
                h = due(g, GLA_FIRST, GLA_PERIOD, 11, GH)
                if h is not None:
                    dve.wait_ge(gl_lev, 2 * h + 2)
                    chain.step(V.tensor_tensor(gm, misf[1], levels, ALU.mult))
                    V.tensor_reduce(g_at[:, 1, :], g_m[:, :, :].rearrange("p l i -> p i l"), AX.X, ALU.add)\
                        .then_inc(gl_at, 1)

            def diff_out(n, s):
                V.tensor_copy(proj2[:, :, C2["dv"] + n * GV:C2["dv"] + (n + 1) * GV],
                              misf[0][:, 0:2 * GV].rearrange("p (t e) -> p t e", t=TT)).then_inc(y_done, 2)

            def strip_o(j):
                for t in range(TT):
                    for g in range(2):
                        h = j // 2 * 2 + g
                        o = o_strips[j][:, t, g * GV:(g + 1) * GV]
                        if j % 2:
                            V.scalar_tensor_tensor(o, o, rs_o[:, 4 * t + h:4 * t + h + 1],
                                                   sig[:, t, h * GV:(h + 1) * GV], ALU.mult, ALU.mult)
                        else:
                            V.tensor_scalar(o, o, rs_o[:, 8 + 2 * h + t:9 + 2 * h + t], 1.0 - LAMBDA_INIT,
                                            ALU.mult, ALU.mult)
                V.engine_nop().then_inc(staged, 2)

            def diff_steps(g):
                attention_steps(g, DIFF_FIRST, 2 * MH, db, float(GK) ** -0.5, dbias, diff_out, True)

            for j in range(NB):
                for c in range(per):
                    if c == LEAD and (j == 0 or BESIDE[j - 1] != C2["gg"]):
                        results(Count(n0), j * per - 1)
                        if j == 0:
                            ev(proj2[:, 1, W:2 * W], (t0 - 1) % 2, rs_in2[:, 1:2])
                            dve.wait_ge(scales_in, 1)
                            V.tensor_tensor(gat[0:GR, :], misf[1][0:GR, 0:T], gat[0:GR, :], ALU.mult)\
                                .then_inc(ga_in, 1)
                        else:
                            ev(proj2[:, 1, BESIDE[j - 1]:BESIDE[j - 1] + W], (t0 + j - 1) % 2, rs_in2[:, 1:2])
                    if j == 4 and c == 0:
                        dve.wait_ge(lam_in, 64)
                        chain.step(V.tensor_tensor(lamj[:, :, :], lamr[:, 0:2, :], lamr[:, 2:4, :], ALU.mult))
                        V.tensor_reduce(lam2, lamj[:, :, :], AX.X, ALU.add).then_inc(lam_sum, 1)
                    if j == 4 and c == 4:
                        dve.wait_ge(lam_exp, 1)
                        chain.step(V.tensor_tensor(lam, lam2[:, 0:1], lam2[:, 1:2], ALU.subtract))
                        chain.step(V.tensor_scalar(lam, lam, LAMBDA_INIT, None, ALU.add))
                        dve.wait_ge(bias_ok, 1)
                    g = j * per + c
                    gla_steps(g)
                    diff_steps(g)
                    if g == 64:
                        dve.wait_ge(gl_sq, GH)
                        norm(5, ss_o[:, 0:8], rs_o[:, 0:8], GV, 0)
                    if g == 69:
                        norm(6, ss_o[:, 8:12], rs_o[:, 8:12], GV, 0)
                    if g == 72:
                        strip_o(0)
                    if g == 76:
                        dve.wait_ge(acc_free[(t0 + NB - 2) % 2], 2 * ((t0 + NB - 2) // 2 + 1))
                        strip_o(1)
                    if g == 77:
                        side_lo(i4, xa, 0, gains(V_DIF, 2) * 2, 1)
                    split(Count(n0), g)

            def last_heads(c):
                diff_steps(NB * KD // CK + c)
                if c == 1:
                    side_lo(i4 + 1, xa, 4, gains(V_GLA, 2) * 2, 1)
                    norm(7, ss_o[:, 12:16], rs_o[:, 12:16], GV, 0)
                    strip_o(2)
                if c == 3:
                    last_tile = PH["o2"][1] - 1
                    dve.wait_ge(acc_free[last_tile % 2], 2 * (last_tile // 2 + 1))
                    strip_o(3)
                if c == 4:
                    side_lo(i4 + 2, xa, 8, gains(V_DIF, 2) * 2, 0)
                if c == 6:
                    side_lo(i4 + 3, xa, 12, gains(V_GLA, 2) * 2, 1)

            n0, t0, i5, per = PH["o2"]

            def gained(dst, tile_no, gain, squared):
                par = tile_no % 2
                V.tensor_tensor(dst[:, 1, :], acc[par][:, 1, :], gain, ALU.mult).then_inc(half_gained, 1)
                dve.wait_ge(squares, squared)
                V.tensor_tensor(dst[:, 0, :], acc[par][:, 0, :], gain, ALU.mult).then_inc(acc_free[par], 1)

            for j in range(DT):
                for c in range(per):
                    if j == 0:
                        last_heads(c)
                    if c == LEAD and j > 0:
                        results(Count(n0), j * per - 1)
                        dve.wait_ge(gbc_in, 32)
                        gained(mres[:, :, (j - 1) * W:j * W], t0 + j - 1, g2bc[:, (j - 1) * W:j * W],
                               SQ["x2"] + j)
                    split(Count(n0), j * per + c)
            t_last = t0 + DT - 1
            n0, t0, i6, per = PH["ffn2"]
            for c in range(LEAD):
                split(Count(n0), c)
            results(Count(n0), -1)
            gained(mres[:, :, (DT - 1) * W:], t_last, g2bc[:, (DT - 1) * W:], SQ["m"])
            dve.wait_ge(acc_free[t_last % 2], 2 * (t_last // 2 + 1))
            norm4(8, ss_m4, ss_m, rs_m, SQ["m"])

            def strip_x3(j):
                for t in range(TT):
                    x = hres[:, t, j * W:(j + 1) * W]
                    V.scalar_tensor_tensor(x, mres[:, t, j * W:(j + 1) * W], rs_m[:, t:t + 1], x, ALU.mult, ALU.add)
                V.engine_nop().then_inc(staged, 2)

            def x3_lo(j):
                side_lo(i5 + j, xb, 4 * j, gains(V_PRE3 + 4 * j), j % 2)

            strip_x3(0)
            strip_x3(1)
            x3_lo(0)
            x3_lo(1)

            def conv_dve(c, item, kb):
                if c == 8:
                    dve.wait_ge(conv_tap, item + (1 - i6))
                    for shift in (1, 2):
                        for q in range(4):
                            last = V.scalar_tensor_tensor(
                                conv[:, q, shift:T], mis[0][:, q, 0:T - shift],
                                vec[:, ds(kb + (V_CW + (2 - shift) * KF + q), 1)], conv[:, q, shift:T],
                                ALU.mult, ALU.add)
                            if shift == 1:
                                chain.mark(last)
                        if shift == 1:
                            chain.join()
                    last.then_inc(conv_ok, 1)
                if c == 10:
                    dve.wait_ge(gelu_ok, item + (1 - i6))
                    V.tensor_tensor(conv[:, :, :], turned_a[:, :, :], mis[1][:, :, :], ALU.mult).then_inc(prod_ok, 1)
                if c == 13:
                    dve.wait_ge(hi_side, item + 1)
                    V.tensor_tensor(ff[1][:, ds(kb, 4), :], conv[:, :, :], ff[0][:, ds(kb, 4), :].bitcast(F32),
                                    ALU.subtract).then_inc(side, 1)

            def stage_b(n):
                results(n, -1)
                for t in range(TT):
                    V.tensor_scalar(stg2[:, t, :], acc[(t0 + 1) % 2][:, t, :], rs_x3[:, t:t + 1], None, ALU.mult)\
                        .then_inc(acc_free[(t0 + 1) % 2], 1)
                V.engine_nop().then_inc(staged, 2)

            for i in pairs(dve, FT):
                n = Count(n0, i, 2 * per)
                first = isinstance(i, int)
                if not first:
                    chain.loop(i, 1, 4)
                for c in range(2 * per):
                    if not first:
                        if c == LEAD:
                            stage_b(n)
                        conv_dve(c, i + (i6 - 1), i * 4 - 4)
                    if first and c == 3:
                        strip_x3(2)
                        strip_x3(3)
                    if first and c in (3, 5):
                        x3_lo(2 + (c - 3) // 2)
                    if first and c == 9:
                        norm(9, ss_x3, rs_x3, D, SQ["x3"])
                    if not (first and c < LEAD):
                        split(n, c)
            chain.end(FT - 1)
            n0, t1, _, per = PH["down2"]
            for j in range(DT):
                for c in range(per):
                    if j == 0:
                        if c == LEAD:
                            stage_b(Count(n0))
                        conv_dve(c, i6 + FT - 1, 4 * (FT - 1))
                    if c == LEAD and j > 0:
                        results(Count(n0), j * per - 1)
                        dve.wait_ge(gbc_in, 48)
                        gained(frow[:, :, (j - 1) * W:j * W], t1 + j - 1, gf2bc[:, (j - 1) * W:j * W],
                               SQ["x3"] + j)
                    split(Count(n0), j * per + c)
            results(Count(n0), DT * per - 1)
            gained(frow[:, :, (DT - 1) * W:], t1 + 3, gf2bc[:, (DT - 1) * W:], SQ["g"])
            dve.wait_ge(acc_free[(t1 + 3) % 2], 2 * ((t1 + 3) // 2 + 1))
            norm4(10, ss_g4, ss_g, rs_g, SQ["g"])
            for j in range(DT):
                for t in range(TT):
                    x = frow[:, t, j * W:(j + 1) * W]
                    V.scalar_tensor_tensor(x, x, rs_g[:, t:t + 1], hres[:, t, j * W:(j + 1) * W], ALU.mult, ALU.add)\
                        .then_inc(fin_ok, 1)

        @block.gpsimd
        def _(pool):
            chain = Chain(pool, pool_chain)
            G_ = nc.gpsimd

            def select(out, pattern, base, mult, compare, fill):
                return G_.affine_select(out=out, in_=out, compare_op=compare, fill=fill, base=base,
                                        pattern=pattern, channel_multiplier=mult)

            G_.memset(ident[:, :], 0.0).then_inc(ident_ok, 1)
            pool.wait_ge(ident_ok, 1)
            select(ident[:, :], [[-1, P]], 0, 1, ALU.not_equal, 1.0).then_inc(ident_ok, 1)
            for row, name, n in ((V_Q, "q_norm", 4), (V_KV, "kv_norm", 2),
                                 (V_FFN, "ffn_norm", 16), (V_FIN, "final_norm", 16),
                                 (V_PRE2, "attn_pre_norm_2", 16), (V_PRE3, "ffn_pre_norm_2", 16),
                                 (V_BAL, "b_alpha_2", 4), (V_GLA, "gla_norm_2", 2), (V_DIF, "diff_norm_2", 2)):
                v = a[name]
                v = v.rearrange("l (k p) -> (l k) p", p=P) if len(v.shape) == 2 else v.rearrange("(k p) -> k p", p=P)
                pool.dma_start(rows[row:row + n, 0, :], v).then_inc(rows_in, 16)
            cw = a["conv_w_2"][0].rearrange("w (k p) -> w k p", p=P)
            pool.dma_start(rows[0:KF, 1, :], cw[0]).then_inc(rows_in, 16)
            pool.dma_start(rows[KF:2 * KF, 1, :], cw[1]).then_inc(rows_in, 16)
            pool.dma_start(rows[0:KF, 2, :], cw[2]).then_inc(rows_in, 16)
            pool.dma_start(rows[KF:2 * KF, 2, :], a["conv_b_2"].rearrange("l (k p) -> (l k) p", p=P))\
                .then_inc(rows_in, 16)
            for t in range(TT):
                pool.dma_start(posi[:, t:t + 1], a["positions"][0:1, t * P:(t + 1) * P].rearrange("b p -> p b"))\
                    .then_inc(tab_in, 16)
            pool.dma_start(invf[:, :], a["inv_freq"].partition_broadcast(P)).then_inc(tab_in, 16)

            chain.step(G_.memset(causal[:, :], 0.0))
            select(causal[:, 0:P], [[-1, P]], 0, 1, ALU.is_ge, NEG)
            select(causal[:, P:384], [[-1, T]], P, 1, ALU.is_ge, NEG).then_inc(masks_ok, 1)

            def rotate(x, t, heads, half, step, outs):
                x1, x2 = x[:, :, 0:half], x[:, :, half:2 * half]
                co, si = (cs[:, t, f, ::step].unsqueeze(1).to_broadcast([P, heads, half]) for f in range(2))
                b = [r[:, 0:heads * half].rearrange("p (h f) -> p h f", h=heads) for r in rope_t]
                chain.mark(G_.tensor_tensor(b[0], x1, co, ALU.mult))
                chain.mark(G_.tensor_tensor(b[1], x2, si, ALU.mult))
                chain.mark(G_.tensor_tensor(b[2], x2, co, ALU.mult))
                chain.step(G_.tensor_tensor(b[3], x1, si, ALU.mult))
                for y in outs:
                    chain.mark(G_.tensor_tensor(y[:, :, 0:half], b[0], b[1], ALU.subtract))
                    chain.mark(G_.tensor_tensor(y[:, :, half:2 * half], b[2], b[3], ALU.add))
                chain.join()

            pool.wait_ge(roped, 1)
            chain.step(G_.memset(krz[:, :, :, :], 0.0))
            pool.wait_ge(squares, SQ["c"])
            for t in range(TT):
                rotate(kr[:, t, :].unsqueeze(1), t, 1, ROPE // 2, 1,
                       [krz[:, t, s:s + 1, s * ROPE:(s + 1) * ROPE] for s in range(2)])
            tu = PH["uq"][1]
            for j in range(3):
                pool.wait_ge(acc_free[(tu + j) % 2], 2 * ((tu + j) // 2 + 1))
            for t in range(TT):
                rotate(qm[:, t, :].rearrange("p (h f) -> p h f", f=NOPE + ROPE)[:, :, NOPE:], t,
                       MH, ROPE // 2, 1, [qr[:, t, :].rearrange("p (h f) -> p h f", f=ROPE)])
            G_.engine_nop().then_inc(roped, 1)
            pool.wait_ge(y_done, 2 * MH)
            for j in range(DT):
                if j:
                    pool.wait_ge(staged, stages(PH["out"][2] + j - 1) - 1)
                pool.dma_start(res[:, :, :], a["x"][0].rearrange("(t p) n -> p t n", p=P)[:, :, j * W:(j + 1) * W])\
                    .then_inc(res_in, 16)
            pool.wait_ge(chunk_used, PH["in2a"][0])
            pool.dma_start(gfbc[:, :], a["final_norm"].partition_broadcast(P)).then_inc(gbc_in, 16)
            for k, name in enumerate(("lambda_q1_2", "lambda_q2_2", "lambda_k1_2", "lambda_k2_2")):
                pool.dma_start(lamr[:, k, :], a[name][0].partition_broadcast(P)).then_inc(lam_in, 16)
            chain.step(G_.iota(dbias[:, 0:P], [[-1, P]], base=0, channel_multiplier=1,
                               allow_small_or_imprecise_dtypes=True))
            chain.step(G_.iota(dbias[:, P:384], [[-1, T]], base=P, channel_multiplier=1,
                               allow_small_or_imprecise_dtypes=True))
            chain.step(select(dbias[:, 0:P], [[-1, P]], 0, 1, ALU.is_ge, -NEG))
            chain.step(select(dbias[:, P:384], [[-1, T]], P, 1, ALU.is_ge, -NEG))
            G_.tensor_scalar(dbias[:, :], dbias[:, :], -0.25, None, ALU.mult).then_inc(bias_ok, 1)
            pool.wait_ge(rstd_ok, 5)
            pool.dma_start(walpha[0:GR, :], a["w_alpha_up_2"][0]).then_inc(wa_in, 16)
            chain.step(G_.memset(g_chunk[:, :], 1.0))
            chain.step(G_.memset(g_chunk[:, ::64], 0.0))
            sc = float(GK) ** -0.5
            chain.step(G_.memset(lmask[:, :, :], 0.0))
            for lv in range(LEVELS - 1):
                s = 1 << lv
                mk = lmask[:, lv, :].rearrange("p (n h s) -> p n h s", h=2, s=s)
                chain.step(G_.memset(mk[:, :, 1, :], sc))
                nb = P // (2 * s)
                flat = lmask[:, lv, :].rearrange("p (n s) -> p n s", s=2 * s)
                chain.step(select(flat, [[-2 * s, nb], [0, 2 * s]], 0, 1, ALU.is_ge, 0.0))
                chain.step(select(flat, [[2 * s, nb], [0, 2 * s]], s - 1, -1, ALU.is_ge, 0.0))
            select(lmask[:, LEVELS - 1, :], [[-1, P]], 0, 1, ALU.not_equal, sc).then_inc(tables_ok, 1)
            pool.wait_ge(turned, PH["in2b"][2] + 4)
            pool.dma_start(g2bc[:, :], a["attn_post_norm_2"][0].partition_broadcast(P)).then_inc(gbc_in, 16)
            pool.wait_ge(chunk_used, PH["down2"][0])
            pool.dma_start(gf2bc[:, :], a["ffn_post_norm_2"][0].partition_broadcast(P)).then_inc(gbc_in, 16)


_INS = ["x", "positions", "attn_norm", "w_in", "q_norm", "w_uq", "kv_norm", "w_ukv", "w_branch_a", "w_branch_b",
        "w_out", "ffn_norm", "w_gate", "w_up", "w_down", "final_norm", "attn_pre_norm_2", "w_in_2", "w_alpha_up_2",
        "b_alpha_2", "gla_norm_2", "lambda_q1_2", "lambda_k1_2", "lambda_q2_2", "lambda_k2_2", "diff_norm_2",
        "w_o_2", "attn_post_norm_2", "ffn_pre_norm_2", "w_ffn_in_2", "conv_w_2", "conv_b_2", "w_ffn_out_2",
        "ffn_post_norm_2"]


def kernel(**inputs):
    import concourse.bacc as _bacc
    from concourse.bass_utils import run_bass_kernel_spmd as _run

    nc = _bacc.Bacc("TRN2", target_bir_lowering=False, num_devices=1)
    arrays = {name: np.ascontiguousarray(inputs[name]) for name in _INS}
    arrays["inv_freq"] = (THETA ** (-np.arange(0, ROPE, 2, dtype=np.float64) / ROPE)).astype(np.float32)
    args = {name: nc.dram_tensor(f"in_{name}", v.shape, mybir.dt.from_np(v.dtype), kind="ExternalInput").ap()
            for name, v in arrays.items()}
    out = nc.dram_tensor("out", (1, T, D), F32, kind="ExternalOutput").ap()
    two_blocks(nc, args, out)
    r = _run(nc, [{f"in_{name}": v for name, v in arrays.items()}], core_ids=[0])
    return r.results[0]["out"]
```
